# Optimizing a Trainium2 kernel written in Bass

```python
import math
import jax, jax.numpy as jnp
from jax import lax
import numpy as np

D_MODEL = 1024
BATCH = 1
SEQ = 256
DEPTH = 2

HG_HEADS = 4
HG_DK = 128
HG_DV = 128
HG_K = HG_HEADS * HG_DK
HG_V = HG_HEADS * HG_DV
HG_CHUNK = 64
SG_GROUPS = 4
SG_WIDTH = 512
SG_GROUP_DIM = SG_WIDTH // SG_GROUPS
SG_CHUNK = 128
D_FF = 2816
ALPHA = (2 * DEPTH) ** 0.25
BETA = (8 * DEPTH) ** -0.25
LN_EPS = 1e-5
RMS_EPS = 1e-6
D_IN = 2 * HG_K + 2 * HG_V + 2 * SG_WIDTH + 2 * D_MODEL
IN_SPLITS = (HG_K,
             2 * HG_K,
             2 * HG_K + HG_V,
             2 * HG_K + 2 * HG_V,
             2 * HG_K + 2 * HG_V + SG_WIDTH,
             2 * HG_K + 2 * HG_V + 2 * SG_WIDTH,
             2 * HG_K + 2 * HG_V + 2 * SG_WIDTH + D_MODEL)


def layer_norm(x, g, b):
    xf = x.astype(jnp.float32)
    mu = jnp.mean(xf, axis=-1, keepdims=True)
    var = jnp.mean(jnp.square(xf - mu), axis=-1, keepdims=True)
    y = (xf - mu) * lax.rsqrt(var + LN_EPS) * g.astype(jnp.float32) + b.astype(jnp.float32)
    return y.astype(x.dtype)

def swiglu(x, w13, w2):
    a, b = jnp.split(x @ w13, 2, axis=-1)
    return (jax.nn.silu(a) * b) @ w2

def hgrn2_chunkwise(q, k, i, log_f):
    B, T, H, _ = q.shape
    n_chunks = T // HG_CHUNK

    def to_chunks(a):
        return a.reshape(B, n_chunks, HG_CHUNK, H, a.shape[-1]).transpose(1, 0, 3, 2, 4)

    causal = jnp.tril(jnp.ones((HG_CHUNK, HG_CHUNK), dtype=bool))[:, :, None]

    def step(S, inp):
        q_c, k_c, i_c, lf_c = inp
        b = jnp.cumsum(lf_c, axis=-2)
        o_inter = jnp.einsum('bhtk,bhkv->bhtv', q_c * jnp.exp(b), S)
        diff = b[:, :, :, None, :] - b[:, :, None, :, :]
        decay = jnp.where(causal, jnp.exp(jnp.where(causal, diff, 0.0)), 0.0)
        scores = jnp.einsum('bhtk,bhtsk,bhsk->bhts', q_c, decay, k_c)
        o_intra = jnp.einsum('bhts,bhsv->bhtv', scores, i_c)
        b_last = b[:, :, -1:, :]
        S_new = jnp.exp(b_last[:, :, 0, :])[..., None] * S + jnp.einsum(
            'bhsk,bhsv->bhkv', k_c * jnp.exp(b_last - b), i_c)
        return S_new, o_inter + o_intra

    S0 = jnp.zeros((B, H, q.shape[-1], i.shape[-1]), jnp.float32)
    _, o = lax.scan(step, S0, (to_chunks(q), to_chunks(k), to_chunks(i), to_chunks(log_f)))
    return o.transpose(1, 0, 3, 2, 4).reshape(B, T, H, i.shape[-1])

def mixer(x, w_in, lb, hg_norm_g, sg_ln_g, sg_ln_b, sg_ws, sg_bs, w_branch_a, w_branch_b, w_out):
    B, T, _ = x.shape
    zq, zf, zi, zg, zu, zv, za, zb = jnp.split(x @ w_in, IN_SPLITS, axis=-1)

    f32 = jnp.float32
    lbf = lb.astype(f32)
    zff = zf.astype(f32)
    f = lbf + (1.0 - lbf) * jax.nn.sigmoid(zff)
    log_f = jnp.log(f)
    k = (1.0 - lbf) * jax.nn.sigmoid(-zff)
    hs = lambda a, d: a.reshape(B, T, HG_HEADS, d)
    o = hgrn2_chunkwise(hs(zq.astype(f32), HG_DK), hs(k, HG_DK),
                        hs(zi.astype(f32), HG_DV), hs(log_f, HG_DK))
    o = o * lax.rsqrt(jnp.mean(jnp.square(o), axis=-1, keepdims=True) + RMS_EPS)
    o = o * hg_norm_g.astype(f32).reshape(HG_HEADS, HG_DV)
    o = o.reshape(B, T, HG_V).astype(x.dtype) * jax.nn.silu(zg)
    y_a = o @ w_branch_a

    u = jax.nn.gelu(zu)
    v = layer_norm(jax.nn.gelu(zv), sg_ln_g, sg_ln_b)
    n_chunks = T // SG_CHUNK
    v = v.reshape(B, n_chunks, SG_CHUNK, SG_GROUPS, SG_GROUP_DIM)
    ws = sg_ws * jnp.tril(jnp.ones((SG_CHUNK, SG_CHUNK), sg_ws.dtype))
    mixed = jnp.einsum('gts,bnsgc->bntgc', ws, v) + sg_bs.T[None, None, :, :, None]
    y_b = (u * mixed.reshape(B, T, SG_WIDTH)) @ w_branch_b

    y = jax.nn.sigmoid(za) * y_a + jax.nn.sigmoid(zb) * y_b
    return y @ w_out

def first_inputs(seed: int = 0) -> dict:
    key = jax.random.key(seed)
    ks = jax.random.split(key, 20)
    n = jax.random.normal
    f32 = jnp.float32
    return {
        "x": n(ks[0], (BATCH, SEQ, D_MODEL), f32),
        "ffn1_w13": n(ks[1], (DEPTH, D_MODEL, 2 * D_FF), f32) * D_MODEL ** -0.5,
        "ffn1_w2": n(ks[2], (DEPTH, D_FF, D_MODEL), f32) * (D_FF ** -0.5 * BETA),
        "ffn2_w13": n(ks[3], (DEPTH, D_MODEL, 2 * D_FF), f32) * D_MODEL ** -0.5,
        "ffn2_w2": n(ks[4], (DEPTH, D_FF, D_MODEL), f32) * (D_FF ** -0.5 * BETA),
        "ln_g": 1.0 + 0.02 * n(ks[5], (DEPTH, 3, D_MODEL), f32),
        "ln_b": 0.02 * n(ks[6], (DEPTH, 3, D_MODEL), f32),
        "w_in": n(ks[7], (DEPTH, D_MODEL, D_IN), f32) * D_MODEL ** -0.5,
        "hg_lb": 0.5 * n(ks[8], (DEPTH, HG_K), f32),
        "hg_norm_g": 1.0 + 0.02 * n(ks[9], (DEPTH, HG_V), f32),
        "sg_ln_g": 1.0 + 0.02 * n(ks[10], (DEPTH, SG_WIDTH), f32),
        "sg_ln_b": 0.02 * n(ks[11], (DEPTH, SG_WIDTH), f32),
        "sg_ws": n(ks[12], (DEPTH, SG_GROUPS, SG_CHUNK, SG_CHUNK), f32) * SG_CHUNK ** -0.5,
        "sg_bs": 1.0 + 0.1 * n(ks[13], (DEPTH, SG_GROUPS, SG_CHUNK), f32),
        "w_branch_a": n(ks[14], (DEPTH, HG_V, D_MODEL), f32) * (HG_V ** -0.5 * BETA),
        "w_branch_b": n(ks[15], (DEPTH, SG_WIDTH, D_MODEL), f32) * (SG_WIDTH ** -0.5 * BETA),
        "w_out": n(ks[16], (DEPTH, D_MODEL, D_MODEL), f32) * (D_MODEL ** -0.5 * BETA),
    }

def first_block(x, ffn1_w13, ffn1_w2, ffn2_w13, ffn2_w2, ln_g, ln_b, w_in, hg_lb, hg_norm_g,
              sg_ln_g, sg_ln_b, sg_ws, sg_bs, w_branch_a, w_branch_b, w_out):
    lb_soft = jax.nn.softmax(hg_lb.astype(jnp.float32), axis=0)
    lower_bounds = jnp.cumsum(lb_soft, axis=0) - lb_soft[0]
    for l in range(DEPTH):
        x = layer_norm(ALPHA * x + 0.5 * swiglu(x, ffn1_w13[l], ffn1_w2[l]), ln_g[l, 0], ln_b[l, 0])
        m = mixer(x, w_in[l], lower_bounds[l], hg_norm_g[l], sg_ln_g[l], sg_ln_b[l], sg_ws[l],
                  sg_bs[l], w_branch_a[l], w_branch_b[l], w_out[l])
        x = layer_norm(ALPHA * x + m, ln_g[l, 1], ln_b[l, 1])
        x = layer_norm(ALPHA * x + 0.5 * swiglu(x, ffn2_w13[l], ffn2_w2[l]), ln_g[l, 2], ln_b[l, 2])
    return x


D_MIX = D_MODEL
D_RG = D_MIX // 2
RG_BLOCKS = 8
RG_BLOCK_W = D_RG // RG_BLOCKS
CONV_W = 4
RG_C = 8.0
GLA_HEADS = 4
GLA_VD = D_MIX - D_RG
GLA_KD = GLA_VD // 2
GLA_DK = GLA_KD // GLA_HEADS
GLA_DV = GLA_VD // GLA_HEADS
GLA_RANK = 16
GLA_TAU = 16.0
GLA_CHUNK = 64
D_IN_2 = 2 * D_RG + 2 * GLA_KD + 2 * GLA_VD + GLA_RANK
N_EXPERTS = 8
TOP_K = 2
N_DENSE = (DEPTH + 1) // 2
N_MOE = DEPTH // 2
EPS = 1e-6


def rms_norm(x, g):
    x32 = x.astype(jnp.float32)
    y = x32 * lax.rsqrt(jnp.mean(jnp.square(x32), axis=-1, keepdims=True) + EPS)
    return (y * g.astype(jnp.float32)).astype(x.dtype)

def modulate(h, shift, scale):
    return h * (1.0 + scale) + shift

def causal_depthwise_conv(u, w, b):
    s = u.shape[1]
    up = jnp.pad(u, ((0, 0), (CONV_W - 1, 0), (0, 0)))
    out = b
    for tap in range(CONV_W):
        out = out + up[:, tap:tap + s] * w[tap]
    return out

def _linear_combine(c1, c2):
    a1, b1 = c1
    a2, b2 = c2
    return a1 * a2, a2 * b1 + b2

def rg_lru(u, wa, ba, wx, bx, lam):
    bsz, s, d = u.shape
    ub = u.reshape(bsz, s, RG_BLOCKS, RG_BLOCK_W)
    r = jax.nn.sigmoid((jnp.einsum('bsnd,nde->bsne', ub, wa).reshape(bsz, s, d) + ba).astype(jnp.float32))
    i = jax.nn.sigmoid((jnp.einsum('bsnd,nde->bsne', ub, wx).reshape(bsz, s, d) + bx).astype(jnp.float32))
    log_a = -RG_C * r * jax.nn.softplus(-lam.astype(jnp.float32))
    a = jnp.exp(log_a)
    mult = jnp.sqrt(-jnp.expm1(2.0 * log_a))
    first = (jnp.arange(s) == 0)[None, :, None]
    mult = jnp.where(first, 1.0, mult)
    b_term = mult * i * u.astype(jnp.float32)
    _, h = lax.associative_scan(_linear_combine, (a, b_term), axis=1)
    return h.astype(u.dtype)

def gla_chunked(q, k, v, log_f):
    out_dtype = v.dtype
    bsz, s, nh, dk = q.shape
    dv = v.shape[-1]
    n = s // GLA_CHUNK
    q = q.astype(jnp.float32) * (dk ** -0.5)
    k = k.astype(jnp.float32)
    v = v.astype(jnp.float32)
    q = q.reshape(bsz, n, GLA_CHUNK, nh, dk)
    k = k.reshape(bsz, n, GLA_CHUNK, nh, dk)
    v = v.reshape(bsz, n, GLA_CHUNK, nh, dv)
    b = jnp.cumsum(log_f.astype(jnp.float32).reshape(bsz, n, GLA_CHUNK, nh, dk), axis=2)
    b_last = b[:, :, -1]
    b_ref = b[:, :, GLA_CHUNK // 2 - 1:GLA_CHUNK // 2]
    q_loc = q * jnp.exp(b - b_ref)
    k_loc = k * jnp.exp(b_ref - b)
    scores = jnp.einsum('bnihd,bnjhd->bnhij', q_loc, k_loc)
    causal = jnp.tril(jnp.ones((GLA_CHUNK, GLA_CHUNK), dtype=bool))
    scores = jnp.where(causal, scores, 0.0)
    o_intra = jnp.einsum('bnhij,bnjhv->bnihv', scores, v)
    k_end = k * jnp.exp(b_last[:, :, None] - b)
    u_chunk = jnp.einsum('bnjhd,bnjhv->bnhdv', k_end, v)
    decay = jnp.exp(b_last)

    def step(state, inp):
        dec, upd = inp
        return dec[..., None] * state + upd, state

    init = jnp.zeros((bsz, nh, dk, dv), jnp.float32)
    _, states = lax.scan(step, init, (jnp.moveaxis(decay, 1, 0), jnp.moveaxis(u_chunk, 1, 0)))
    states = jnp.moveaxis(states, 0, 1)
    o_inter = jnp.einsum('bnihd,bnhdv->bnihv', q * jnp.exp(b), states)
    o = (o_intra + o_inter).reshape(bsz, s, nh, dv)
    return o.astype(out_dtype)

def gla_branch(q, k, v, g, f_low, wg2, bg, norm_g):
    bsz, s, _ = q.shape
    log_f = jax.nn.log_sigmoid((f_low @ wg2 + bg).astype(jnp.float32)) / GLA_TAU
    o = gla_chunked(q.reshape(bsz, s, GLA_HEADS, GLA_DK),
                    k.reshape(bsz, s, GLA_HEADS, GLA_DK),
                    v.reshape(bsz, s, GLA_HEADS, GLA_DV),
                    log_f.reshape(bsz, s, GLA_HEADS, GLA_DK))
    o = rms_norm(o, norm_g)
    return o.reshape(bsz, s, GLA_VD) * jax.nn.silu(g)

def hybrid_mixer(h, w_in, conv_w, conv_b, wa, ba, wx, bx, lam, wg2, bg, gla_g, w_out):
    z = h @ w_in
    splits = np.cumsum([D_RG, D_RG, GLA_KD, GLA_KD, GLA_VD, GLA_VD]).tolist()
    rg_x, rg_gate, q, k, v, g, f_low = jnp.split(z, splits, axis=-1)
    u = causal_depthwise_conv(rg_x, conv_w, conv_b)
    rg_out = rg_lru(u, wa, ba, wx, bx, lam) * jax.nn.gelu(rg_gate)
    gla_out = gla_branch(q, k, v, g, f_low, wg2, bg, gla_g)
    return jnp.concatenate([rg_out, gla_out], axis=-1) @ w_out

def swiglu_2(h, w1, w3, w2):
    return (jax.nn.silu(h @ w1) * (h @ w3)) @ w2

def moe_swiglu(h, router_w, w1, w3, w2):
    logits = (h @ router_w).astype(jnp.float32)
    top_v, top_i = lax.top_k(logits, TOP_K)
    probs = jax.nn.softmax(top_v, axis=-1)
    gates = jnp.sum(jax.nn.one_hot(top_i, N_EXPERTS, dtype=jnp.float32) * probs[..., None], axis=-2)
    gates = gates.astype(h.dtype)
    y = jnp.zeros_like(h)
    for e in range(N_EXPERTS):
        y = y + gates[..., e:e + 1] * swiglu_2(h, w1[e], w3[e], w2[e])
    return y

def second_inputs(seed: int = 0) -> dict:
    key = jax.random.key(seed)
    ks = jax.random.split(key, 32)

    def nrm(k, shape, scale):
        return scale * jax.random.normal(k, shape, jnp.float32)

    a0 = jax.random.uniform(ks[13], (DEPTH, D_RG), jnp.float32, 0.9, 0.999)
    a_root = a0 ** (1.0 / RG_C)
    rg_lambda = jnp.log(a_root) - jnp.log1p(-a_root)
    return {
        "x": nrm(ks[0], (BATCH, SEQ, D_MODEL), 1.0),
        "c": nrm(ks[1], (BATCH, D_MODEL), 1.0),
        "ada_w": nrm(ks[2], (DEPTH, D_MODEL, 6 * D_MODEL), 0.5 * D_MODEL ** -0.5),
        "ada_b": nrm(ks[3], (DEPTH, 6 * D_MODEL), 0.01),
        "norm_mix_g": 1.0 + nrm(ks[4], (DEPTH, D_MODEL), 0.05),
        "norm_ffn_g": 1.0 + nrm(ks[5], (DEPTH, D_MODEL), 0.05),
        "w_in": nrm(ks[6], (DEPTH, D_MODEL, D_IN_2), D_MODEL ** -0.5),
        "rg_conv_w": nrm(ks[7], (DEPTH, CONV_W, D_RG), CONV_W ** -0.5),
        "rg_conv_b": nrm(ks[8], (DEPTH, D_RG), 0.01),
        "rg_wa": nrm(ks[9], (DEPTH, RG_BLOCKS, RG_BLOCK_W, RG_BLOCK_W), RG_BLOCK_W ** -0.5),
        "rg_ba": nrm(ks[10], (DEPTH, D_RG), 0.01),
        "rg_wx": nrm(ks[11], (DEPTH, RG_BLOCKS, RG_BLOCK_W, RG_BLOCK_W), RG_BLOCK_W ** -0.5),
        "rg_bx": nrm(ks[12], (DEPTH, D_RG), 0.01),
        "rg_lambda": rg_lambda,
        "gla_wg2": nrm(ks[14], (DEPTH, GLA_RANK, GLA_KD), GLA_RANK ** -0.5),
        "gla_bg": nrm(ks[15], (DEPTH, GLA_KD), 0.1),
        "gla_norm_g": 1.0 + nrm(ks[16], (DEPTH, GLA_DV), 0.05),
        "w_out": nrm(ks[17], (DEPTH, D_MIX, D_MODEL), D_MIX ** -0.5),
        "ffn_w1": nrm(ks[18], (N_DENSE, D_MODEL, D_FF), D_MODEL ** -0.5),
        "ffn_w3": nrm(ks[19], (N_DENSE, D_MODEL, D_FF), D_MODEL ** -0.5),
        "ffn_w2": nrm(ks[20], (N_DENSE, D_FF, D_MODEL), D_FF ** -0.5),
        "router_w": nrm(ks[21], (N_MOE, D_MODEL, N_EXPERTS), D_MODEL ** -0.5),
        "moe_w1": nrm(ks[22], (N_MOE, N_EXPERTS, D_MODEL, D_FF), D_MODEL ** -0.5),
        "moe_w3": nrm(ks[23], (N_MOE, N_EXPERTS, D_MODEL, D_FF), D_MODEL ** -0.5),
        "moe_w2": nrm(ks[24], (N_MOE, N_EXPERTS, D_FF, D_MODEL), D_FF ** -0.5),
        "final_g": 1.0 + nrm(ks[25], (D_MODEL,), 0.05),
    }

def second_block(x, c, ada_w, ada_b, norm_mix_g, norm_ffn_g, w_in, rg_conv_w, rg_conv_b,
              rg_wa, rg_ba, rg_wx, rg_bx, rg_lambda, gla_wg2, gla_bg, gla_norm_g, w_out,
              ffn_w1, ffn_w3, ffn_w2, router_w, moe_w1, moe_w3, moe_w2, final_g):
    c_act = jax.nn.silu(c)
    for layer in range(DEPTH):
        mod = c_act @ ada_w[layer] + ada_b[layer]
        sh_m, sc_m, gt_m, sh_f, sc_f, gt_f = [m[:, None, :] for m in jnp.split(mod, 6, axis=-1)]
        h = modulate(rms_norm(x, norm_mix_g[layer]), sh_m, sc_m)
        mix = hybrid_mixer(h, w_in[layer], rg_conv_w[layer], rg_conv_b[layer],
                           rg_wa[layer], rg_ba[layer], rg_wx[layer], rg_bx[layer], rg_lambda[layer],
                           gla_wg2[layer], gla_bg[layer], gla_norm_g[layer], w_out[layer])
        x = x + gt_m * mix
        h = modulate(rms_norm(x, norm_ffn_g[layer]), sh_f, sc_f)
        j = layer // 2
        if layer % 2 == 0:
            f = swiglu_2(h, ffn_w1[j], ffn_w3[j], ffn_w2[j])
        else:
            f = moe_swiglu(h, router_w[j], moe_w1[j], moe_w3[j], moe_w2[j])
        x = x + gt_f * f
    return rms_norm(x, final_g)


def setup_inputs(seed=0):
    out = dict(first_inputs(seed))
    for name, value in second_inputs(seed + 1).items():
        if name != "x":
            out[name + "_2"] = value
    return out


def reference(
    x, ffn1_w13, ffn1_w2, ffn2_w13, ffn2_w2, ln_g, ln_b, w_in, hg_lb, hg_norm_g, sg_ln_g,
    sg_ln_b, sg_ws, sg_bs, w_branch_a, w_branch_b, w_out, c_2, ada_w_2, ada_b_2, norm_mix_g_2,
    norm_ffn_g_2, w_in_2, rg_conv_w_2, rg_conv_b_2, rg_wa_2, rg_ba_2, rg_wx_2, rg_bx_2,
    rg_lambda_2, gla_wg2_2, gla_bg_2, gla_norm_g_2, w_out_2, ffn_w1_2, ffn_w3_2, ffn_w2_2,
    router_w_2, moe_w1_2, moe_w3_2, moe_w2_2, final_g_2,
):
    x = first_block(
        x, ffn1_w13, ffn1_w2, ffn2_w13, ffn2_w2, ln_g, ln_b, w_in, hg_lb, hg_norm_g, sg_ln_g,
        sg_ln_b, sg_ws, sg_bs, w_branch_a, w_branch_b, w_out,
    )
    return second_block(
        x, c_2, ada_w_2, ada_b_2, norm_mix_g_2, norm_ffn_g_2, w_in_2, rg_conv_w_2, rg_conv_b_2,
        rg_wa_2, rg_ba_2, rg_wx_2, rg_bx_2, rg_lambda_2, gla_wg2_2, gla_bg_2, gla_norm_g_2,
        w_out_2, ffn_w1_2, ffn_w3_2, ffn_w2_2, router_w_2, moe_w1_2, moe_w3_2, moe_w2_2,
        final_g_2,
    )


_drawn_inputs = setup_inputs


def setup_inputs(seed=0):
    import zlib

    import numpy as np

    out = dict(_drawn_inputs(seed))
    spreads = {}
    factors = {'hg_norm_g': 23.731,
     'sg_ln_g': 29.14,
     'sg_ln_b': 28.65,
     'sg_bs': 5.402,
     'rg_conv_b_2': 5.228,
     'rg_ba_2': 64.0,
     'rg_bx_2': 39.403,
     'gla_bg_2': 5.328,
     'gla_norm_g_2': 4.319}
    for name, (base, spread) in spreads.items():
        noise = np.random.default_rng([zlib.crc32(name.encode()), seed]).standard_normal(out[name].shape)
        drawn = base * np.exp(spread * noise) if base else spread * noise
        out[name] = __import__('jax').numpy.asarray(drawn.astype(out[name].dtype))
    for name, factor in factors.items():
        out[name] = (out[name] * factor).astype(out[name].dtype)
    return out
```

```python
from contextlib import ExitStack

import numpy as np

import concourse.bass as bass
from concourse import mybir

F32 = mybir.dt.float32
F32R = mybir.dt.float32r
U8 = mybir.dt.uint8
U32 = mybir.dt.uint32
ACT = mybir.ActivationFunctionType
ALU = mybir.AluOpType

P = 128
SEQ = 256
TILES = SEQ // P
D = 1024
KT = D // P
DEPTH = 2
D_FF = 2816
HEADS = 4
HALF = D // 2
BT = HALF // P
GLA_KD = 256
GLA_DK = GLA_KD // HEADS
GLA_RANK = 16
CONV_W = 4
EXPERTS = 8
CHUNK = 64
FF_CHUNK = 256
FF_TURNS = D_FF // FF_CHUNK
N = 512
UNIT = 4 * N

ALPHA = (2 * DEPTH) ** 0.25
LN_EPS = 1e-5
RMS_EPS = 1e-6
RG_C = 8.0
GLA_TAU = 16.0
LN_SHIFT = 64
LN_LOW = 2.0 ** -60

RAW_SLOTS = 4
SPLIT_SLOTS = 4

COLS = {}
_at = 0
for _name, _n in (("lb", DEPTH * HEADS), ("conv_w", DEPTH * CONV_W * BT), ("conv_b", DEPTH * BT),
                  ("rg_ba", DEPTH * BT), ("rg_bx", DEPTH * BT), ("lam", DEPTH * BT),
                  ("gla_bg", DEPTH * 2), ("sg_bs", DEPTH * HEADS), ("c", KT),
                  ("router", KT * EXPERTS), ("iota", EXPERTS)):
    COLS[_name] = (_at, _n)
    _at += _n
N_COLS = _at

LEVELS = [1, 2, 4, 8, 16, 32, 64, 128]
LOCAL = len(LEVELS)


def level_masks():
    s, t = np.arange(P)[:, None], np.arange(P)[None, :]
    out = np.zeros((P, len(LEVELS) + 1, P), np.float32)
    for i, b in enumerate(LEVELS):
        if b == 1:
            out[:, i] = s == t
        else:
            out[:, i] = (s // b == t // b) & (s % b < b // 2) & (t % b >= b // 2)
    out[:, LOCAL] = (s <= t) & (s // CHUNK == t // CHUNK)
    return out.reshape(P, -1)


class Queue:

    def __init__(self, engine, semaphore):
        self.engine = engine
        self.done = semaphore
        self.count = 0
        self.seen = {}

    def wait(self, *tokens):
        for t in tokens:
            if t is None:
                continue
            if isinstance(t, list):
                self.wait(*t)
                continue
            sem, value = t
            if self.seen.get(id(sem), 0) < value:
                self.seen[id(sem)] = value
                self.engine.wait_ge(sem, value)

    def now(self):
        return (self.done, self.count) if self.count else None

    def free(self, issue, *tokens):
        self.wait(*tokens)
        self.count += 1
        issue(self.engine).then_inc(self.done, 1)
        return self.done, self.count

    def then(self, issue, *tokens):
        return self.free(issue, self.now(), *tokens)

    def quiet(self, issue, *tokens):
        self.wait(*tokens)
        return issue(self.engine)


def build(nc, w, out):
    with ExitStack() as ctx:
        def sb(name, shape, dtype=F32, where=ctx):
            return where.enter_context(nc.sbuf_tensor(name, shape, dtype))

        def sem(name):
            return ctx.enter_context(nc.semaphore(name))

        pe, act = Queue(nc.tensor, sem("pe_done")), Queue(nc.scalar, sem("act_done"))
        dve, pool = Queue(nc.vector, sem("dve_done")), Queue(nc.gpsimd, sem("pool_done"))
        sp = Queue(nc.sync, None)
        small_loaded = sem("small_loaded")
        out_written = sem("out_written")
        raw_loaded = [sem(f"raw_loaded_{i}") for i in range(RAW_SLOTS)]

        banks = [ctx.enter_context(nc.psum_tensor(f"bank{i}", [P, N], F32)) for i in range(8)]
        bank_read = [None] * 8

        raw = sb("raw", [P, RAW_SLOTS, UNIT])
        w_hi = sb("w_hi", [P, SPLIT_SLOTS, UNIT], F32R)
        w_lo = sb("w_lo", [P, SPLIT_SLOTS, UNIT], F32R)
        x = sb("x", [P, TILES, D])
        y = sb("y", [P, TILES, D])
        xt_hi = sb("xt_hi", [P, KT, SEQ], F32R)
        xt_lo = sb("xt_lo", [P, KT, SEQ], F32R)
        ht_hi = sb("ht_hi", [P, 2, SEQ], F32R)
        ht_lo = sb("ht_lo", [P, 2, SEQ], F32R)
        hidden2 = sb("hidden2", [P, 2 * TILES * FF_CHUNK])
        silu_a = hidden2[:, 0:TILES * FF_CHUNK].rearrange("p (t n) -> p t n", t=TILES)
        hidden = hidden2[:, TILES * FF_CHUNK:].rearrange("p (t n) -> p t n", t=TILES)
        ident = sb("ident", [P, P])
        causal = sb("causal", [P, P])
        masks = sb("masks", [P, LOCAL + 1, P], U8)
        cols = sb("cols", [P, N_COLS])
        stats = sb("stats", [P, TILES, 2, 6])
        mean_var = sb("mean_var", [P, TILES, 2])
        rstd = sb("rstd", [P, TILES])
        sums = sb("sums", [P, 8])
        lb = sb("lb", [P, 8, HEADS])
        gates = sb("gates", [P, TILES, EXPERTS])
        tiny = sb("tiny", [P, 64])

        def col(name, i, n=1):
            at = COLS[name][0] + i
            return cols[:, at:at + n]

        small_count = [0]

        def load(dst, src, *tokens):
            pool.wait(*tokens)
            if small_count[0]:
                pool.wait((small_loaded, small_count[0]))
            small_count[0] += 16
            pool.quiet(lambda e: e.dma_start(dst, src).then_inc(small_loaded, 16))
            return small_loaded, small_count[0]

        stream = []

        def product_units(array, first, n):
            stream.extend((array[first + i], UNIT) for i in range(n))

        def feed_forward_units(up, down, first_turn, turns, before, last):
            for j in range(turns):
                product_units(up, 2 * (first_turn + j), 2)
                if before or j:
                    product_units(down, first_turn + j - 1, 1)
            if last:
                product_units(down, first_turn + turns - 1, 1)

        for l in range(DEPTH):
            feed_forward_units(w["ffn1_up"][l], w["ffn1_down"][l], 0, FF_TURNS, False, True)
            product_units(w["mix_in"][l], 0, 20)
            product_units(w["branch_a"][l], 0, 2)
            product_units(w["branch_b"][l], 0, 2)
            product_units(w["mix_out"][l], 0, 4)
            feed_forward_units(w["ffn2_up"][l], w["ffn2_down"][l], 0, FF_TURNS, False, True)
        for l in range(DEPTH):
            product_units(w["ada"][l], 0, 12)
            product_units(w["mix_in_2"][l], 0, 4)
            stream.append((w["mix_in_2_tail"][l], KT * P))
            product_units(w["mix_in_2"][l], 4, 6)
            product_units(w["mix_out_2"][l], 0, 4)
            product_units(w["ada"][l], 12, 12)
            if l % 2 == 0:
                feed_forward_units(w["dense_up"][l // 2], w["dense_down"][l // 2], 0, FF_TURNS, False, True)
            else:
                feed_forward_units(w["moe_up"][l // 2], w["moe_down"][l // 2], 0, EXPERTS * FF_TURNS, False, True)

        used = []
        split = []
        loads = [0]

        def load_unit():
            n = loads[0]
            if n >= len(stream):
                return
            loads[0] += 1
            src, size = stream[n]
            slot = n % RAW_SLOTS
            if n >= RAW_SLOTS:
                sp.wait(split[n - RAW_SLOTS])
            sp.quiet(lambda e: e.dma_start(raw[:, slot, 0:size], src).then_inc(raw_loaded[slot], 16))

        def split_unit():
            n = len(split)
            if n >= len(stream):
                return
            size = stream[n][1]
            src = raw[:, n % RAW_SLOTS, 0:size]
            hi, lo = w_hi[:, n % SPLIT_SLOTS, 0:size], w_lo[:, n % SPLIT_SLOTS, 0:size]
            arrived = (raw_loaded[n % RAW_SLOTS], 16 * (n // RAW_SLOTS + 1))
            free = used[n - SPLIT_SLOTS] if n >= SPLIT_SLOTS else None
            rounded = act.free(lambda e: e.activation(hi, src, ACT.Copy), arrived, free)
            split.append(dve.free(lambda e: e.tensor_tensor(lo, src, hi.bitcast(F32), ALU.subtract),
                                  arrived, free, rounded))
            load_unit()

        for _ in range(RAW_SLOTS):
            load_unit()

        def unit():
            n = len(used)
            while len(split) < min(n + SPLIT_SLOTS, len(stream)):
                split_unit()
            slot = n % SPLIT_SLOTS
            hi = w_hi[:, slot, :].rearrange("p (k n) -> p k n", n=N)
            lo = w_lo[:, slot, :].rearrange("p (k n) -> p k n", n=N)
            return hi, lo, split[n]

        def product(dst, hi_l, lo_l, hi_r, lo_r, start, stop, wait, skip=False):
            for i, (a, b) in enumerate(((hi_l, hi_r), (hi_l, lo_r), (lo_l, hi_r))):
                first, last = start and i == 0, stop and i == 2
                yield lambda e, a=a, b=b, first=first, last=last: e.matmul(
                    dst, a, b, start=first, stop=last, skip_group_check=skip)

        def issue_all(steps, *tokens):
            steps = list(steps)
            pe.wait(*tokens)
            for s in steps[:-1]:
                pe.quiet(s)
            return pe.free(steps[-1])

        def token_block(pair, lhs_hi, lhs_lo, units, kt0=0, *tokens):
            for u in range(units):
                hi, lo, ready = unit()
                for tile in range(TILES):
                    s = []
                    for k in range(4):
                        kt = kt0 + 4 * u + k
                        cut = slice(tile * P, (tile + 1) * P)
                        s += product(banks[pair[tile]][:, :], lhs_hi[:, kt, cut], lhs_lo[:, kt, cut],
                                     hi[:, k, :], lo[:, k, :], u == 0 and k == 0,
                                     u == units - 1 and k == 3, None)
                    done = issue_all(s, ready, bank_read[pair[tile]], *tokens)
                used.append(done)
            return done

        def feature_block(pair, *tokens):
            for u in range(2):
                hi, lo, ready = unit()
                for m in range(4):
                    dst = banks[pair[m // 2]][:, (m % 2) * SEQ:(m % 2 + 1) * SEQ]
                    s = []
                    for k in range(4):
                        kt = 4 * u + k
                        cut = slice(m * P, (m + 1) * P)
                        s += product(dst, hi[:, k, cut], lo[:, k, cut], xt_hi[:, kt, :], xt_lo[:, kt, :],
                                     u == 0 and k == 0 and m % 2 == 0, u == 1 and k == 3, None, skip=True)
                    done = issue_all(s, ready, bank_read[pair[m // 2]], *tokens)
                used.append(done)
            return done

        def evacuate(engine_op, bank, *tokens):
            bank_read[bank] = engine_op
            return engine_op

        def transpose_into(src_of, kts, tile, dst_hi, dst_lo, pair, *tokens):
            done = None
            for g in range(0, len(kts), 4):
                group = kts[g:g + 4]
                b = pair[g // 4]
                bank = banks[b]
                pe.wait(bank_read[b], *tokens)
                for i, (src_i, _) in enumerate(group):
                    step = lambda e, i=i, src_i=src_i: e.transpose(bank[:, i * P:(i + 1) * P], src_of(src_i), ident[:, :])
                    if i == len(group) - 1:
                        turned = pe.free(step)
                    else:
                        pe.quiet(step)
                k0 = group[0][1]
                cut = slice(tile * P, (tile + 1) * P)
                hi = dst_hi[:, k0:k0 + len(group), cut]
                lo = dst_lo[:, k0:k0 + len(group), cut]
                src = bank[:, 0:len(group) * P].rearrange("p (k t) -> p k t", t=P)
                rounded = act.free(lambda e: e.activation(hi, src, ACT.Copy), turned)
                done = dve.free(lambda e: e.tensor_tensor(lo, src, hi.bitcast(F32), ALU.subtract), rounded)
                bank_read[b] = done
            return done

        def rstd_of(dst, src, scale, eps, *tokens):
            t = dve.then(lambda e: e.tensor_scalar(dst, src, scale, eps, ALU.mult, ALU.add), *tokens)
            t = act.then(lambda e: e.activation(dst, dst, ACT.Sqrt), t)
            return dve.then(lambda e: e.reciprocal(dst, dst), t)

        def layer_norm(src, tile, width, gain, shift, params, *tokens):
            n = width // N
            for i in range(n):
                t = dve.then(lambda e, i=i: e.bn_stats(stats[:, tile, i, :], src[:, i * N:(i + 1) * N]), *tokens)
            t = dve.then(lambda e: e.bn_aggr(mean_var[:, tile, :], stats[:, tile, 0:n, :].rearrange("p a b -> p (a b)")), t)
            t = rstd_of(rstd[:, tile:tile + 1], mean_var[:, tile, 1:2], 1.0, LN_EPS, t)
            t = dve.then(lambda e: e.scalar_tensor_tensor(src, src, mean_var[:, tile, 0:1], gain, ALU.subtract, ALU.mult), t, params)
            return dve.then(lambda e: e.scalar_tensor_tensor(src, src, rstd[:, tile:tile + 1], shift, ALU.mult, ALU.add), t)

        def feed_forward(turns, gate_of, x_ready):
            def up(j):
                token_block((0, 1), xt_hi, xt_lo, 2, 0, x_ready)
                last = pe.now()
                ready = None
                for tile in range(TILES):
                    bank = banks[tile]
                    a, b = bank[:, 0:FF_CHUNK], bank[:, FF_CHUNK:N]
                    s = act.free(lambda e, tile=tile, a=a: e.activation(silu_a[:, tile, :], a, ACT.Silu), last)
                    gate = gate_of(j, tile)
                    if gate is None:
                        ready = dve.free(lambda e, tile=tile, b=b: e.tensor_tensor(
                            hidden[:, tile, :], b, silu_a[:, tile, :], ALU.mult), s)
                    else:
                        ready = dve.free(lambda e, tile=tile, b=b, gate=gate: e.scalar_tensor_tensor(
                            hidden[:, tile, :], b, gate, silu_a[:, tile, :], ALU.mult, ALU.mult), s)
                    bank_read[tile] = ready
                return ready

            def turn(ready):
                b = 2
                pe.wait(bank_read[b], ready)
                for k in range(2):
                    for tile in range(TILES):
                        step = lambda e, k=k, tile=tile: e.transpose(
                            banks[b][:, k * SEQ + tile * P:k * SEQ + (tile + 1) * P],
                            hidden[:, tile, k * P:(k + 1) * P], ident[:, :])
                        if k == 1 and tile == 1:
                            turned = pe.free(step)
                        else:
                            pe.quiet(step)
                src = banks[b][:, :].rearrange("p (k t) -> p k t", t=SEQ)
                rounded = act.free(lambda e: e.activation(ht_hi[:, :, :], src, ACT.Copy), turned)
                bank_read[b] = dve.free(lambda e: e.tensor_tensor(
                    ht_lo[:, :, :], src, ht_hi[:, :, :].bitcast(F32), ALU.subtract), rounded)
                return bank_read[b]

            def down(j, ready):
                hi, lo, there = unit()
                s = []
                pe.wait(there, ready)
                for tile in range(TILES):
                    for half in range(2):
                        bank = 4 + 2 * tile + half
                        s = []
                        for k in range(2):
                            cut = slice(tile * P, (tile + 1) * P)
                            s += product(banks[bank][:, :], ht_hi[:, k, cut], ht_lo[:, k, cut],
                                         hi[:, 2 * k + half, :], lo[:, 2 * k + half, :],
                                         j == 0 and k == 0, j == turns - 1 and k == 1, None)
                        done = issue_all(s, bank_read[bank] if j == 0 else None)
                used.append(done)
                return done

            turned = None
            for j in range(turns):
                ready = up(j)
                if j:
                    down(j - 1, turned)
                turned = turn(ready)
            return down(turns - 1, turned)

        def add_scaled_and_normalise(banks_of, scale, params, done):
            for tile in range(TILES):
                for half in range(2):
                    b = banks_of(tile, half)
                    t = act.free(lambda e, tile=tile, half=half, b=b: e.activation(
                        y[:, tile, half * N:(half + 1) * N], banks[b][:, :], ACT.Copy, scale=scale), done)
                    bank_read[b] = t
                t = dve.then(lambda e, tile=tile: e.scalar_tensor_tensor(
                    x[:, tile, :], x[:, tile, :], ALPHA, y[:, tile, :], ALU.mult, ALU.add), t)
                layer_norm(x[:, tile, :], tile, D, ln_p[:, 0, :], ln_p[:, 1, :], params, t)

        def transpose_x(src):
            for tile in range(TILES):
                t = transpose_into(lambda k, tile=tile: src[:, tile, k * P:(k + 1) * P],
                                   [(k, k) for k in range(KT)], tile, xt_hi, xt_lo,
                                   ((0, 1), (2, 3))[tile], dve.now())
            return t

        for tile in range(TILES):
            load(x[:, tile, :], w["x"][tile])
        load(ident[:, :], w["ident"])
        load(causal[:, :], w["causal"])
        y_flat = y[:, :, :].rearrange("p a b -> p (a b)")[:, 0:(LOCAL + 1) * P]
        load(y_flat, w["masks"])
        consts_in = load(cols[:, :], w["cols"])
        pe.wait(consts_in)
        dve.wait(consts_in)
        act.wait(consts_in)
        dve.then(lambda e: e.tensor_copy(masks[:, :, :].rearrange("p a b -> p (a b)"), y_flat))

        L = lambda i: lb[:, i, :]
        raw_lb = lambda l: col("lb", l * HEADS, HEADS)
        dve.then(lambda e: e.tensor_tensor(L(2), raw_lb(0), raw_lb(1), ALU.max))
        dve.then(lambda e: e.tensor_tensor(L(0), raw_lb(0), L(2), ALU.subtract))
        t = dve.then(lambda e: e.tensor_tensor(L(1), raw_lb(1), L(2), ALU.subtract))
        t = act.then(lambda e: e.activation(lb[:, 0:2, :], lb[:, 0:2, :], ACT.Exp), t)
        dve.then(lambda e: e.tensor_tensor(L(2), L(0), L(1), ALU.add), t)
        dve.then(lambda e: e.reciprocal(L(2), L(2)))
        dve.then(lambda e: e.tensor_tensor(L(0), L(0), L(2), ALU.mult))
        dve.then(lambda e: e.tensor_tensor(L(1), L(1), L(2), ALU.mult))
        dve.then(lambda e: e.tensor_tensor(L(3), L(0), L(1), ALU.add))
        dve.then(lambda e: e.tensor_tensor(L(4), L(0), L(0), ALU.subtract))
        dve.then(lambda e: e.tensor_tensor(L(5), L(3), L(0), ALU.subtract))
        dve.then(lambda e: e.tensor_scalar(lb[:, 6:8, :], lb[:, 4:6, :], -1.0, 1.0, ALU.mult, ALU.add))

        def level(bc, diff, scale, block, groups, plain_right):
            half = block // 2
            n = groups * SEQ // block
            v = bc.rearrange("p h t -> p (h t)").rearrange("p (n b) -> p n b", b=block)
            d = diff.rearrange("p h t -> p (h t)").rearrange("p (n b) -> p n b", b=block)
            left, right, mid = v[:, :, 0:half], v[:, :, half:], v[:, :, half - 1:half].broadcast_to([P, n, half])
            t = dve.then(lambda e: e.tensor_tensor(d[:, :, 0:half], mid, left, ALU.subtract))
            if plain_right:
                t = dve.then(lambda e: e.tensor_copy(d[:, :, half:], right))
            else:
                t = dve.then(lambda e: e.tensor_tensor(d[:, :, half:], right, mid, ALU.subtract))
            t = act.then(lambda e: e.activation(diff, diff, ACT.Exp, scale=scale), t)
            return d, half, t

        def attend(scores, scores_x, v_of, values_ready):
            for tile in range(TILES):
                s = []
                for h in range(HEADS):
                    cut = slice(h * P, (h + 1) * P)
                    s.append(lambda e, tile=tile, h=h, cut=cut: e.matmul(
                        banks[2 + tile][:, cut], scores[:, tile * HEADS + h, :], v_of(tile)[:, cut],
                        start=True, stop=tile == 0))
                    if tile:
                        s.append(lambda e, h=h, cut=cut: e.matmul(
                            banks[3][:, cut], scores_x[:, h, :], v_of(0)[:, cut], start=False, stop=True))
                done = issue_all(s, bank_read[2 + tile], *values_ready)
            return done

        def head_norm(done, gain_of, gate, dst, params, junk):
            for tile in range(TILES):
                for h in range(HEADS):
                    cut = slice(h * P, (h + 1) * P)
                    t = act.free(lambda e, tile=tile, h=h, cut=cut: e.activation(
                        junk[:, cut], banks[2 + tile][:, cut], ACT.Square,
                        accum_out=sums[:, tile * HEADS + h:tile * HEADS + h + 1]), done, dve.now(), act.now())
            t = rstd_of(sums[:, :], sums[:, :], 1.0 / P, RMS_EPS, t)
            for tile in range(TILES):
                for h in range(HEADS):
                    i = tile * HEADS + h
                    cut = slice(h * P, (h + 1) * P)
                    t = dve.then(lambda e, tile=tile, cut=cut, i=i, h=h: e.scalar_tensor_tensor(
                        dst[:, tile, cut], banks[2 + tile][:, cut], sums[:, i:i + 1], gain_of(h),
                        ALU.mult, ALU.mult), params)
                bank_read[2 + tile] = t
                t = dve.then(lambda e, tile=tile: e.tensor_tensor(
                    dst[:, tile, :], dst[:, tile, :], gate[:, tile, :], ALU.mult), act.now())
            return t

        def take_scores(scores, index, bank_tokens):
            for tile in range(TILES):
                mask = masks[:, index:index + 1, :].broadcast_to([P, HEADS, P])
                bank_read[2 + tile] = dve.then(lambda e, tile=tile, mask=mask: e.copy_predicated(
                    scores[:, tile * HEADS:(tile + 1) * HEADS, :], mask,
                    banks[2 + tile][:, :].rearrange("p (h t) -> p h t", t=P)), bank_tokens)

        def score_products(k_of, q_of, ready):
            s = []
            pe.wait(bank_read[2], bank_read[3])
            for tile in range(TILES):
                for h in range(HEADS):
                    cut = slice(tile * P, (tile + 1) * P)
                    s.append(lambda e, tile=tile, h=h, cut=cut: e.matmul(
                        banks[2 + tile][:, h * P:(h + 1) * P], k_of(h)[:, cut], q_of(h)[:, cut],
                        start=True, stop=True))
            return issue_all(s, ready)

        def cross_products(scores_x, k_of, q_of, ready):
            s = [lambda e, h=h: e.matmul(banks[2][:, h * P:(h + 1) * P], k_of(h)[:, 0:P], q_of(h)[:, P:SEQ],
                                         start=True, stop=True) for h in range(HEADS)]
            done = issue_all(s, ready, bank_read[2])
            bank_read[2] = act.then(lambda e: e.activation(
                scores_x[:, :, :], banks[2][:, :].rearrange("p (h t) -> p h t", t=P), ACT.Copy), done)
            return bank_read[2]

        def restart_mask(tile, n, *tokens):
            t = pool.then(lambda e: e.memset(tile[:, 0:n], 1.0), *tokens)
            return pool.then(lambda e: e.memset(tile[:, 0:n].rearrange("p (c t) -> p c t", t=CHUNK)[:, :, 0:1], 0.0), t)

        def all_done():
            return [t for t in (pe.now(), act.now(), dve.now(), pool.now()) if t]

        first = ExitStack()
        with first:
            def sb1(name, shape, dtype=F32):
                return sb(name, shape, dtype, first)

            ln_p = sb1("ln_p", [P, 2, D])
            q_t = sb1("q_t", [P, HEADS, SEQ])
            k_t = sb1("k_t", [P, HEADS, SEQ])
            logf = sb1("logf", [P, HEADS, SEQ])
            bc = sb1("bc", [P, HEADS, SEQ])
            qe = sb1("qe", [P, HEADS, SEQ])
            ke = sb1("ke", [P, HEADS, SEQ])
            scores = sb1("scores", [P, TILES * HEADS, P])
            scores_x = sb1("scores_x", [P, HEADS, P])
            values = sb1("values", [P, TILES, HALF])
            gate_g = sb1("gate_g", [P, TILES, HALF])
            u_sg = sb1("u_sg", [P, TILES, HALF])
            v_sg = sb1("v_sg", [P, TILES, HALF])
            sig_b = sb1("sig_b", [P, TILES, D])
            ws = sb1("ws", [P, HEADS, P])

            flat = lambda a: a[:, :, :].rearrange("p a b -> p (a b)")
            ln_flat = flat(ln_p)
            hg_gain, sg_gain, sg_shift = (ln_flat[:, i * HALF:(i + 1) * HALF] for i in range(3))

            def load_ln(l, i, *tokens):
                load(ln_p[:, 0, :], w["ln_g"][l, i, :].partition_broadcast(P), *tokens)
                return load(ln_p[:, 1, :], w["ln_b"][l, i, :].partition_broadcast(P))

            def hgrn(l, fed):
                f_pair, f_done = fed["f"]
                for i in range(2):
                    src = banks[f_pair[i]][:, :].rearrange("p (m t) -> p m t", t=SEQ)
                    act.then(lambda e, i=i, src=src: e.activation(logf[:, 2 * i:2 * i + 2, :], src, ACT.Sigmoid), f_done)
                    t = act.then(lambda e, i=i, src=src: e.activation(k_t[:, 2 * i:2 * i + 2, :], src, ACT.Sigmoid, scale=-1.0))
                    bank_read[f_pair[i]] = t
                for h in range(HEADS):
                    less, bound = lb[:, 6 + l, h:h + 1], lb[:, 4 + l, h:h + 1]
                    dve.then(lambda e, h=h, less=less, bound=bound: e.tensor_scalar(
                        logf[:, h, :], logf[:, h, :], less, bound, ALU.mult, ALU.add), t)
                    f_set = dve.then(lambda e, h=h, less=less: e.tensor_scalar(
                        k_t[:, h, :], k_t[:, h, :], less, None, ALU.mult))
                yield
                t = act.then(lambda e: e.activation(flat(qe), flat(logf), ACT.Ln, scale=2.0 ** LN_SHIFT), f_set)
                dve.then(lambda e: e.tensor_scalar(flat(ke).bitcast(U32), flat(logf), LN_LOW, None, ALU.is_lt))
                low = dve.then(lambda e: e.tensor_scalar(flat(qe), flat(qe), -LN_SHIFT * float(np.log(2.0)), None, ALU.add), t)
                t = act.then(lambda e: e.activation(flat(logf), flat(logf), ACT.Ln), low)
                t = dve.then(lambda e: e.copy_predicated(flat(logf), flat(ke).bitcast(U32), flat(qe)), t)
                restart = restart_mask(flat(qe), HEADS * SEQ, t)
                t = dve.then(lambda e: e.tensor_tensor_scan(flat(bc), flat(qe), flat(logf), 0.0, ALU.mult, ALU.add), restart)
                q_pair, q_done = fed["q"]
                for i in range(2):
                    src = banks[q_pair[i]][:, :].rearrange("p (m t) -> p m t", t=SEQ)
                    bank_read[q_pair[i]] = act.then(lambda e, i=i, src=src: e.activation(
                        q_t[:, 2 * i:2 * i + 2, :], src, ACT.Copy), q_done)
                zeroed = pool.then(lambda e: e.memset(scores[:, :, :], 0.0), pe.now())
                yield
                for index, block in enumerate(LEVELS + [SEQ]):
                    if block == 1:
                        ready = score_products(lambda h: k_t[:, h, :], lambda h: q_t[:, h, :],
                                               [act.now(), dve.now()])
                    else:
                        d, half, decays = level(bc[:, :, :], logf[:, :, :], 1.0, block, HEADS, block >= P)
                        view = lambda a: flat(a).rearrange("p (n b) -> p n b", b=block)
                        dve.then(lambda e: e.tensor_tensor(view(qe)[:, :, half:], view(q_t)[:, :, half:], d[:, :, half:], ALU.mult),
                                 decays, pe.now())
                        t = dve.then(lambda e: e.tensor_tensor(view(ke)[:, :, 0:half], view(k_t)[:, :, 0:half], d[:, :, 0:half], ALU.mult))
                        pair = (lambda h: ke[:, h, :], lambda h: qe[:, h, :], t)
                        if block == SEQ:
                            crossed = cross_products(scores_x, *pair)
                            break
                        ready = score_products(*pair)
                    if block == P:
                        v = flat(bc).rearrange("p (n c t) -> p n c t", c=2, t=CHUNK)
                        last = v[:, :, 0, CHUNK - 1:CHUNK].broadcast_to([P, HEADS * TILES, CHUNK])
                        dve.then(lambda e: e.tensor_tensor(v[:, :, 1, :], v[:, :, 1, :], last, ALU.add))
                    yield
                    take_scores(scores, index, [ready, zeroed])
                fed["scored"] = [crossed, dve.now()]

            for l in range(DEPTH):
                params = load_ln(l, 0, *all_done())
                if l == 0:
                    transpose_x(x)
                done = feed_forward(FF_TURNS, lambda j, tile: None, dve.now())
                add_scaled_and_normalise(lambda tile, half: 4 + 2 * tile + half, 0.5, params, done)
                x_ready = transpose_x(x)

                normed = dve.now()
                load(hg_gain, w["hg_norm_g"][l].partition_broadcast(P), normed)
                load(sg_gain, w["sg_ln_g"][l].partition_broadcast(P))
                load(ws[:, :, :], w["sg_ws_t"][l], pe.now())
                params = load(sg_shift, w["sg_ln_b"][l].partition_broadcast(P))
                fed = {}
                fed["f"] = ((4, 5), feature_block((4, 5), x_ready))
                recurrence = hgrn(l, fed)
                next(recurrence)
                fed["q"] = ((6, 7), feature_block((6, 7)))
                next(recurrence)
                done = token_block((0, 1), xt_hi, xt_lo, 2)
                for tile in range(TILES):
                    bank_read[tile] = act.free(lambda e, tile=tile: e.activation(
                        values[:, tile, :], banks[tile][:, :], ACT.Copy), done)
                values_in = act.now()
                next(recurrence)

                done = token_block((4, 5), xt_hi, xt_lo, 2)
                for tile in range(TILES):
                    bank_read[4 + tile] = act.free(lambda e, tile=tile: e.activation(
                        v_sg[:, tile, :], banks[4 + tile][:, :], ACT.Gelu_apprx_tanh), done)
                v_in = act.now()
                next(recurrence)
                done = token_block((6, 7), xt_hi, xt_lo, 2)
                for tile in range(TILES):
                    bank_read[6 + tile] = act.free(lambda e, tile=tile: e.activation(
                        u_sg[:, tile, :], banks[6 + tile][:, :], ACT.Gelu_apprx_tanh), done)
                u_in = act.now()
                for tile in range(TILES):
                    layer_norm(v_sg[:, tile, :], tile, HALF, sg_gain, sg_shift, params, v_in)
                for h in range(HEADS):
                    dve.then(lambda e, h=h: e.tensor_tensor(ws[:, h, :], ws[:, h, :], causal[:, :], ALU.mult))
                v_ready = dve.now()
                next(recurrence)
                done = token_block((0, 1), xt_hi, xt_lo, 2)
                for tile in range(TILES):
                    bank_read[tile] = act.free(lambda e, tile=tile: e.activation(
                        gate_g[:, tile, :], banks[tile][:, :], ACT.Silu), done)
                next(recurrence)
                s = []
                for tile in range(TILES):
                    for h in range(HEADS):
                        cut = slice(h * P, (h + 1) * P)
                        s.append(lambda e, tile=tile, h=h, cut=cut: e.matmul(
                            banks[4 + tile][:, cut], ws[:, h, :], v_sg[:, tile, cut], start=True, stop=True))
                mixed = issue_all(s, v_ready, bank_read[4], bank_read[5])
                for tile in range(TILES):
                    for h in range(HEADS):
                        cut = slice(h * P, (h + 1) * P)
                        bank_read[4 + tile] = dve.then(lambda e, tile=tile, h=h, cut=cut: e.scalar_tensor_tensor(
                            u_sg[:, tile, cut], banks[4 + tile][:, cut], col("sg_bs", l * HEADS + h), u_sg[:, tile, cut],
                            ALU.add, ALU.mult), mixed, u_in)
                for i, pair in enumerate(((6, 7), (0, 1), (4, 5), (6, 7))):
                    done = token_block(pair, xt_hi, xt_lo, 2)
                    dst = (y, sig_b)[i // 2]
                    for tile in range(TILES):
                        bank_read[pair[tile]] = act.free(lambda e, tile=tile, i=i, dst=dst, pair=pair: e.activation(
                            dst[:, tile, (i % 2) * N:(i % 2 + 1) * N], banks[pair[tile]][:, :], ACT.Sigmoid), done)
                    next(recurrence)
                for _ in recurrence:
                    pass
                done = attend(scores, scores_x, lambda tile: values[:, tile, :], [*fed["scored"], values_in])
                o = flat(qe).rearrange("p (t n) -> p t n", t=TILES)
                head_norm(done, lambda h: hg_gain[:, h * P:(h + 1) * P], gate_g, o, params, flat(ke))
                for tile in range(TILES):
                    transpose_into(lambda k, tile=tile: u_sg[:, tile, k * P:(k + 1) * P],
                                   [(k, BT + k) for k in range(BT)], tile, xt_hi, xt_lo, (tile,), dve.now())
                for tile in range(TILES):
                    t = transpose_into(lambda k, tile=tile, o=o: o[:, tile, k * P:(k + 1) * P],
                                       [(k, k) for k in range(BT)], tile, xt_hi, xt_lo, (2 + tile,), dve.now())
                params = load_ln(l, 1, dve.now())
                for branch in range(2):
                    for half in range(2):
                        pair = (4, 5) if half == 0 else (6, 7)
                        done = token_block(pair, xt_hi, xt_lo, 1, branch * BT, t)
                        for tile in range(TILES):
                            cut = slice(half * N, (half + 1) * N)
                            if branch == 0:
                                bank_read[pair[tile]] = dve.then(lambda e, tile=tile, cut=cut, b=pair[tile]: e.tensor_tensor(
                                    y[:, tile, cut], banks[b][:, :], y[:, tile, cut], ALU.mult), done)
                            else:
                                bank_read[pair[tile]] = dve.then(lambda e, tile=tile, cut=cut, b=pair[tile]: e.tensor_tensor(
                                    sig_b[:, tile, cut], banks[b][:, :], sig_b[:, tile, cut], ALU.mult), done)
                                dve.then(lambda e, tile=tile, cut=cut: e.tensor_tensor(
                                    y[:, tile, cut], y[:, tile, cut], sig_b[:, tile, cut], ALU.add))
                t = transpose_x(y)
                token_block((4, 6), xt_hi, xt_lo, 2, 0, t)
                done = token_block((5, 7), xt_hi, xt_lo, 2)
                add_scaled_and_normalise(lambda tile, half: 4 + 2 * tile + half, 1.0, params, done)
                params = load_ln(l, 2, dve.now())
                x_ready = transpose_x(x)

                done = feed_forward(FF_TURNS, lambda j, tile: None, x_ready)
                add_scaled_and_normalise(lambda tile, half: 4 + 2 * tile + half, 0.5, params, done)
                if l < DEPTH - 1:
                    transpose_x(x)

        second = ctx.enter_context(ExitStack())

        def sb2(name, shape, dtype=F32):
            return sb(name, shape, dtype, second)

        norm_g = sb2("norm_g", [P, D])
        sh = sb2("sh", [P, D])
        sc = sb2("sc", [P, D])
        gt = [sb2(f"gt_{n}", [P, D]) for n in ("mix", "ffn")]
        c_hi = sb2("c_hi", [P, KT, P], F32R)
        c_lo = sb2("c_lo", [P, KT, P], F32R)
        router_hi = sb2("router_hi", [P, KT, EXPERTS], F32R)
        router_lo = sb2("router_lo", [P, KT, EXPERTS], F32R)
        decay_c = sb2("decay_c", [P, 8, DEPTH * BT])
        g_norm = sb2("g_norm", [P, P])
        wg2 = sb2("wg2", [GLA_RANK, GLA_KD])
        block_w = sb2("block_w", [P, 2 * BT, P])
        x_pad = sb2("x_pad", [P, BT, SEQ + CONV_W - 1])
        u_rg = sb2("u_rg", [P, BT, SEQ])
        r_rg = sb2("r_rg", [P, BT, SEQ])
        th_rg = sb2("th_rg", [P, BT, SEQ])
        i_rg = sb2("i_rg", [P, BT, SEQ])
        q_g = sb2("q_g", [P, 2, SEQ])
        k_g = sb2("k_g", [P, 2, SEQ])
        lf_g = sb2("lf_g", [P, 2, SEQ])
        bc_g = sb2("bc_g", [P, 2, SEQ])
        ke_g = sb2("ke_g", [P, 2, SEQ])
        scores = sb2("scores_2", [P, TILES * HEADS, P])
        scores_x = sh[:, 0:HEADS * P].rearrange("p (h t) -> p h t", t=P)
        qe_g = hidden2[:, :].rearrange("p (h t) -> p h t", t=SEQ)
        values = flat(y)[:, 0:TILES * HALF].rearrange("p (t n) -> p t n", t=TILES)
        gate_g = flat(y)[:, TILES * HALF:].rearrange("p (t n) -> p t n", t=TILES)

        over = all_done() + [(small_loaded, small_count[0])]
        for q in (act, dve, pool):
            q.wait(*over)

        t = act.then(lambda e: e.activation(tiny[:, 0:KT], col("c", 0, KT), ACT.Silu))
        wide = tiny[:, 0:KT].unsqueeze(2).broadcast_to([P, KT, P])
        t = act.then(lambda e: e.activation(c_hi[:, :, :], wide, ACT.Copy), t)
        c_ready = dve.then(lambda e: e.tensor_tensor(c_lo[:, :, :], wide, c_hi[:, :, :].bitcast(F32), ALU.subtract), t)
        router = col("router", 0, KT * EXPERTS).rearrange("p (k e) -> p k e", e=EXPERTS)
        t = act.then(lambda e: e.activation(router_hi[:, :, :], router, ACT.Copy))
        router_ready = dve.then(lambda e: e.tensor_tensor(router_lo[:, :, :], router, router_hi[:, :, :].bitcast(F32), ALU.subtract), t)

        R = lambda i: decay_c[:, i, :]
        lam = col("lam", 0, DEPTH * BT)
        t = act.then(lambda e: e.activation(R(1), lam, ACT.Abs))
        t = act.then(lambda e: e.activation(R(1), R(1), ACT.Exp, scale=-1.0), t)
        dve.then(lambda e: e.tensor_scalar(R(2), R(1), 2.0, None, ALU.add), t)
        dve.then(lambda e: e.reciprocal(R(2), R(2)))
        dve.then(lambda e: e.tensor_tensor(R(1), R(1), R(2), ALU.mult))
        dve.then(lambda e: e.tensor_tensor(R(2), R(1), R(1), ALU.mult))
        dve.then(lambda e: e.memset(R(3), 1.0 / 19))
        for n in range(17, 0, -2):
            dve.then(lambda e: e.tensor_tensor(R(3), R(3), R(2), ALU.mult))
            dve.then(lambda e, n=n: e.tensor_scalar(R(3), R(3), 1.0 / n, None, ALU.add))
        dve.then(lambda e: e.tensor_tensor(R(3), R(3), R(1), ALU.mult))
        dve.then(lambda e: e.tensor_scalar(R(4), lam, -1.0, 0.0, ALU.mult, ALU.max))
        dve.then(lambda e: e.scalar_tensor_tensor(R(0), R(3), 2.0, R(4), ALU.mult, ALU.add))
        dve.then(lambda e: e.tensor_scalar(R(5), R(0), -RG_C, None, ALU.mult))
        dve.then(lambda e: e.tensor_scalar(R(0), R(0), RG_C, None, ALU.mult))
        pool.then(lambda e: e.memset(x_pad[:, :, 0:CONV_W - 1], 0.0))

        def modulation(l, part):
            targets = (sh, sc, gt[part])
            for i, tile in enumerate(targets):
                bias = load(tile[:, :], w["ada_b"][l, (3 * part + i) * D:(3 * part + i + 1) * D].partition_broadcast(P),
                            dve.now())
            for i, tile in enumerate(targets):
                for half in range(2):
                    b = (0, 1)[half]
                    for u in range(2):
                        hi, lo, ready = unit()
                        s = []
                        for k in range(4):
                            kt = 4 * u + k
                            s += product(banks[b][:, :], c_hi[:, kt, :], c_lo[:, kt, :], hi[:, k, :], lo[:, k, :],
                                         u == 0 and k == 0, u == 1 and k == 3, None)
                        done = issue_all(s, ready, c_ready, bank_read[b])
                        used.append(done)
                    cut = slice(half * N, (half + 1) * N)
                    bank_read[b] = dve.then(lambda e, tile=tile, cut=cut, b=b: e.tensor_tensor(
                        tile[:, cut], banks[b][:, :], tile[:, cut], ALU.add), done, bias)

        def rms_rstd(*tokens):
            for tile in range(TILES):
                t = act.then(lambda e, tile=tile: e.activation(y[:, tile, :], x[:, tile, :], ACT.Square,
                                                               accum_out=rstd[:, tile:tile + 1]), dve.now(), *tokens)
            return rstd_of(rstd[:, :], rstd[:, :], 1.0 / D, RMS_EPS, t)

        def modulated(params):
            dve.then(lambda e: e.scalar_tensor_tensor(sc[:, :], sc[:, :], 1.0, norm_g[:, :], ALU.add, ALU.mult), params)
            for tile in range(TILES):
                dve.then(lambda e, tile=tile: e.scalar_tensor_tensor(
                    y[:, tile, :], x[:, tile, :], rstd[:, tile:tile + 1], sc[:, :], ALU.mult, ALU.mult))
                dve.then(lambda e, tile=tile: e.tensor_tensor(y[:, tile, :], y[:, tile, :], sh[:, :], ALU.add))
            return transpose_x(y)

        def add_gated(part, done):
            for tile in range(TILES):
                for half in range(2):
                    b = 4 + 2 * tile + half
                    cut = slice(half * N, (half + 1) * N)
                    bank_read[b] = dve.then(lambda e, tile=tile, cut=cut, b=b: e.tensor_tensor(
                        y[:, tile, cut], banks[b][:, :], gt[part][:, cut], ALU.mult), done)
                dve.then(lambda e, tile=tile: e.tensor_tensor(x[:, tile, :], x[:, tile, :], y[:, tile, :], ALU.add))

        head_rows = lambda h: slice((h % 2) * GLA_DK, (h % 2 + 1) * GLA_DK)

        for l in range(DEPTH):
            params = load(norm_g[:, :], w["norm_mix_g"][l].partition_broadcast(P), dve.now())
            rms_rstd()
            modulation(l, 0)
            x_ready = modulated(params)
            free = all_done()
            load(g_norm[:, :], w["gla_norm_g"][l].partition_broadcast(P), *free)
            load(wg2[:, :], w["gla_wg2"][l])
            params = load(block_w[:, :, :], w["rg_w"][l])
            norm_f = load(norm_g[:, :], w["norm_ffn_g"][l].partition_broadcast(P))

            done = feature_block((4, 5), x_ready)
            for i in range(2):
                src = banks[4 + i][:, :].rearrange("p (m t) -> p m t", t=SEQ)
                bank_read[4 + i] = act.then(lambda e, i=i, src=src: e.activation(
                    x_pad[:, 2 * i:2 * i + 2, CONV_W - 1:], src, ACT.Copy), done, free, pool.now())
            t = act.now()
            for f in range(BT):
                tap = lambda n, f=f: (x_pad[:, f, n:n + SEQ], col("conv_w", (l * CONV_W + n) * BT + f))
                dve.then(lambda e, f=f, tap=tap: e.tensor_scalar(
                    u_rg[:, f, :], tap(0)[0], tap(0)[1], col("conv_b", l * BT + f), ALU.mult, ALU.add), t)
                for n in range(1, CONV_W):
                    dve.then(lambda e, f=f, n=n, tap=tap: e.scalar_tensor_tensor(
                        u_rg[:, f, :], tap(n)[0], tap(n)[1], u_rg[:, f, :], ALU.mult, ALU.add))
            u_ready = dve.now()
            done = feature_block((6, 7))
            for i, dst in enumerate((q_g, k_g)):
                src = banks[6 + i][:, :].rearrange("p (m t) -> p m t", t=SEQ)
                bank_read[6 + i] = act.then(lambda e, i=i, src=src, dst=dst: e.activation(
                    dst[:, :, :], src, ACT.Copy, scale=(GLA_DK ** -0.5, 1.0)[i]), done)

            hi, lo, ready = unit()
            s = []
            tail = lambda a: a.rearrange("p k n -> p (k n)")[:, 0:KT * P].rearrange("p (k n) -> p k n", n=P)
            for k in range(KT):
                s += product(banks[0][:, 0:SEQ], tail(hi)[:, k, :], tail(lo)[:, k, :], xt_hi[:, k, :], xt_lo[:, k, :],
                             k == 0, k == KT - 1, None)
            done = issue_all(s, ready, bank_read[0])
            used.append(done)
            bank_read[0] = t = act.then(lambda e: e.activation(ke_g[0:GLA_RANK, 0, :], banks[0][0:GLA_RANK, 0:SEQ], ACT.Copy), done, free)
            s = [lambda e, m=m: e.matmul(banks[1][:, m * SEQ:(m + 1) * SEQ], wg2[:, m * P:(m + 1) * P],
                                         ke_g[0:GLA_RANK, 0, :], start=True, stop=True) for m in range(2)]
            done = issue_all(s, t, params, bank_read[1])
            for m in range(2):
                bank_read[1] = dve.then(lambda e, m=m: e.tensor_scalar(
                    lf_g[:, m, :], banks[1][:, m * SEQ:(m + 1) * SEQ], col("gla_bg", l * 2 + m), None, ALU.add), done, free)
            act.then(lambda e: e.activation(flat(bc_g), flat(lf_g), ACT.Abs), dve.now())
            t = act.then(lambda e: e.activation(flat(bc_g), flat(bc_g), ACT.Exp, scale=-1.0))
            t = dve.then(lambda e: e.tensor_scalar(flat(bc_g), flat(bc_g), 1.0, None, ALU.add), t)
            t = act.then(lambda e: e.activation(flat(bc_g), flat(bc_g), ACT.Ln), t)
            t = dve.then(lambda e: e.scalar_tensor_tensor(flat(lf_g), flat(lf_g), 0.0, flat(bc_g), ALU.min, ALU.subtract), t)
            restart = restart_mask(flat(ke_g), 2 * SEQ, t, pe.now())
            dve.then(lambda e: e.tensor_tensor_scan(flat(bc_g), flat(ke_g), flat(lf_g), 0.0, ALU.mult, ALU.add), restart)

            for g, (dst, bias) in enumerate(((r_rg, "rg_ba"), (i_rg, "rg_bx"))):
                s = [lambda e, f=f, g=g: e.matmul(banks[2 + f // 2][:, (f % 2) * SEQ:(f % 2 + 1) * SEQ],
                                                  block_w[:, g * BT + f, :], u_rg[:, f, :], start=True, stop=True)
                     for f in range(BT)]
                done = issue_all(s, u_ready, params, bank_read[2], bank_read[3])
                for f in range(BT):
                    bank_read[2 + f // 2] = act.then(lambda e, f=f, dst=dst, bias=bias: e.activation(
                        dst[:, f, :], banks[2 + f // 2][:, (f % 2) * SEQ:(f % 2 + 1) * SEQ], ACT.Sigmoid,
                        bias=col(bias, l * BT + f)), done)
            gates_in = act.now()

            done = token_block((0, 1), xt_hi, xt_lo, 2)
            for tile in range(TILES):
                bank_read[tile] = act.free(lambda e, tile=tile: e.activation(
                    values[:, tile, :], banks[tile][:, :], ACT.Copy), done)
            values_in = act.now()
            for f in range(BT):
                act.then(lambda e, f=f: e.activation(th_rg[:, f, :], r_rg[:, f, :], ACT.Tanh, scale=decay_c[:, 0, l * BT + f:l * BT + f + 1]))
            for f in range(BT):
                t = act.then(lambda e, f=f: e.activation(r_rg[:, f, :], r_rg[:, f, :], ACT.Exp, scale=decay_c[:, 5, l * BT + f:l * BT + f + 1]))
            spare = flat(x_pad)[:, 0:BT * SEQ]
            dve.then(lambda e: e.tensor_scalar(spare, flat(th_rg), 1.0, None, ALU.add), t)
            dve.then(lambda e: e.reciprocal(spare, spare))
            t = dve.then(lambda e: e.scalar_tensor_tensor(flat(th_rg), flat(th_rg), 2.0, spare, ALU.mult, ALU.mult))
            t = act.then(lambda e: e.activation(flat(th_rg), flat(th_rg), ACT.Sqrt), t)
            dve.then(lambda e: e.memset(th_rg[:, :, 0:1], 1.0), t)
            dve.then(lambda e: e.memset(r_rg[:, :, 0:1], 0.0))
            dve.then(lambda e: e.tensor_tensor(flat(i_rg), flat(i_rg), flat(th_rg), ALU.mult), gates_in)
            dve.then(lambda e: e.tensor_tensor(flat(i_rg), flat(i_rg), flat(u_rg), ALU.mult))
            dve.then(lambda e: e.tensor_tensor_scan(flat(u_rg), flat(r_rg), flat(i_rg), 0.0, ALU.mult, ALU.add))
            h_ready = dve.now()
            pad_again = pool.then(lambda e: e.memset(x_pad[:, :, 0:CONV_W - 1], 0.0), h_ready)

            zeroed = pool.then(lambda e: e.memset(qe_g, 0.0), all_done())
            zeroed = pool.then(lambda e: e.memset(scores[:, :, :], 0.0))
            mid = flat(bc_g).rearrange("p (n b) -> p n b", b=CHUNK)[:, :, CHUNK // 2 - 1:CHUNK // 2].broadcast_to([P, 2 * SEQ // CHUNK, CHUNK])
            chunks = lambda a: flat(a).rearrange("p (n b) -> p n b", b=CHUNK)
            t = dve.then(lambda e: e.tensor_tensor(chunks(lf_g), chunks(bc_g), mid, ALU.subtract))
            t = act.then(lambda e: e.activation(flat(ke_g), flat(lf_g), ACT.Exp, scale=1.0 / GLA_TAU), t)
            for h in range(2):
                rows = head_rows(h)
                t = dve.then(lambda e, h=h, rows=rows: e.tensor_tensor(
                    qe_g[rows, h::2, :], q_g[rows, :, :], ke_g[rows, :, :], ALU.mult), t, zeroed)
            t = act.then(lambda e: e.activation(flat(ke_g), flat(lf_g), ACT.Exp, scale=-1.0 / GLA_TAU), t)
            t = dve.then(lambda e: e.tensor_tensor(flat(ke_g), flat(ke_g), flat(k_g), ALU.mult), t)
            k_of, q_of = (lambda h: ke_g[:, h // 2, :]), (lambda h: qe_g[:, h, :])

            scored = score_products(k_of, q_of, t)
            take_scores(scores, LOCAL, scored)
            done = feature_block((4, 5))
            for i in range(2):
                src = banks[4 + i][:, :].rearrange("p (m t) -> p m t", t=SEQ)
                bank_read[4 + i] = act.then(lambda e, i=i, src=src: e.activation(
                    th_rg[:, 2 * i:2 * i + 2, :], src, ACT.Gelu_apprx_tanh), done, h_ready)
            t = dve.then(lambda e: e.tensor_tensor(flat(u_rg), flat(u_rg), flat(th_rg), ALU.mult), act.now())

            for block in (P, SEQ):
                d, half, decays = level(bc_g[:, :, :], lf_g[:, :, :], 1.0 / GLA_TAU, block, 2, True)
                for h in range(2):
                    rows = head_rows(h)
                    n = SEQ // block
                    qv = qe_g[rows, h::2, :].rearrange("p h (n b) -> p h n b", b=block)[:, :, :, half:]
                    src = q_g[rows, :, :].rearrange("p h (n b) -> p h n b", b=block)[:, :, :, half:]
                    dv = lf_g[rows, :, :].rearrange("p h (n b) -> p h n b", b=block)[:, :, :, half:]
                    dve.then(lambda e, qv=qv, src=src, dv=dv: e.tensor_tensor(qv, src, dv, ALU.mult), decays, pe.now())
                view = lambda a: flat(a).rearrange("p (n b) -> p n b", b=block)
                t = dve.then(lambda e: e.tensor_tensor(view(ke_g)[:, :, 0:half], view(k_g)[:, :, 0:half], d[:, :, 0:half], ALU.mult))
                if block == P:
                    scored = score_products(k_of, q_of, t)
                    take_scores(scores, LEVELS.index(P), scored)
                    v = flat(bc_g).rearrange("p (n c t) -> p n c t", c=2, t=CHUNK)
                    last = v[:, :, 0, CHUNK - 1:CHUNK].broadcast_to([P, 2 * TILES, CHUNK])
                    dve.then(lambda e: e.tensor_tensor(v[:, :, 1, :], v[:, :, 1, :], last, ALU.add))
                else:
                    crossed = cross_products(scores_x, k_of, q_of, t)
            scored = [crossed, dve.now()]
            done = token_block((6, 7), xt_hi, xt_lo, 2)
            for tile in range(TILES):
                bank_read[6 + tile] = act.free(lambda e, tile=tile: e.activation(
                    gate_g[:, tile, :], banks[6 + tile][:, :], ACT.Silu), done)
            t = act.then(lambda e: e.activation(xt_hi[:, 0:BT, :], u_rg[:, :, :], ACT.Copy), done, dve.now())
            dve.then(lambda e: e.tensor_tensor(xt_lo[:, 0:BT, :], u_rg[:, :, :], xt_hi[:, 0:BT, :].bitcast(F32), ALU.subtract), t)
            done = attend(scores, scores_x, lambda tile: values[:, tile, :], [*scored, values_in])
            o = flat(r_rg).rearrange("p (t n) -> p t n", t=TILES)
            head_norm(done, lambda h: g_norm[:, :], gate_g, o, params, flat(i_rg))
            for tile in range(TILES):
                t = transpose_into(lambda k, tile=tile, o=o: o[:, tile, k * P:(k + 1) * P],
                                   [(k, BT + k) for k in range(BT)], tile, xt_hi, xt_lo, (2 + tile,), dve.now())
            token_block((4, 6), xt_hi, xt_lo, 2, 0, t)
            done = token_block((5, 7), xt_hi, xt_lo, 2)
            add_gated(0, done)

            rms_rstd()
            modulation(l, 1)
            x_ready = modulated(norm_f)
            if l % 2 == 0:
                done = feed_forward(FF_TURNS, lambda j, tile: None, x_ready)
            else:
                for tile in range(TILES):
                    s = []
                    for k in range(KT):
                        cut = slice(tile * P, (tile + 1) * P)
                        s += product(banks[tile][:, 0:EXPERTS], xt_hi[:, k, cut], xt_lo[:, k, cut],
                                     router_hi[:, k, :], router_lo[:, k, :], k == 0, k == KT - 1, None)
                    done = issue_all(s, x_ready, router_ready, bank_read[tile])
                    logits, top = tiny[:, 0:8], tiny[:, 8:16]
                    where, where_f = tiny[:, 16:24].bitcast(U32), tiny[:, 24:32]
                    e2, p1, p2, g2 = tiny[:, 32:33], tiny[:, 33:34], tiny[:, 34:35], tiny[:, 40:48]
                    bank_read[tile] = dve.then(lambda e, tile=tile: e.tensor_copy(logits, banks[tile][:, 0:EXPERTS]), done)
                    dve.then(lambda e: e.max(top, logits))
                    dve.then(lambda e: e.max_index(where, top, logits))
                    dve.then(lambda e: e.tensor_copy(where_f, where))
                    t = dve.then(lambda e: e.tensor_tensor(e2, top[:, 1:2], top[:, 0:1], ALU.subtract))
                    t = act.then(lambda e: e.activation(e2, e2, ACT.Exp), t)
                    dve.then(lambda e: e.tensor_scalar(p1, e2, 1.0, None, ALU.add), t)
                    dve.then(lambda e: e.reciprocal(p1, p1))
                    dve.then(lambda e: e.tensor_tensor(p2, p1, e2, ALU.mult))
                    iota = col("iota", 0, EXPERTS)
                    dve.then(lambda e, tile=tile: e.tensor_scalar(gates[:, tile, :], iota, where_f[:, 0:1], p1, ALU.is_equal, ALU.mult))
                    dve.then(lambda e: e.tensor_scalar(g2, iota, where_f[:, 1:2], p2, ALU.is_equal, ALU.mult))
                    dve.then(lambda e, tile=tile: e.tensor_tensor(gates[:, tile, :], gates[:, tile, :], g2, ALU.add))
                dve.wait(dve.now())
                done = feed_forward(EXPERTS * FF_TURNS,
                                    lambda j, tile: gates[:, tile, j // FF_TURNS:j // FF_TURNS + 1], x_ready)
            add_gated(1, done)

        params = load(norm_g[:, :], w["final_g"].partition_broadcast(P), dve.now())
        rms_rstd()
        for tile in range(TILES):
            t = dve.then(lambda e, tile=tile: e.scalar_tensor_tensor(
                y[:, tile, :], x[:, tile, :], rstd[:, tile:tile + 1], norm_g[:, :], ALU.mult, ALU.mult), params)
            sp.wait(t)
            sp.quiet(lambda e, tile=tile: e.dma_start(out[tile * P:(tile + 1) * P, :], y[:, tile, :]).then_inc(out_written, 16))
        sp.quiet(lambda e: e.wait_ge(out_written, 16 * TILES))
        assert len(used) == len(stream), (len(used), len(stream))


def pack(a, order=None):
    lead, (k, n) = a.shape[:-2], a.shape[-2:]
    a = a.reshape(*lead, k // (4 * P), 4, P, n // N, N)
    m = len(lead)
    a = a.transpose(*range(m), m + 3, m, m + 2, m + 1, m + 4)
    if order is not None:
        a = a[..., order, :, :, :, :]
    return np.ascontiguousarray(a).reshape(*lead, -1, P, UNIT)


def pack_up(a, b):
    lead = a.shape[:-2]
    turns = [z.reshape(*lead, D, FF_TURNS, FF_CHUNK) for z in (a, b)]
    both = np.stack(turns, axis=-2)
    return pack(both.reshape(*lead, D, FF_TURNS * N))


def pack_down(a):
    lead = a.shape[:-2]
    m = len(lead)
    a = a.reshape(*lead, FF_TURNS, 2, P, 2, N).transpose(*range(m), m, m + 2, m + 1, m + 3, m + 4)
    return np.ascontiguousarray(a).reshape(*lead, FF_TURNS, P, UNIT)


def lay_out(i):
    f32 = np.float32
    w13 = lambda a: pack_up(a[..., :D_FF], a[..., D_FF:])
    out = {
        "x": i["x"].reshape(TILES, P, D),
        "ident": np.eye(P, dtype=f32),
        "causal": np.triu(np.ones((P, P), f32)),
        "masks": level_masks(),
        "ffn1_up": w13(i["ffn1_w13"]), "ffn1_down": pack_down(i["ffn1_w2"]),
        "ffn2_up": w13(i["ffn2_w13"]), "ffn2_down": pack_down(i["ffn2_w2"]),
        "mix_in": pack(i["w_in"], [1, 0, 2, 5, 4, 3, 6, 7, 8, 9]),
        "branch_a": pack(i["w_branch_a"]), "branch_b": pack(i["w_branch_b"]), "mix_out": pack(i["w_out"]),
        "ada": pack(i["ada_w_2"]),
        "mix_in_2": pack(i["w_in_2"][:, :, :5 * N], [0, 2, 3, 1, 4]),
        "mix_out_2": pack(i["w_out_2"]),
        "dense_up": pack_up(i["ffn_w1_2"], i["ffn_w3_2"]), "dense_down": pack_down(i["ffn_w2_2"]),
    }
    up = pack_up(i["moe_w1_2"], i["moe_w3_2"])
    down = pack_down(i["moe_w2_2"])
    out["moe_up"] = up.reshape(up.shape[0], -1, P, UNIT)
    out["moe_down"] = down.reshape(down.shape[0], -1, P, UNIT)
    tail = np.zeros((DEPTH, P, KT, P), f32)
    tail[..., :GLA_RANK] = i["w_in_2"][:, :, 5 * N:].reshape(DEPTH, KT, P, GLA_RANK).transpose(0, 2, 1, 3)
    out["mix_in_2_tail"] = tail.reshape(DEPTH, P, KT * P)
    for name in ("ln_g", "ln_b", "hg_norm_g", "sg_ln_g", "sg_ln_b"):
        out[name] = i[name]
    for name in ("norm_mix_g", "norm_ffn_g", "ada_b", "final_g", "gla_norm_g", "gla_wg2"):
        out[name] = i[name + "_2"]
    out["sg_ws_t"] = np.ascontiguousarray(i["sg_ws"].transpose(0, 3, 1, 2))
    rg = np.zeros((DEPTH, P, 2, BT, P), f32)
    for g, name in enumerate(("rg_wa_2", "rg_wx_2")):
        blocks = i[name].reshape(DEPTH, BT, 2, P // 2, P // 2)
        for b in range(2):
            cut = slice(b * P // 2, (b + 1) * P // 2)
            rg[:, cut, g, :, cut] = blocks[:, :, b].transpose(0, 2, 1, 3)
    out["rg_w"] = rg.reshape(DEPTH, P, 2 * BT, P)

    def columns(a):
        return a.reshape(-1, P).T

    table = {
        "lb": columns(i["hg_lb"]), "conv_w": columns(i["rg_conv_w_2"]), "conv_b": columns(i["rg_conv_b_2"]),
        "rg_ba": columns(i["rg_ba_2"]), "rg_bx": columns(i["rg_bx_2"]), "lam": columns(i["rg_lambda_2"]),
        "gla_bg": columns(i["gla_bg_2"]), "sg_bs": columns(i["sg_bs"]), "c": columns(i["c_2"]),
        "router": i["router_w_2"].reshape(KT, P, EXPERTS).transpose(1, 0, 2).reshape(P, -1),
        "iota": np.tile(np.arange(EXPERTS, dtype=f32), (P, 1)),
    }
    out["cols"] = np.ascontiguousarray(np.concatenate([table[n] for n in COLS], axis=1))
    return {n: np.ascontiguousarray(a) for n, a in out.items()}


def kernel(**inputs):
    import concourse.bacc as bacc
    from concourse.bass_utils import run_bass_kernel_spmd

    arrays = lay_out({n: np.asarray(a) for n, a in inputs.items()})
    nc = bacc.Bacc("TRN2", target_bir_lowering=False, num_devices=1)
    w = {n: nc.dram_tensor(f"in_{n}", a.shape, mybir.dt.from_np(a.dtype), kind="ExternalInput").ap()
         for n, a in arrays.items()}
    out = nc.dram_tensor("result", (SEQ, D), F32, kind="ExternalOutput").ap()
    build(nc, w, out)
    got = run_bass_kernel_spmd(nc, [{f"in_{n}": a for n, a in arrays.items()}], core_ids=[0])
    return got.results[0]["result"].reshape(1, SEQ, D)
```

```python
from contextlib import ExitStack

import numpy as np

import concourse.bass as bass
from concourse import mybir

F32 = mybir.dt.float32
F32R = mybir.dt.float32r
U8 = mybir.dt.uint8
U32 = mybir.dt.uint32
I32 = mybir.dt.int32
ACT = mybir.ActivationFunctionType
ALU = mybir.AluOpType

P = 128
SEQ = 256
TILES = SEQ // P
D = 1024
KT = D // P
DEPTH = 2
D_FF = 2816
HEADS = 4
HALF = D // 2
BT = HALF // P
GLA_KD = 256
GLA_DK = GLA_KD // HEADS
GLA_RANK = 16
CONV_W = 4
EXPERTS = 8
CHUNK = 64
FF_CHUNK = 256
FF_TURNS = D_FF // FF_CHUNK
N = 512
UNIT = 4 * N

ALPHA = (2 * DEPTH) ** 0.25
LN_EPS = 1e-5
RMS_EPS = 1e-6
RG_C = 8.0
GLA_TAU = 16.0
LN_SHIFT = 64
LN_LOW = 2.0 ** -60

RAW_SLOTS = 4
SPLIT_SLOTS = 4

COLS = {}
_at = 0
for _name, _n in (("lb", DEPTH * HEADS), ("conv_w", DEPTH * CONV_W * BT), ("conv_b", DEPTH * BT),
                  ("rg_ba", DEPTH * BT), ("rg_bx", DEPTH * BT), ("lam", DEPTH * BT),
                  ("gla_bg", DEPTH * 2), ("sg_bs", DEPTH * HEADS), ("c", KT),
                  ("router", KT * EXPERTS), ("iota", EXPERTS)):
    COLS[_name] = (_at, _n)
    _at += _n
N_COLS = _at

LEVELS = [1, 2, 4, 8, 16, 32, 64, 128]
LOCAL = len(LEVELS)


def level_masks():
    s, t = np.arange(P)[:, None], np.arange(P)[None, :]
    out = np.zeros((P, len(LEVELS) + 1, P), np.float32)
    for i, b in enumerate(LEVELS):
        if b == 1:
            out[:, i] = s == t
        else:
            out[:, i] = (s // b == t // b) & (s % b < b // 2) & (t % b >= b // 2)
    out[:, LOCAL] = (s <= t) & (s // CHUNK == t // CHUNK)
    return out.reshape(P, -1)


class Queue:

    def __init__(self, engine, semaphore):
        self.engine = engine
        self.done = semaphore
        self.count = 0
        self.seen = {}
        self.tape = None
        self.second = True

    def wait(self, *tokens):
        for t in tokens:
            if t is None:
                continue
            if isinstance(t, list):
                self.wait(*t)
                continue
            sem, value = t
            if self.seen.get(id(sem), 0) < value:
                self.seen[id(sem)] = value
                self._issue(lambda e, sem=sem, value=value: e.wait_ge(sem, value))

    def now(self):
        return (self.done, self.count) if self.count else None

    def free(self, issue, *tokens):
        self.wait(*tokens)
        self.count += 1
        self._issue(lambda e: issue(e).then_inc(self.done, 1))
        return self.done, self.count

    def then(self, issue, *tokens):
        return self.free(issue, self.now(), *tokens)

    def quiet(self, issue, *tokens):
        self.wait(*tokens)
        self._issue(issue)

    def second_only(self, issue, *tokens):
        self.wait(*tokens)
        self._issue(issue, True)

    def _issue(self, issue, second_only=False):
        if self.tape is None:
            issue(self.engine)
        else:
            self.tape.append((issue, second_only))

    def record(self):
        self.tape = []

    def play_if(self, has_second):
        tape, self.tape = self.tape, None
        for second in (True, False):
            self.second = second
            with self.engine.If(has_second) if second else self.engine.Else():
                for issue, second_only in tape:
                    if second or not second_only:
                        issue(self.engine)
        self.second = True


def build(nc, w, out):
    with ExitStack() as ctx:
        def sb(name, shape, dtype=F32, where=ctx):
            return where.enter_context(nc.sbuf_tensor(name, shape, dtype))

        def sem(name):
            return ctx.enter_context(nc.semaphore(name))

        pe, act = Queue(nc.tensor, sem("pe_done")), Queue(nc.scalar, sem("act_done"))
        dve, pool = Queue(nc.vector, sem("dve_done")), Queue(nc.gpsimd, sem("pool_done"))
        sp = Queue(nc.sync, None)
        small_loaded = sem("small_loaded")
        out_written = sem("out_written")
        raw_loaded = [sem(f"raw_loaded_{i}") for i in range(RAW_SLOTS)]

        banks = [ctx.enter_context(nc.psum_tensor(f"bank{i}", [P, N], F32)) for i in range(8)]
        bank_read = [None] * 8

        raw = sb("raw", [P, RAW_SLOTS, UNIT])
        w_hi = sb("w_hi", [P, SPLIT_SLOTS, UNIT], F32R)
        w_lo = sb("w_lo", [P, SPLIT_SLOTS, UNIT], F32R)
        x = sb("x", [P, TILES, D])
        y = sb("y", [P, TILES, D])
        xt_hi = sb("xt_hi", [P, KT, SEQ], F32R)
        xt_lo = sb("xt_lo", [P, KT, SEQ], F32R)
        ht_hi = sb("ht_hi", [P, 2, SEQ], F32R)
        ht_lo = sb("ht_lo", [P, 2, SEQ], F32R)
        hidden2 = sb("hidden2", [P, 2 * TILES * FF_CHUNK])
        silu_a = hidden2[:, 0:TILES * FF_CHUNK].rearrange("p (t n) -> p t n", t=TILES)
        hidden = hidden2[:, TILES * FF_CHUNK:].rearrange("p (t n) -> p t n", t=TILES)
        ident = sb("ident", [P, P])
        causal = sb("causal", [P, P])
        masks = sb("masks", [P, LOCAL + 1, P], U8)
        cols = sb("cols", [P, N_COLS])
        stats = sb("stats", [P, TILES, 2, 6])
        mean_var = sb("mean_var", [P, TILES, 2])
        rstd = sb("rstd", [P, TILES])
        sums = sb("sums", [P, 8])
        lb = sb("lb", [P, 8, HEADS])
        gates = sb("gates", [P, TILES, EXPERTS])
        tiny = sb("tiny", [P, 64])

        def col(name, i, n=1):
            at = COLS[name][0] + i
            return cols[:, at:at + n]

        small_count = [0]

        def load(dst, src, *tokens):
            pool.wait(*tokens)
            if small_count[0]:
                pool.wait((small_loaded, small_count[0]))
            small_count[0] += 16
            pool.quiet(lambda e: e.dma_start(dst, src).then_inc(small_loaded, 16))
            return small_loaded, small_count[0]

        stream = []

        def product_units(array, first, n):
            stream.extend((array[first + i], UNIT) for i in range(n))

        def feed_forward_units(up, down, first_turn, turns, before, last):
            for j in range(turns):
                product_units(up, 2 * (first_turn + j), 2)
                if before or j:
                    product_units(down, first_turn + j - 1, 1)
            if last:
                product_units(down, first_turn + turns - 1, 1)

        for l in range(DEPTH):
            feed_forward_units(w["ffn1_up"][l], w["ffn1_down"][l], 0, FF_TURNS, False, True)
            product_units(w["mix_in"][l], 0, 20)
            product_units(w["branch_a"][l], 0, 2)
            product_units(w["branch_b"][l], 0, 2)
            product_units(w["mix_out"][l], 0, 4)
            feed_forward_units(w["ffn2_up"][l], w["ffn2_down"][l], 0, FF_TURNS, False, True)
        for l in range(DEPTH):
            product_units(w["ada"][l], 0, 12)
            product_units(w["mix_in_2"][l], 0, 4)
            stream.append((w["mix_in_2_tail"][l], KT * P))
            product_units(w["mix_in_2"][l], 4, 6)
            product_units(w["mix_out_2"][l], 0, 4)
            product_units(w["ada"][l], 12, 12)
            if l % 2 == 0:
                feed_forward_units(w["dense_up"][l // 2], w["dense_down"][l // 2], 0, FF_TURNS, False, True)
            else:
                for x_of in range(EXPERTS):
                    feed_forward_units(w["moe_up"][l // 2], w["moe_down"][l // 2], x_of * FF_TURNS, FF_TURNS, False, True)

        used = []
        split = []
        loads = [0]

        def load_unit():
            n = loads[0]
            if n >= len(stream):
                return
            loads[0] += 1
            src, size = stream[n]
            slot = n % RAW_SLOTS
            if n >= RAW_SLOTS:
                sp.wait(split[n - RAW_SLOTS])
            sp.quiet(lambda e: e.dma_start(raw[:, slot, 0:size], src).then_inc(raw_loaded[slot], 16))

        def split_unit():
            n = len(split)
            if n >= len(stream):
                return
            size = stream[n][1]
            src = raw[:, n % RAW_SLOTS, 0:size]
            hi, lo = w_hi[:, n % SPLIT_SLOTS, 0:size], w_lo[:, n % SPLIT_SLOTS, 0:size]
            arrived = (raw_loaded[n % RAW_SLOTS], 16 * (n // RAW_SLOTS + 1))
            free = used[n - SPLIT_SLOTS] if n >= SPLIT_SLOTS else None
            rounded = act.free(lambda e: e.activation(hi, src, ACT.Copy), arrived, free)
            split.append(dve.free(lambda e: e.tensor_tensor(lo, src, hi.bitcast(F32), ALU.subtract),
                                  arrived, free, rounded))
            load_unit()

        for _ in range(RAW_SLOTS):
            load_unit()

        def unit():
            n = len(used)
            while len(split) < min(n + SPLIT_SLOTS, len(stream)):
                split_unit()
            slot = n % SPLIT_SLOTS
            hi = w_hi[:, slot, :].rearrange("p (k n) -> p k n", n=N)
            lo = w_lo[:, slot, :].rearrange("p (k n) -> p k n", n=N)
            return hi, lo, split[n]

        def product(dst, hi_l, lo_l, hi_r, lo_r, start, stop, wait, skip=False):
            for i, (a, b) in enumerate(((hi_l, hi_r), (hi_l, lo_r), (lo_l, hi_r))):
                first, last = start and i == 0, stop and i == 2
                yield lambda e, a=a, b=b, first=first, last=last: e.matmul(
                    dst, a, b, start=first, stop=last, skip_group_check=skip)

        def issue_all(steps, *tokens):
            steps = list(steps)
            pe.wait(*tokens)
            for s in steps[:-1]:
                pe.quiet(s)
            return pe.free(steps[-1])

        def token_block(pair, lhs_hi, lhs_lo, units, kt0=0, *tokens):
            for u in range(units):
                hi, lo, ready = unit()
                for tile in range(TILES):
                    s = []
                    for k in range(4):
                        kt = kt0 + 4 * u + k
                        cut = slice(tile * P, (tile + 1) * P)
                        s += product(banks[pair[tile]][:, :], lhs_hi[:, kt, cut], lhs_lo[:, kt, cut],
                                     hi[:, k, :], lo[:, k, :], u == 0 and k == 0,
                                     u == units - 1 and k == 3, None)
                    done = issue_all(s, ready, bank_read[pair[tile]], *tokens)
                used.append(done)
            return done

        def feature_block(pair, *tokens):
            for u in range(2):
                hi, lo, ready = unit()
                for m in range(4):
                    dst = banks[pair[m // 2]][:, (m % 2) * SEQ:(m % 2 + 1) * SEQ]
                    s = []
                    for k in range(4):
                        kt = 4 * u + k
                        cut = slice(m * P, (m + 1) * P)
                        s += product(dst, hi[:, k, cut], lo[:, k, cut], xt_hi[:, kt, :], xt_lo[:, kt, :],
                                     u == 0 and k == 0 and m % 2 == 0, u == 1 and k == 3, None, skip=True)
                    done = issue_all(s, ready, bank_read[pair[m // 2]], *tokens)
                used.append(done)
            return done

        def evacuate(engine_op, bank, *tokens):
            bank_read[bank] = engine_op
            return engine_op

        def transpose_into(src_of, kts, tile, dst_hi, dst_lo, pair, *tokens):
            done = None
            for g in range(0, len(kts), 4):
                group = kts[g:g + 4]
                b = pair[g // 4]
                bank = banks[b]
                pe.wait(bank_read[b], *tokens)
                for i, (src_i, _) in enumerate(group):
                    step = lambda e, i=i, src_i=src_i: e.transpose(bank[:, i * P:(i + 1) * P], src_of(src_i), ident[:, :])
                    if i == len(group) - 1:
                        turned = pe.free(step)
                    else:
                        pe.quiet(step)
                k0 = group[0][1]
                cut = slice(tile * P, (tile + 1) * P)
                hi = dst_hi[:, k0:k0 + len(group), cut]
                lo = dst_lo[:, k0:k0 + len(group), cut]
                src = bank[:, 0:len(group) * P].rearrange("p (k t) -> p k t", t=P)
                rounded = act.free(lambda e: e.activation(hi, src, ACT.Copy), turned)
                done = dve.free(lambda e: e.tensor_tensor(lo, src, hi.bitcast(F32), ALU.subtract), rounded)
                bank_read[b] = done
            return done

        def rstd_of(dst, src, scale, eps, *tokens):
            t = dve.then(lambda e: e.tensor_scalar(dst, src, scale, eps, ALU.mult, ALU.add), *tokens)
            t = act.then(lambda e: e.activation(dst, dst, ACT.Sqrt), t)
            return dve.then(lambda e: e.reciprocal(dst, dst), t)

        def layer_norm(src, tile, width, gain, shift, params, *tokens):
            n = width // N
            for i in range(n):
                t = dve.then(lambda e, i=i: e.bn_stats(stats[:, tile, i, :], src[:, i * N:(i + 1) * N]), *tokens)
            t = dve.then(lambda e: e.bn_aggr(mean_var[:, tile, :], stats[:, tile, 0:n, :].rearrange("p a b -> p (a b)")), t)
            t = rstd_of(rstd[:, tile:tile + 1], mean_var[:, tile, 1:2], 1.0, LN_EPS, t)
            t = dve.then(lambda e: e.scalar_tensor_tensor(src, src, mean_var[:, tile, 0:1], gain, ALU.subtract, ALU.mult), t, params)
            return dve.then(lambda e: e.scalar_tensor_tensor(src, src, rstd[:, tile:tile + 1], shift, ALU.mult, ALU.add), t)

        def feed_forward(turns, x_ready):
            def up(j):
                token_block((0, 1), xt_hi, xt_lo, 2, 0, x_ready)
                last = pe.now()
                ready = None
                for tile in range(TILES):
                    bank = banks[tile]
                    a, b = bank[:, 0:FF_CHUNK], bank[:, FF_CHUNK:N]
                    s = act.free(lambda e, tile=tile, a=a: e.activation(silu_a[:, tile, :], a, ACT.Silu), last)
                    ready = dve.free(lambda e, tile=tile, b=b: e.tensor_tensor(
                        hidden[:, tile, :], b, silu_a[:, tile, :], ALU.mult), s)
                    bank_read[tile] = ready
                return ready

            def turn(ready):
                b = 2
                pe.wait(bank_read[b], ready)
                for k in range(2):
                    for tile in range(TILES):
                        step = lambda e, k=k, tile=tile: e.transpose(
                            banks[b][:, k * SEQ + tile * P:k * SEQ + (tile + 1) * P],
                            hidden[:, tile, k * P:(k + 1) * P], ident[:, :])
                        if k == 1 and tile == 1:
                            turned = pe.free(step)
                        else:
                            pe.quiet(step)
                src = banks[b][:, :].rearrange("p (k t) -> p k t", t=SEQ)
                rounded = act.free(lambda e: e.activation(ht_hi[:, :, :], src, ACT.Copy), turned)
                bank_read[b] = dve.free(lambda e: e.tensor_tensor(
                    ht_lo[:, :, :], src, ht_hi[:, :, :].bitcast(F32), ALU.subtract), rounded)
                return bank_read[b]

            def down(j, ready):
                hi, lo, there = unit()
                s = []
                pe.wait(there, ready)
                for tile in range(TILES):
                    for half in range(2):
                        bank = 4 + 2 * tile + half
                        s = []
                        for k in range(2):
                            cut = slice(tile * P, (tile + 1) * P)
                            s += product(banks[bank][:, :], ht_hi[:, k, cut], ht_lo[:, k, cut],
                                         hi[:, 2 * k + half, :], lo[:, 2 * k + half, :],
                                         j == 0 and k == 0, j == turns - 1 and k == 1, None)
                        done = issue_all(s, bank_read[bank] if j == 0 else None)
                used.append(done)
                return done

            turned = None
            for j in range(turns):
                ready = up(j)
                if j:
                    down(j - 1, turned)
                turned = turn(ready)
            return down(turns - 1, turned)

        def add_scaled_and_normalise(banks_of, scale, params, done):
            for tile in range(TILES):
                for half in range(2):
                    b = banks_of(tile, half)
                    t = act.free(lambda e, tile=tile, half=half, b=b: e.activation(
                        y[:, tile, half * N:(half + 1) * N], banks[b][:, :], ACT.Copy, scale=scale), done)
                    bank_read[b] = t
                t = dve.then(lambda e, tile=tile: e.scalar_tensor_tensor(
                    x[:, tile, :], x[:, tile, :], ALPHA, y[:, tile, :], ALU.mult, ALU.add), t)
                layer_norm(x[:, tile, :], tile, D, ln_p[:, 0, :], ln_p[:, 1, :], params, t)

        def transpose_x(src):
            for tile in range(TILES):
                t = transpose_into(lambda k, tile=tile: src[:, tile, k * P:(k + 1) * P],
                                   [(k, k) for k in range(KT)], tile, xt_hi, xt_lo,
                                   ((0, 1), (2, 3))[tile], dve.now())
            return t

        for tile in range(TILES):
            load(x[:, tile, :], w["x"][tile])
        load(ident[:, :], w["ident"])
        load(causal[:, :], w["causal"])
        y_flat = y[:, :, :].rearrange("p a b -> p (a b)")[:, 0:(LOCAL + 1) * P]
        load(y_flat, w["masks"])
        consts_in = load(cols[:, :], w["cols"])
        pe.wait(consts_in)
        dve.wait(consts_in)
        act.wait(consts_in)
        dve.then(lambda e: e.tensor_copy(masks[:, :, :].rearrange("p a b -> p (a b)"), y_flat))

        L = lambda i: lb[:, i, :]
        raw_lb = lambda l: col("lb", l * HEADS, HEADS)
        dve.then(lambda e: e.tensor_tensor(L(2), raw_lb(0), raw_lb(1), ALU.max))
        dve.then(lambda e: e.tensor_tensor(L(0), raw_lb(0), L(2), ALU.subtract))
        t = dve.then(lambda e: e.tensor_tensor(L(1), raw_lb(1), L(2), ALU.subtract))
        t = act.then(lambda e: e.activation(lb[:, 0:2, :], lb[:, 0:2, :], ACT.Exp), t)
        dve.then(lambda e: e.tensor_tensor(L(2), L(0), L(1), ALU.add), t)
        dve.then(lambda e: e.reciprocal(L(2), L(2)))
        dve.then(lambda e: e.tensor_tensor(L(0), L(0), L(2), ALU.mult))
        dve.then(lambda e: e.tensor_tensor(L(1), L(1), L(2), ALU.mult))
        dve.then(lambda e: e.tensor_tensor(L(3), L(0), L(1), ALU.add))
        dve.then(lambda e: e.tensor_tensor(L(4), L(0), L(0), ALU.subtract))
        dve.then(lambda e: e.tensor_tensor(L(5), L(3), L(0), ALU.subtract))
        dve.then(lambda e: e.tensor_scalar(lb[:, 6:8, :], lb[:, 4:6, :], -1.0, 1.0, ALU.mult, ALU.add))

        def level(bc, diff, scale, block, groups, plain_right):
            half = block // 2
            n = groups * SEQ // block
            v = bc.rearrange("p h t -> p (h t)").rearrange("p (n b) -> p n b", b=block)
            d = diff.rearrange("p h t -> p (h t)").rearrange("p (n b) -> p n b", b=block)
            left, right, mid = v[:, :, 0:half], v[:, :, half:], v[:, :, half - 1:half].broadcast_to([P, n, half])
            t = dve.then(lambda e: e.tensor_tensor(d[:, :, 0:half], mid, left, ALU.subtract))
            if plain_right:
                t = dve.then(lambda e: e.tensor_copy(d[:, :, half:], right))
            else:
                t = dve.then(lambda e: e.tensor_tensor(d[:, :, half:], right, mid, ALU.subtract))
            t = act.then(lambda e: e.activation(diff, diff, ACT.Exp, scale=scale), t)
            return d, half, t

        def attend(scores, scores_x, v_of, values_ready):
            for tile in range(TILES):
                s = []
                for h in range(HEADS):
                    cut = slice(h * P, (h + 1) * P)
                    s.append(lambda e, tile=tile, h=h, cut=cut: e.matmul(
                        banks[2 + tile][:, cut], scores[:, tile * HEADS + h, :], v_of(tile)[:, cut],
                        start=True, stop=tile == 0))
                    if tile:
                        s.append(lambda e, h=h, cut=cut: e.matmul(
                            banks[3][:, cut], scores_x[:, h, :], v_of(0)[:, cut], start=False, stop=True))
                done = issue_all(s, bank_read[2 + tile], *values_ready)
            return done

        def head_norm(done, gain_of, gate, dst, params, junk):
            for tile in range(TILES):
                for h in range(HEADS):
                    cut = slice(h * P, (h + 1) * P)
                    t = act.free(lambda e, tile=tile, h=h, cut=cut: e.activation(
                        junk[:, cut], banks[2 + tile][:, cut], ACT.Square,
                        accum_out=sums[:, tile * HEADS + h:tile * HEADS + h + 1]), done, dve.now(), act.now())
            t = rstd_of(sums[:, :], sums[:, :], 1.0 / P, RMS_EPS, t)
            for tile in range(TILES):
                for h in range(HEADS):
                    i = tile * HEADS + h
                    cut = slice(h * P, (h + 1) * P)
                    t = dve.then(lambda e, tile=tile, cut=cut, i=i, h=h: e.scalar_tensor_tensor(
                        dst[:, tile, cut], banks[2 + tile][:, cut], sums[:, i:i + 1], gain_of(h),
                        ALU.mult, ALU.mult), params)
                bank_read[2 + tile] = t
                t = dve.then(lambda e, tile=tile: e.tensor_tensor(
                    dst[:, tile, :], dst[:, tile, :], gate[:, tile, :], ALU.mult), act.now())
            return t

        def take_scores(scores, index, bank_tokens):
            for tile in range(TILES):
                mask = masks[:, index:index + 1, :].broadcast_to([P, HEADS, P])
                bank_read[2 + tile] = dve.then(lambda e, tile=tile, mask=mask: e.copy_predicated(
                    scores[:, tile * HEADS:(tile + 1) * HEADS, :], mask,
                    banks[2 + tile][:, :].rearrange("p (h t) -> p h t", t=P)), bank_tokens)

        def score_products(k_of, q_of, ready):
            s = []
            pe.wait(bank_read[2], bank_read[3])
            for tile in range(TILES):
                for h in range(HEADS):
                    cut = slice(tile * P, (tile + 1) * P)
                    s.append(lambda e, tile=tile, h=h, cut=cut: e.matmul(
                        banks[2 + tile][:, h * P:(h + 1) * P], k_of(h)[:, cut], q_of(h)[:, cut],
                        start=True, stop=True))
            return issue_all(s, ready)

        def cross_products(scores_x, k_of, q_of, ready):
            s = [lambda e, h=h: e.matmul(banks[2][:, h * P:(h + 1) * P], k_of(h)[:, 0:P], q_of(h)[:, P:SEQ],
                                         start=True, stop=True) for h in range(HEADS)]
            done = issue_all(s, ready, bank_read[2])
            bank_read[2] = act.then(lambda e: e.activation(
                scores_x[:, :, :], banks[2][:, :].rearrange("p (h t) -> p h t", t=P), ACT.Copy), done)
            return bank_read[2]

        def restart_mask(tile, n, *tokens):
            t = pool.then(lambda e: e.memset(tile[:, 0:n], 1.0), *tokens)
            return pool.then(lambda e: e.memset(tile[:, 0:n].rearrange("p (c t) -> p c t", t=CHUNK)[:, :, 0:1], 0.0), t)

        def all_done():
            return [t for t in (pe.now(), act.now(), dve.now(), pool.now()) if t]

        first = ExitStack()
        with first:
            def sb1(name, shape, dtype=F32):
                return sb(name, shape, dtype, first)

            ln_p = sb1("ln_p", [P, 2, D])
            q_t = sb1("q_t", [P, HEADS, SEQ])
            k_t = sb1("k_t", [P, HEADS, SEQ])
            logf = sb1("logf", [P, HEADS, SEQ])
            bc = sb1("bc", [P, HEADS, SEQ])
            qe = sb1("qe", [P, HEADS, SEQ])
            ke = sb1("ke", [P, HEADS, SEQ])
            scores = sb1("scores", [P, TILES * HEADS, P])
            scores_x = sb1("scores_x", [P, HEADS, P])
            values = sb1("values", [P, TILES, HALF])
            gate_g = sb1("gate_g", [P, TILES, HALF])
            u_sg = sb1("u_sg", [P, TILES, HALF])
            v_sg = sb1("v_sg", [P, TILES, HALF])
            sig_b = sb1("sig_b", [P, TILES, D])
            ws = sb1("ws", [P, HEADS, P])

            flat = lambda a: a[:, :, :].rearrange("p a b -> p (a b)")
            ln_flat = flat(ln_p)
            hg_gain, sg_gain, sg_shift = (ln_flat[:, i * HALF:(i + 1) * HALF] for i in range(3))

            def load_ln(l, i, *tokens):
                load(ln_p[:, 0, :], w["ln_g"][l, i, :].partition_broadcast(P), *tokens)
                return load(ln_p[:, 1, :], w["ln_b"][l, i, :].partition_broadcast(P))

            def hgrn(l, fed):
                f_pair, f_done = fed["f"]
                for i in range(2):
                    src = banks[f_pair[i]][:, :].rearrange("p (m t) -> p m t", t=SEQ)
                    act.then(lambda e, i=i, src=src: e.activation(logf[:, 2 * i:2 * i + 2, :], src, ACT.Sigmoid), f_done)
                    t = act.then(lambda e, i=i, src=src: e.activation(k_t[:, 2 * i:2 * i + 2, :], src, ACT.Sigmoid, scale=-1.0))
                    bank_read[f_pair[i]] = t
                for h in range(HEADS):
                    less, bound = lb[:, 6 + l, h:h + 1], lb[:, 4 + l, h:h + 1]
                    dve.then(lambda e, h=h, less=less, bound=bound: e.tensor_scalar(
                        logf[:, h, :], logf[:, h, :], less, bound, ALU.mult, ALU.add), t)
                    f_set = dve.then(lambda e, h=h, less=less: e.tensor_scalar(
                        k_t[:, h, :], k_t[:, h, :], less, None, ALU.mult))
                yield
                t = act.then(lambda e: e.activation(flat(qe), flat(logf), ACT.Ln, scale=2.0 ** LN_SHIFT), f_set)
                dve.then(lambda e: e.tensor_scalar(flat(ke).bitcast(U32), flat(logf), LN_LOW, None, ALU.is_lt))
                low = dve.then(lambda e: e.tensor_scalar(flat(qe), flat(qe), -LN_SHIFT * float(np.log(2.0)), None, ALU.add), t)
                t = act.then(lambda e: e.activation(flat(logf), flat(logf), ACT.Ln), low)
                t = dve.then(lambda e: e.copy_predicated(flat(logf), flat(ke).bitcast(U32), flat(qe)), t)
                restart = restart_mask(flat(qe), HEADS * SEQ, t)
                t = dve.then(lambda e: e.tensor_tensor_scan(flat(bc), flat(qe), flat(logf), 0.0, ALU.mult, ALU.add), restart)
                q_pair, q_done = fed["q"]
                for i in range(2):
                    src = banks[q_pair[i]][:, :].rearrange("p (m t) -> p m t", t=SEQ)
                    bank_read[q_pair[i]] = act.then(lambda e, i=i, src=src: e.activation(
                        q_t[:, 2 * i:2 * i + 2, :], src, ACT.Copy), q_done)
                zeroed = pool.then(lambda e: e.memset(scores[:, :, :], 0.0), pe.now())
                yield
                for index, block in enumerate(LEVELS + [SEQ]):
                    if block == 1:
                        ready = score_products(lambda h: k_t[:, h, :], lambda h: q_t[:, h, :],
                                               [act.now(), dve.now()])
                    else:
                        d, half, decays = level(bc[:, :, :], logf[:, :, :], 1.0, block, HEADS, block >= P)
                        view = lambda a: flat(a).rearrange("p (n b) -> p n b", b=block)
                        dve.then(lambda e: e.tensor_tensor(view(qe)[:, :, half:], view(q_t)[:, :, half:], d[:, :, half:], ALU.mult),
                                 decays, pe.now())
                        t = dve.then(lambda e: e.tensor_tensor(view(ke)[:, :, 0:half], view(k_t)[:, :, 0:half], d[:, :, 0:half], ALU.mult))
                        pair = (lambda h: ke[:, h, :], lambda h: qe[:, h, :], t)
                        if block == SEQ:
                            crossed = cross_products(scores_x, *pair)
                            break
                        ready = score_products(*pair)
                    if block == P:
                        v = flat(bc).rearrange("p (n c t) -> p n c t", c=2, t=CHUNK)
                        last = v[:, :, 0, CHUNK - 1:CHUNK].broadcast_to([P, HEADS * TILES, CHUNK])
                        dve.then(lambda e: e.tensor_tensor(v[:, :, 1, :], v[:, :, 1, :], last, ALU.add))
                    yield
                    take_scores(scores, index, [ready, zeroed])
                fed["scored"] = [crossed, dve.now()]

            for l in range(DEPTH):
                params = load_ln(l, 0, *all_done())
                if l == 0:
                    transpose_x(x)
                done = feed_forward(FF_TURNS, dve.now())
                add_scaled_and_normalise(lambda tile, half: 4 + 2 * tile + half, 0.5, params, done)
                x_ready = transpose_x(x)

                normed = dve.now()
                load(hg_gain, w["hg_norm_g"][l].partition_broadcast(P), normed)
                load(sg_gain, w["sg_ln_g"][l].partition_broadcast(P))
                load(ws[:, :, :], w["sg_ws_t"][l], pe.now())
                params = load(sg_shift, w["sg_ln_b"][l].partition_broadcast(P))
                fed = {}
                fed["f"] = ((4, 5), feature_block((4, 5), x_ready))
                recurrence = hgrn(l, fed)
                next(recurrence)
                fed["q"] = ((6, 7), feature_block((6, 7)))
                next(recurrence)
                done = token_block((0, 1), xt_hi, xt_lo, 2)
                for tile in range(TILES):
                    bank_read[tile] = act.free(lambda e, tile=tile: e.activation(
                        values[:, tile, :], banks[tile][:, :], ACT.Copy), done)
                values_in = act.now()
                next(recurrence)

                done = token_block((4, 5), xt_hi, xt_lo, 2)
                for tile in range(TILES):
                    bank_read[4 + tile] = act.free(lambda e, tile=tile: e.activation(
                        v_sg[:, tile, :], banks[4 + tile][:, :], ACT.Gelu_apprx_tanh), done)
                v_in = act.now()
                next(recurrence)
                done = token_block((6, 7), xt_hi, xt_lo, 2)
                for tile in range(TILES):
                    bank_read[6 + tile] = act.free(lambda e, tile=tile: e.activation(
                        u_sg[:, tile, :], banks[6 + tile][:, :], ACT.Gelu_apprx_tanh), done)
                u_in = act.now()
                for tile in range(TILES):
                    layer_norm(v_sg[:, tile, :], tile, HALF, sg_gain, sg_shift, params, v_in)
                for h in range(HEADS):
                    dve.then(lambda e, h=h: e.tensor_tensor(ws[:, h, :], ws[:, h, :], causal[:, :], ALU.mult))
                v_ready = dve.now()
                next(recurrence)
                done = token_block((0, 1), xt_hi, xt_lo, 2)
                for tile in range(TILES):
                    bank_read[tile] = act.free(lambda e, tile=tile: e.activation(
                        gate_g[:, tile, :], banks[tile][:, :], ACT.Silu), done)
                next(recurrence)
                s = []
                for tile in range(TILES):
                    for h in range(HEADS):
                        cut = slice(h * P, (h + 1) * P)
                        s.append(lambda e, tile=tile, h=h, cut=cut: e.matmul(
                            banks[4 + tile][:, cut], ws[:, h, :], v_sg[:, tile, cut], start=True, stop=True))
                mixed = issue_all(s, v_ready, bank_read[4], bank_read[5])
                for tile in range(TILES):
                    for h in range(HEADS):
                        cut = slice(h * P, (h + 1) * P)
                        bank_read[4 + tile] = dve.then(lambda e, tile=tile, h=h, cut=cut: e.scalar_tensor_tensor(
                            u_sg[:, tile, cut], banks[4 + tile][:, cut], col("sg_bs", l * HEADS + h), u_sg[:, tile, cut],
                            ALU.add, ALU.mult), mixed, u_in)
                for i, pair in enumerate(((6, 7), (0, 1), (4, 5), (6, 7))):
                    done = token_block(pair, xt_hi, xt_lo, 2)
                    dst = (y, sig_b)[i // 2]
                    for tile in range(TILES):
                        bank_read[pair[tile]] = act.free(lambda e, tile=tile, i=i, dst=dst, pair=pair: e.activation(
                            dst[:, tile, (i % 2) * N:(i % 2 + 1) * N], banks[pair[tile]][:, :], ACT.Sigmoid), done)
                    next(recurrence)
                for _ in recurrence:
                    pass
                done = attend(scores, scores_x, lambda tile: values[:, tile, :], [*fed["scored"], values_in])
                o = flat(qe).rearrange("p (t n) -> p t n", t=TILES)
                head_norm(done, lambda h: hg_gain[:, h * P:(h + 1) * P], gate_g, o, params, flat(ke))
                for tile in range(TILES):
                    transpose_into(lambda k, tile=tile: u_sg[:, tile, k * P:(k + 1) * P],
                                   [(k, BT + k) for k in range(BT)], tile, xt_hi, xt_lo, (tile,), dve.now())
                for tile in range(TILES):
                    t = transpose_into(lambda k, tile=tile, o=o: o[:, tile, k * P:(k + 1) * P],
                                       [(k, k) for k in range(BT)], tile, xt_hi, xt_lo, (2 + tile,), dve.now())
                params = load_ln(l, 1, dve.now())
                for branch in range(2):
                    for half in range(2):
                        pair = (4, 5) if half == 0 else (6, 7)
                        done = token_block(pair, xt_hi, xt_lo, 1, branch * BT, t)
                        for tile in range(TILES):
                            cut = slice(half * N, (half + 1) * N)
                            if branch == 0:
                                bank_read[pair[tile]] = dve.then(lambda e, tile=tile, cut=cut, b=pair[tile]: e.tensor_tensor(
                                    y[:, tile, cut], banks[b][:, :], y[:, tile, cut], ALU.mult), done)
                            else:
                                bank_read[pair[tile]] = dve.then(lambda e, tile=tile, cut=cut, b=pair[tile]: e.tensor_tensor(
                                    sig_b[:, tile, cut], banks[b][:, :], sig_b[:, tile, cut], ALU.mult), done)
                                dve.then(lambda e, tile=tile, cut=cut: e.tensor_tensor(
                                    y[:, tile, cut], y[:, tile, cut], sig_b[:, tile, cut], ALU.add))
                t = transpose_x(y)
                token_block((4, 6), xt_hi, xt_lo, 2, 0, t)
                done = token_block((5, 7), xt_hi, xt_lo, 2)
                add_scaled_and_normalise(lambda tile, half: 4 + 2 * tile + half, 1.0, params, done)
                params = load_ln(l, 2, dve.now())
                x_ready = transpose_x(x)

                done = feed_forward(FF_TURNS, x_ready)
                add_scaled_and_normalise(lambda tile, half: 4 + 2 * tile + half, 0.5, params, done)
                if l < DEPTH - 1:
                    transpose_x(x)

        second = ctx.enter_context(ExitStack())

        def sb2(name, shape, dtype=F32):
            return sb(name, shape, dtype, second)

        norm_g = sb2("norm_g", [P, D])
        sh = sb2("sh", [P, D])
        sc = sb2("sc", [P, D])
        gt = [sb2(f"gt_{n}", [P, D]) for n in ("mix", "ffn")]
        c_hi = sb2("c_hi", [P, KT, P], F32R)
        c_lo = sb2("c_lo", [P, KT, P], F32R)
        router_hi = sb2("router_hi", [P, KT, EXPERTS], F32R)
        router_lo = sb2("router_lo", [P, KT, EXPERTS], F32R)
        decay_c = sb2("decay_c", [P, 8, DEPTH * BT])
        mixer_memory = ctx.enter_context(ExitStack())

        def sbm(name, shape, dtype=F32):
            return sb(name, shape, dtype, mixer_memory)

        g_norm = sbm("g_norm", [P, P])
        wg2 = sbm("wg2", [GLA_RANK, GLA_KD])
        block_w = sbm("block_w", [P, 2 * BT, P])
        x_pad = sbm("x_pad", [P, BT, SEQ + CONV_W - 1])
        u_rg = sbm("u_rg", [P, BT, SEQ])
        r_rg = sbm("r_rg", [P, BT, SEQ])
        th_rg = sbm("th_rg", [P, BT, SEQ])
        i_rg = sbm("i_rg", [P, BT, SEQ])
        q_g = sbm("q_g", [P, 2, SEQ])
        k_g = sbm("k_g", [P, 2, SEQ])
        lf_g = sbm("lf_g", [P, 2, SEQ])
        bc_g = sbm("bc_g", [P, 2, SEQ])
        ke_g = sbm("ke_g", [P, 2, SEQ])
        scores = sbm("scores_2", [P, TILES * HEADS, P])
        scores_x = sh[:, 0:HEADS * P].rearrange("p (h t) -> p h t", t=P)
        qe_g = hidden2[:, :].rearrange("p (h t) -> p h t", t=SEQ)
        values = flat(y)[:, 0:TILES * HALF].rearrange("p (t n) -> p t n", t=TILES)
        gate_g = flat(y)[:, TILES * HALF:].rearrange("p (t n) -> p t n", t=TILES)

        over = all_done() + [(small_loaded, small_count[0])]
        for q in (act, dve, pool):
            q.wait(*over)

        t = act.then(lambda e: e.activation(tiny[:, 0:KT], col("c", 0, KT), ACT.Silu))
        wide = tiny[:, 0:KT].unsqueeze(2).broadcast_to([P, KT, P])
        t = act.then(lambda e: e.activation(c_hi[:, :, :], wide, ACT.Copy), t)
        c_ready = dve.then(lambda e: e.tensor_tensor(c_lo[:, :, :], wide, c_hi[:, :, :].bitcast(F32), ALU.subtract), t)
        router = col("router", 0, KT * EXPERTS).rearrange("p (k e) -> p k e", e=EXPERTS)
        t = act.then(lambda e: e.activation(router_hi[:, :, :], router, ACT.Copy))
        router_ready = dve.then(lambda e: e.tensor_tensor(router_lo[:, :, :], router, router_hi[:, :, :].bitcast(F32), ALU.subtract), t)

        R = lambda i: decay_c[:, i, :]
        lam = col("lam", 0, DEPTH * BT)
        t = act.then(lambda e: e.activation(R(1), lam, ACT.Abs))
        t = act.then(lambda e: e.activation(R(1), R(1), ACT.Exp, scale=-1.0), t)
        dve.then(lambda e: e.tensor_scalar(R(2), R(1), 2.0, None, ALU.add), t)
        dve.then(lambda e: e.reciprocal(R(2), R(2)))
        dve.then(lambda e: e.tensor_tensor(R(1), R(1), R(2), ALU.mult))
        dve.then(lambda e: e.tensor_tensor(R(2), R(1), R(1), ALU.mult))
        dve.then(lambda e: e.memset(R(3), 1.0 / 19))
        for n in range(17, 0, -2):
            dve.then(lambda e: e.tensor_tensor(R(3), R(3), R(2), ALU.mult))
            dve.then(lambda e, n=n: e.tensor_scalar(R(3), R(3), 1.0 / n, None, ALU.add))
        dve.then(lambda e: e.tensor_tensor(R(3), R(3), R(1), ALU.mult))
        dve.then(lambda e: e.tensor_scalar(R(4), lam, -1.0, 0.0, ALU.mult, ALU.max))
        dve.then(lambda e: e.scalar_tensor_tensor(R(0), R(3), 2.0, R(4), ALU.mult, ALU.add))
        dve.then(lambda e: e.tensor_scalar(R(5), R(0), -RG_C, None, ALU.mult))
        dve.then(lambda e: e.tensor_scalar(R(0), R(0), RG_C, None, ALU.mult))
        pool.then(lambda e: e.memset(x_pad[:, :, 0:CONV_W - 1], 0.0))

        def modulation(l, part):
            targets = (sh, sc, gt[part])
            for i, tile in enumerate(targets):
                bias = load(tile[:, :], w["ada_b"][l, (3 * part + i) * D:(3 * part + i + 1) * D].partition_broadcast(P),
                            dve.now())
            for i, tile in enumerate(targets):
                for half in range(2):
                    b = (0, 1)[half]
                    for u in range(2):
                        hi, lo, ready = unit()
                        s = []
                        for k in range(4):
                            kt = 4 * u + k
                            s += product(banks[b][:, :], c_hi[:, kt, :], c_lo[:, kt, :], hi[:, k, :], lo[:, k, :],
                                         u == 0 and k == 0, u == 1 and k == 3, None)
                        done = issue_all(s, ready, c_ready, bank_read[b])
                        used.append(done)
                    cut = slice(half * N, (half + 1) * N)
                    bank_read[b] = dve.then(lambda e, tile=tile, cut=cut, b=b: e.tensor_tensor(
                        tile[:, cut], banks[b][:, :], tile[:, cut], ALU.add), done, bias)

        def rms_rstd(*tokens):
            for tile in range(TILES):
                t = act.then(lambda e, tile=tile: e.activation(y[:, tile, :], x[:, tile, :], ACT.Square,
                                                               accum_out=rstd[:, tile:tile + 1]), dve.now(), *tokens)
            return rstd_of(rstd[:, :], rstd[:, :], 1.0 / D, RMS_EPS, t)

        def modulated(params):
            dve.then(lambda e: e.scalar_tensor_tensor(sc[:, :], sc[:, :], 1.0, norm_g[:, :], ALU.add, ALU.mult), params)
            for tile in range(TILES):
                dve.then(lambda e, tile=tile: e.scalar_tensor_tensor(
                    y[:, tile, :], x[:, tile, :], rstd[:, tile:tile + 1], sc[:, :], ALU.mult, ALU.mult))
                dve.then(lambda e, tile=tile: e.tensor_tensor(y[:, tile, :], y[:, tile, :], sh[:, :], ALU.add))
            return transpose_x(y)

        def add_gated(part, done):
            for tile in range(TILES):
                for half in range(2):
                    b = 4 + 2 * tile + half
                    cut = slice(half * N, (half + 1) * N)
                    bank_read[b] = dve.then(lambda e, tile=tile, cut=cut, b=b: e.tensor_tensor(
                        y[:, tile, cut], banks[b][:, :], gt[part][:, cut], ALU.mult), done)
                dve.then(lambda e, tile=tile: e.tensor_tensor(x[:, tile, :], x[:, tile, :], y[:, tile, :], ALU.add))

        def expert_stage():
            def sbe(name, shape, dtype=F32):
                return sb(name, shape, dtype, second)

            h_hi, h_lo = sbe("h_hi", [P, TILES, D], F32R), sbe("h_lo", [P, TILES, D], F32R)
            slots_hi = (xt_hi, sbe("xe_hi", [P, KT, SEQ], F32R))
            slots_lo = (xt_lo, sbe("xe_lo", [P, KT, SEQ], F32R))
            to_slot = sbe("to_slot", [P, TILES, SEQ], F32R)
            from_slot = sbe("from_slot", [P, TILES, SEQ])
            slot_iota = sbe("slot_iota", [P, SEQ])
            before, ones = sbe("before", [P, P]), sbe("ones", [P, P])
            chosen = sbe("chosen", [P, TILES, EXPERTS])
            rank = sbe("rank", [P, TILES + 1, EXPERTS])
            counts = sbe("counts", [P, EXPERTS], I32)
            total = (sh, sc)
            slot_out = y

            def count_and_rank():
                dve.then(lambda e: e.tensor_tensor(before[:, :], causal[:, :], ident[:, :], ALU.subtract))
                t = dve.then(lambda e: e.memset(ones[:, :], 1.0))
                sums_of = (((before, 0),), ((ones, 0), (before, 1)), ((ones, 0), (ones, 1)))
                s = []
                for i, parts in enumerate(sums_of):
                    for n, (m, tile) in enumerate(parts):
                        s.append(lambda e, i=i, n=n, m=m, tile=tile, last=n == len(parts) - 1: e.matmul(
                            banks[3][:, i * EXPERTS:(i + 1) * EXPERTS], m[:, :], chosen[:, tile, :],
                            start=n == 0, stop=last))
                done = issue_all(s, t, bank_read[3])
                bank_read[3] = dve.then(lambda e: e.tensor_copy(
                    rank[:, :, :].rearrange("p a b -> p (a b)"), banks[3][:, 0:(TILES + 1) * EXPERTS]), done)
                return dve.then(lambda e: e.tensor_copy(counts[:, :], rank[:, TILES, :]))

            def build_to_slot(x_of, *tokens):
                for tile in range(TILES):
                    t = dve.then(lambda e, tile=tile: e.tensor_scalar(
                        to_slot[:, tile, :], slot_iota[:, :], rank[:, tile, x_of:x_of + 1],
                        chosen[:, tile, x_of:x_of + 1], ALU.is_equal, ALU.mult), *tokens)
                return t

            def gather(x_of, r, ready):
                hi_to, lo_to = slots_hi[x_of % 2], slots_lo[x_of % 2]
                s = []
                for k in range(2):
                    cut = slice((2 * r + k) * P, (2 * r + k + 1) * P)
                    parts = [(part, tile) for tile in range(TILES) for part in (h_hi, h_lo)]
                    for n, (part, tile) in enumerate(parts):
                        s.append(lambda e, k=k, cut=cut, n=n, part=part, tile=tile: e.matmul(
                            banks[3][:, k * SEQ:(k + 1) * SEQ], part[:, tile, cut], to_slot[:, tile, :],
                            start=n == 0, stop=n == 2 * TILES - 1))
                done = issue_all(s, ready, bank_read[3])
                src = banks[3][:, :].rearrange("p (k t) -> p k t", t=SEQ)
                hi, lo = hi_to[:, 2 * r:2 * r + 2, :], lo_to[:, 2 * r:2 * r + 2, :]
                t = act.free(lambda e: e.activation(hi, src, ACT.Copy), done)
                bank_read[3] = dve.free(lambda e: e.tensor_tensor(lo, src, hi.bitcast(F32), ALU.subtract), t)
                return bank_read[3]

            def turn_from_slot():
                pe.wait(bank_read[3])
                for st in range(TILES):
                    for tile in range(TILES):
                        step = lambda e, st=st, tile=tile: e.transpose(
                            banks[3][:, st * SEQ + tile * P:st * SEQ + (tile + 1) * P],
                            to_slot[:, tile, st * P:(st + 1) * P].bitcast(F32), ident[:, :])
                        if st == 1 and tile == 1:
                            done = pe.free(step)
                        else:
                            pe.quiet(step)
                bank_read[3] = act.free(lambda e: e.activation(
                    from_slot[:, :, :], banks[3][:, :].rearrange("p (s t) -> p s t", t=SEQ), ACT.Copy), done)
                return done, bank_read[3]

            def two_tiles(steps_of, *tokens):
                pe.wait(*tokens)
                for s in steps_of(1):
                    pe.second_only(s)
                steps = list(steps_of(0))
                for s in steps[:-1]:
                    pe.quiet(s)
                return pe.free(steps[-1])

            def up(x_of, x_ready):
                hi_x, lo_x = slots_hi[x_of % 2], slots_lo[x_of % 2]
                for u in range(2):
                    hi, lo, ready = unit()

                    def steps_of(tile):
                        cut = slice(tile * P, (tile + 1) * P)
                        for k in range(4):
                            yield from product(banks[tile][:, :], hi_x[:, 4 * u + k, cut], lo_x[:, 4 * u + k, cut],
                                               hi[:, k, :], lo[:, k, :], u == 0 and k == 0, u == 1 and k == 3, None)
                    done = two_tiles(steps_of, ready, x_ready, bank_read[0], bank_read[1])
                    used.append(done)
                for tile in range(TILES):
                    a, b = banks[tile][:, 0:FF_CHUNK], banks[tile][:, FF_CHUNK:N]
                    t = act.free(lambda e: e.activation(silu_a[:, tile, :], a, ACT.Silu), done)
                    bank_read[tile] = dve.free(lambda e: e.tensor_tensor(
                        hidden[:, tile, :], b, silu_a[:, tile, :], ALU.mult), t)
                return bank_read[1]

            def turn(ready):
                pe.wait(bank_read[2], ready)
                for k in range(2):
                    for tile in range(TILES):
                        step = lambda e, k=k, tile=tile: e.transpose(
                            banks[2][:, k * SEQ + tile * P:k * SEQ + (tile + 1) * P],
                            hidden[:, tile, k * P:(k + 1) * P], ident[:, :])
                        if k == 1 and tile == 1:
                            done = pe.free(step)
                        else:
                            pe.quiet(step)
                src = banks[2][:, :].rearrange("p (k t) -> p k t", t=SEQ)
                t = act.free(lambda e: e.activation(ht_hi[:, :, :], src, ACT.Copy), done)
                bank_read[2] = dve.free(lambda e: e.tensor_tensor(
                    ht_lo[:, :, :], src, ht_hi[:, :, :].bitcast(F32), ALU.subtract), t)
                return bank_read[2]

            def down(j, ready):
                hi, lo, there = unit()

                def steps_of(tile):
                    cut = slice(tile * P, (tile + 1) * P)
                    for half in range(2):
                        for k in range(2):
                            yield from product(banks[4 + 2 * tile + half][:, :], ht_hi[:, k, cut], ht_lo[:, k, cut],
                                               hi[:, 2 * k + half, :], lo[:, 2 * k + half, :],
                                               j == 0 and k == 0, j == FF_TURNS - 1 and k == 1, None)
                done = two_tiles(steps_of, there, ready, *(bank_read[4:8] if j == 0 else ()))
                used.append(done)
                return done

            def scatter(x_of, ready):
                pe.wait(ready, *bank_read[4:8])
                for tile in range(TILES):
                    cut = slice(tile * P, (tile + 1) * P)
                    for half in range(2):
                        wide = slice(half * N, (half + 1) * N)
                        bank = banks[4 + 2 * tile + half]
                        pe.second_only(lambda e, bank=bank, cut=cut, wide=wide: e.matmul(
                            bank[:, :], from_slot[:, 1, cut], slot_out[:, 1, wide], start=True, stop=False))
                        done = pe.free(lambda e, bank=bank, cut=cut, wide=wide: e.matmul(
                            bank[:, :], from_slot[:, 0, cut], slot_out[:, 0, wide], start=not pe.second, stop=True))
                        gate = gates[:, tile, x_of:x_of + 1]
                        dst = total[tile][:, wide]
                        if x_of == 0:
                            t = dve.free(lambda e: e.tensor_scalar(dst, bank[:, :], gate, None, ALU.mult), done)
                        else:
                            t = dve.free(lambda e: e.scalar_tensor_tensor(dst, bank[:, :], gate, dst, ALU.mult, ALU.add), done)
                        bank_read[4 + 2 * tile + half] = t

            def has_second(x_of):
                return nc.tensor.value_load(counts[0:1, x_of:x_of + 1]) > P

            def run(x_ready):
                loaded = load(slot_iota[:, :], w["slots"])
                split_h = []
                for tile in range(TILES):
                    t = act.free(lambda e, tile=tile: e.activation(h_hi[:, tile, :], y[:, tile, :], ACT.Copy), x_ready)
                    split_h.append(dve.free(lambda e, tile=tile: e.tensor_tensor(
                        h_lo[:, tile, :], y[:, tile, :], h_hi[:, tile, :].bitcast(F32), ALU.subtract), t))
                counted = count_and_rank()
                t = build_to_slot(0, loaded)
                for r in range(KT // 2):
                    gathered = gather(0, r, [t, *split_h])
                pe.wait(counted)
                out_ready = split_h
                returned = None
                for x_of in range(EXPERTS):
                    branch = has_second(x_of)
                    pe.record()
                    hidden_in = up(x_of, gathered)
                    pe.play_if(branch)
                    if x_of:
                        branch = has_second(x_of - 1)
                        pe.record()
                        scatter(x_of - 1, [out_ready, returned])
                        pe.play_if(branch)
                    branch = has_second(x_of)
                    pe.record()
                    for j in range(FF_TURNS):
                        if j:
                            hidden_in = up(x_of, gathered)
                            down(j - 1, turned)
                        turned = turn(hidden_in)
                        if j == 1:
                            slot_used, returned = turn_from_slot()
                        if x_of < EXPERTS - 1:
                            if j == 3:
                                t = build_to_slot(x_of + 1, slot_used)
                            if j in (5, 6, 7, FF_TURNS - 1):
                                next_in = gather(x_of + 1, min(j - 5, 3), t)
                    done = down(FF_TURNS - 1, turned)
                    pe.play_if(branch)
                    for tile in range(TILES):
                        for half in range(2):
                            b = 4 + 2 * tile + half
                            bank_read[b] = act.free(lambda e, tile=tile, half=half, b=b: e.activation(
                                slot_out[:, tile, half * N:(half + 1) * N], banks[b][:, :], ACT.Copy), done, out_ready)
                    out_ready = act.now()
                    if x_of < EXPERTS - 1:
                        gathered = next_in
                branch = has_second(EXPERTS - 1)
                pe.record()
                scatter(EXPERTS - 1, [out_ready, returned])
                pe.play_if(branch)

            run.chosen = chosen
            return run

        head_rows = lambda h: slice((h % 2) * GLA_DK, (h % 2 + 1) * GLA_DK)

        for l in range(DEPTH):
            params = load(norm_g[:, :], w["norm_mix_g"][l].partition_broadcast(P), dve.now())
            rms_rstd()
            modulation(l, 0)
            x_ready = modulated(params)
            free = all_done()
            load(g_norm[:, :], w["gla_norm_g"][l].partition_broadcast(P), *free)
            load(wg2[:, :], w["gla_wg2"][l])
            params = load(block_w[:, :, :], w["rg_w"][l])
            norm_f = load(norm_g[:, :], w["norm_ffn_g"][l].partition_broadcast(P))

            done = feature_block((4, 5), x_ready)
            for i in range(2):
                src = banks[4 + i][:, :].rearrange("p (m t) -> p m t", t=SEQ)
                bank_read[4 + i] = act.then(lambda e, i=i, src=src: e.activation(
                    x_pad[:, 2 * i:2 * i + 2, CONV_W - 1:], src, ACT.Copy), done, free, pool.now())
            t = act.now()
            for f in range(BT):
                tap = lambda n, f=f: (x_pad[:, f, n:n + SEQ], col("conv_w", (l * CONV_W + n) * BT + f))
                dve.then(lambda e, f=f, tap=tap: e.tensor_scalar(
                    u_rg[:, f, :], tap(0)[0], tap(0)[1], col("conv_b", l * BT + f), ALU.mult, ALU.add), t)
                for n in range(1, CONV_W):
                    dve.then(lambda e, f=f, n=n, tap=tap: e.scalar_tensor_tensor(
                        u_rg[:, f, :], tap(n)[0], tap(n)[1], u_rg[:, f, :], ALU.mult, ALU.add))
            u_ready = dve.now()
            done = feature_block((6, 7))
            for i, dst in enumerate((q_g, k_g)):
                src = banks[6 + i][:, :].rearrange("p (m t) -> p m t", t=SEQ)
                bank_read[6 + i] = act.then(lambda e, i=i, src=src, dst=dst: e.activation(
                    dst[:, :, :], src, ACT.Copy, scale=(GLA_DK ** -0.5, 1.0)[i]), done)

            hi, lo, ready = unit()
            s = []
            tail = lambda a: a.rearrange("p k n -> p (k n)")[:, 0:KT * P].rearrange("p (k n) -> p k n", n=P)
            for k in range(KT):
                s += product(banks[0][:, 0:SEQ], tail(hi)[:, k, :], tail(lo)[:, k, :], xt_hi[:, k, :], xt_lo[:, k, :],
                             k == 0, k == KT - 1, None)
            done = issue_all(s, ready, bank_read[0])
            used.append(done)
            bank_read[0] = t = act.then(lambda e: e.activation(ke_g[0:GLA_RANK, 0, :], banks[0][0:GLA_RANK, 0:SEQ], ACT.Copy), done, free)
            s = [lambda e, m=m: e.matmul(banks[1][:, m * SEQ:(m + 1) * SEQ], wg2[:, m * P:(m + 1) * P],
                                         ke_g[0:GLA_RANK, 0, :], start=True, stop=True) for m in range(2)]
            done = issue_all(s, t, params, bank_read[1])
            for m in range(2):
                bank_read[1] = dve.then(lambda e, m=m: e.tensor_scalar(
                    lf_g[:, m, :], banks[1][:, m * SEQ:(m + 1) * SEQ], col("gla_bg", l * 2 + m), None, ALU.add), done, free)
            act.then(lambda e: e.activation(flat(bc_g), flat(lf_g), ACT.Abs), dve.now())
            t = act.then(lambda e: e.activation(flat(bc_g), flat(bc_g), ACT.Exp, scale=-1.0))
            t = dve.then(lambda e: e.tensor_scalar(flat(bc_g), flat(bc_g), 1.0, None, ALU.add), t)
            t = act.then(lambda e: e.activation(flat(bc_g), flat(bc_g), ACT.Ln), t)
            t = dve.then(lambda e: e.scalar_tensor_tensor(flat(lf_g), flat(lf_g), 0.0, flat(bc_g), ALU.min, ALU.subtract), t)
            restart = restart_mask(flat(ke_g), 2 * SEQ, t, pe.now())
            dve.then(lambda e: e.tensor_tensor_scan(flat(bc_g), flat(ke_g), flat(lf_g), 0.0, ALU.mult, ALU.add), restart)

            for g, (dst, bias) in enumerate(((r_rg, "rg_ba"), (i_rg, "rg_bx"))):
                s = [lambda e, f=f, g=g: e.matmul(banks[2 + f // 2][:, (f % 2) * SEQ:(f % 2 + 1) * SEQ],
                                                  block_w[:, g * BT + f, :], u_rg[:, f, :], start=True, stop=True)
                     for f in range(BT)]
                done = issue_all(s, u_ready, params, bank_read[2], bank_read[3])
                for f in range(BT):
                    bank_read[2 + f // 2] = act.then(lambda e, f=f, dst=dst, bias=bias: e.activation(
                        dst[:, f, :], banks[2 + f // 2][:, (f % 2) * SEQ:(f % 2 + 1) * SEQ], ACT.Sigmoid,
                        bias=col(bias, l * BT + f)), done)
            gates_in = act.now()

            done = token_block((0, 1), xt_hi, xt_lo, 2)
            for tile in range(TILES):
                bank_read[tile] = act.free(lambda e, tile=tile: e.activation(
                    values[:, tile, :], banks[tile][:, :], ACT.Copy), done)
            values_in = act.now()
            for f in range(BT):
                act.then(lambda e, f=f: e.activation(th_rg[:, f, :], r_rg[:, f, :], ACT.Tanh, scale=decay_c[:, 0, l * BT + f:l * BT + f + 1]))
            for f in range(BT):
                t = act.then(lambda e, f=f: e.activation(r_rg[:, f, :], r_rg[:, f, :], ACT.Exp, scale=decay_c[:, 5, l * BT + f:l * BT + f + 1]))
            spare = flat(x_pad)[:, 0:BT * SEQ]
            dve.then(lambda e: e.tensor_scalar(spare, flat(th_rg), 1.0, None, ALU.add), t)
            dve.then(lambda e: e.reciprocal(spare, spare))
            t = dve.then(lambda e: e.scalar_tensor_tensor(flat(th_rg), flat(th_rg), 2.0, spare, ALU.mult, ALU.mult))
            t = act.then(lambda e: e.activation(flat(th_rg), flat(th_rg), ACT.Sqrt), t)
            dve.then(lambda e: e.memset(th_rg[:, :, 0:1], 1.0), t)
            dve.then(lambda e: e.memset(r_rg[:, :, 0:1], 0.0))
            dve.then(lambda e: e.tensor_tensor(flat(i_rg), flat(i_rg), flat(th_rg), ALU.mult), gates_in)
            dve.then(lambda e: e.tensor_tensor(flat(i_rg), flat(i_rg), flat(u_rg), ALU.mult))
            dve.then(lambda e: e.tensor_tensor_scan(flat(u_rg), flat(r_rg), flat(i_rg), 0.0, ALU.mult, ALU.add))
            h_ready = dve.now()
            pad_again = pool.then(lambda e: e.memset(x_pad[:, :, 0:CONV_W - 1], 0.0), h_ready)

            zeroed = pool.then(lambda e: e.memset(qe_g, 0.0), all_done())
            zeroed = pool.then(lambda e: e.memset(scores[:, :, :], 0.0))
            mid = flat(bc_g).rearrange("p (n b) -> p n b", b=CHUNK)[:, :, CHUNK // 2 - 1:CHUNK // 2].broadcast_to([P, 2 * SEQ // CHUNK, CHUNK])
            chunks = lambda a: flat(a).rearrange("p (n b) -> p n b", b=CHUNK)
            t = dve.then(lambda e: e.tensor_tensor(chunks(lf_g), chunks(bc_g), mid, ALU.subtract))
            t = act.then(lambda e: e.activation(flat(ke_g), flat(lf_g), ACT.Exp, scale=1.0 / GLA_TAU), t)
            for h in range(2):
                rows = head_rows(h)
                t = dve.then(lambda e, h=h, rows=rows: e.tensor_tensor(
                    qe_g[rows, h::2, :], q_g[rows, :, :], ke_g[rows, :, :], ALU.mult), t, zeroed)
            t = act.then(lambda e: e.activation(flat(ke_g), flat(lf_g), ACT.Exp, scale=-1.0 / GLA_TAU), t)
            t = dve.then(lambda e: e.tensor_tensor(flat(ke_g), flat(ke_g), flat(k_g), ALU.mult), t)
            k_of, q_of = (lambda h: ke_g[:, h // 2, :]), (lambda h: qe_g[:, h, :])

            scored = score_products(k_of, q_of, t)
            take_scores(scores, LOCAL, scored)
            done = feature_block((4, 5))
            for i in range(2):
                src = banks[4 + i][:, :].rearrange("p (m t) -> p m t", t=SEQ)
                bank_read[4 + i] = act.then(lambda e, i=i, src=src: e.activation(
                    th_rg[:, 2 * i:2 * i + 2, :], src, ACT.Gelu_apprx_tanh), done, h_ready)
            t = dve.then(lambda e: e.tensor_tensor(flat(u_rg), flat(u_rg), flat(th_rg), ALU.mult), act.now())

            for block in (P, SEQ):
                d, half, decays = level(bc_g[:, :, :], lf_g[:, :, :], 1.0 / GLA_TAU, block, 2, True)
                for h in range(2):
                    rows = head_rows(h)
                    n = SEQ // block
                    qv = qe_g[rows, h::2, :].rearrange("p h (n b) -> p h n b", b=block)[:, :, :, half:]
                    src = q_g[rows, :, :].rearrange("p h (n b) -> p h n b", b=block)[:, :, :, half:]
                    dv = lf_g[rows, :, :].rearrange("p h (n b) -> p h n b", b=block)[:, :, :, half:]
                    dve.then(lambda e, qv=qv, src=src, dv=dv: e.tensor_tensor(qv, src, dv, ALU.mult), decays, pe.now())
                view = lambda a: flat(a).rearrange("p (n b) -> p n b", b=block)
                t = dve.then(lambda e: e.tensor_tensor(view(ke_g)[:, :, 0:half], view(k_g)[:, :, 0:half], d[:, :, 0:half], ALU.mult))
                if block == P:
                    scored = score_products(k_of, q_of, t)
                    take_scores(scores, LEVELS.index(P), scored)
                    v = flat(bc_g).rearrange("p (n c t) -> p n c t", c=2, t=CHUNK)
                    last = v[:, :, 0, CHUNK - 1:CHUNK].broadcast_to([P, 2 * TILES, CHUNK])
                    dve.then(lambda e: e.tensor_tensor(v[:, :, 1, :], v[:, :, 1, :], last, ALU.add))
                else:
                    crossed = cross_products(scores_x, k_of, q_of, t)
            scored = [crossed, dve.now()]
            done = token_block((6, 7), xt_hi, xt_lo, 2)
            for tile in range(TILES):
                bank_read[6 + tile] = act.free(lambda e, tile=tile: e.activation(
                    gate_g[:, tile, :], banks[6 + tile][:, :], ACT.Silu), done)
            t = act.then(lambda e: e.activation(xt_hi[:, 0:BT, :], u_rg[:, :, :], ACT.Copy), done, dve.now())
            dve.then(lambda e: e.tensor_tensor(xt_lo[:, 0:BT, :], u_rg[:, :, :], xt_hi[:, 0:BT, :].bitcast(F32), ALU.subtract), t)
            done = attend(scores, scores_x, lambda tile: values[:, tile, :], [*scored, values_in])
            o = flat(r_rg).rearrange("p (t n) -> p t n", t=TILES)
            head_norm(done, lambda h: g_norm[:, :], gate_g, o, params, flat(i_rg))
            for tile in range(TILES):
                t = transpose_into(lambda k, tile=tile, o=o: o[:, tile, k * P:(k + 1) * P],
                                   [(k, BT + k) for k in range(BT)], tile, xt_hi, xt_lo, (2 + tile,), dve.now())
            token_block((4, 6), xt_hi, xt_lo, 2, 0, t)
            done = token_block((5, 7), xt_hi, xt_lo, 2)
            add_gated(0, done)

            rms_rstd()
            modulation(l, 1)
            x_ready = modulated(norm_f)
            if l % 2 == 0:
                done = feed_forward(FF_TURNS, x_ready)
                add_gated(1, done)
            else:
                mixer_memory.close()
                experts = expert_stage()
                chosen = experts.chosen
                for tile in range(TILES):
                    s = []
                    for k in range(KT):
                        cut = slice(tile * P, (tile + 1) * P)
                        s += product(banks[tile][:, 0:EXPERTS], xt_hi[:, k, cut], xt_lo[:, k, cut],
                                     router_hi[:, k, :], router_lo[:, k, :], k == 0, k == KT - 1, None)
                    done = issue_all(s, x_ready, router_ready, bank_read[tile])
                    logits, top = tiny[:, 0:8], tiny[:, 8:16]
                    where, where_f = tiny[:, 16:24].bitcast(U32), tiny[:, 24:32]
                    e2, p1, p2, g2 = tiny[:, 32:33], tiny[:, 33:34], tiny[:, 34:35], tiny[:, 40:48]
                    bank_read[tile] = dve.then(lambda e, tile=tile: e.tensor_copy(logits, banks[tile][:, 0:EXPERTS]), done)
                    dve.then(lambda e: e.max(top, logits))
                    dve.then(lambda e: e.max_index(where, top, logits))
                    dve.then(lambda e: e.tensor_copy(where_f, where))
                    t = dve.then(lambda e: e.tensor_tensor(e2, top[:, 1:2], top[:, 0:1], ALU.subtract))
                    t = act.then(lambda e: e.activation(e2, e2, ACT.Exp), t)
                    dve.then(lambda e: e.tensor_scalar(p1, e2, 1.0, None, ALU.add), t)
                    dve.then(lambda e: e.reciprocal(p1, p1))
                    dve.then(lambda e: e.tensor_tensor(p2, p1, e2, ALU.mult))
                    iota = col("iota", 0, EXPERTS)
                    dve.then(lambda e, tile=tile: e.tensor_scalar(gates[:, tile, :], iota, where_f[:, 0:1], p1, ALU.is_equal, ALU.mult))
                    dve.then(lambda e: e.tensor_scalar(g2, iota, where_f[:, 1:2], p2, ALU.is_equal, ALU.mult))
                    dve.then(lambda e, tile=tile: e.tensor_tensor(gates[:, tile, :], gates[:, tile, :], g2, ALU.add))
                    dve.then(lambda e, tile=tile: e.tensor_scalar(chosen[:, tile, :], iota, where_f[:, 0:1], None, ALU.is_equal))
                    dve.then(lambda e, tile=tile: e.scalar_tensor_tensor(
                        chosen[:, tile, :], iota, where_f[:, 1:2], chosen[:, tile, :], ALU.is_equal, ALU.add))
                experts(x_ready)
                for tile in range(TILES):
                    dve.then(lambda e, tile=tile: e.tensor_tensor(y[:, tile, :], (sh, sc)[tile][:, :], gt[1][:, :], ALU.mult))
                    dve.then(lambda e, tile=tile: e.tensor_tensor(x[:, tile, :], x[:, tile, :], y[:, tile, :], ALU.add))
        params = load(norm_g[:, :], w["final_g"].partition_broadcast(P), dve.now())
        rms_rstd()
        for tile in range(TILES):
            t = dve.then(lambda e, tile=tile: e.scalar_tensor_tensor(
                y[:, tile, :], x[:, tile, :], rstd[:, tile:tile + 1], norm_g[:, :], ALU.mult, ALU.mult), params)
            sp.wait(t)
            sp.quiet(lambda e, tile=tile: e.dma_start(out[tile * P:(tile + 1) * P, :], y[:, tile, :]).then_inc(out_written, 16))
        sp.quiet(lambda e: e.wait_ge(out_written, 16 * TILES))
        assert len(used) == len(stream), (len(used), len(stream))


def pack(a, order=None):
    lead, (k, n) = a.shape[:-2], a.shape[-2:]
    a = a.reshape(*lead, k // (4 * P), 4, P, n // N, N)
    m = len(lead)
    a = a.transpose(*range(m), m + 3, m, m + 2, m + 1, m + 4)
    if order is not None:
        a = a[..., order, :, :, :, :]
    return np.ascontiguousarray(a).reshape(*lead, -1, P, UNIT)


def pack_up(a, b):
    lead = a.shape[:-2]
    turns = [z.reshape(*lead, D, FF_TURNS, FF_CHUNK) for z in (a, b)]
    both = np.stack(turns, axis=-2)
    return pack(both.reshape(*lead, D, FF_TURNS * N))


def pack_down(a):
    lead = a.shape[:-2]
    m = len(lead)
    a = a.reshape(*lead, FF_TURNS, 2, P, 2, N).transpose(*range(m), m, m + 2, m + 1, m + 3, m + 4)
    return np.ascontiguousarray(a).reshape(*lead, FF_TURNS, P, UNIT)


def lay_out(i):
    f32 = np.float32
    w13 = lambda a: pack_up(a[..., :D_FF], a[..., D_FF:])
    out = {
        "x": i["x"].reshape(TILES, P, D),
        "ident": np.eye(P, dtype=f32),
        "causal": np.triu(np.ones((P, P), f32)),
        "masks": level_masks(),
        "slots": np.tile(np.arange(SEQ, dtype=f32), (P, 1)),
        "ffn1_up": w13(i["ffn1_w13"]), "ffn1_down": pack_down(i["ffn1_w2"]),
        "ffn2_up": w13(i["ffn2_w13"]), "ffn2_down": pack_down(i["ffn2_w2"]),
        "mix_in": pack(i["w_in"], [1, 0, 2, 5, 4, 3, 6, 7, 8, 9]),
        "branch_a": pack(i["w_branch_a"]), "branch_b": pack(i["w_branch_b"]), "mix_out": pack(i["w_out"]),
        "ada": pack(i["ada_w_2"]),
        "mix_in_2": pack(i["w_in_2"][:, :, :5 * N], [0, 2, 3, 1, 4]),
        "mix_out_2": pack(i["w_out_2"]),
        "dense_up": pack_up(i["ffn_w1_2"], i["ffn_w3_2"]), "dense_down": pack_down(i["ffn_w2_2"]),
    }
    up = pack_up(i["moe_w1_2"], i["moe_w3_2"])
    down = pack_down(i["moe_w2_2"])
    out["moe_up"] = up.reshape(up.shape[0], -1, P, UNIT)
    out["moe_down"] = down.reshape(down.shape[0], -1, P, UNIT)
    tail = np.zeros((DEPTH, P, KT, P), f32)
    tail[..., :GLA_RANK] = i["w_in_2"][:, :, 5 * N:].reshape(DEPTH, KT, P, GLA_RANK).transpose(0, 2, 1, 3)
    out["mix_in_2_tail"] = tail.reshape(DEPTH, P, KT * P)
    for name in ("ln_g", "ln_b", "hg_norm_g", "sg_ln_g", "sg_ln_b"):
        out[name] = i[name]
    for name in ("norm_mix_g", "norm_ffn_g", "ada_b", "final_g", "gla_norm_g", "gla_wg2"):
        out[name] = i[name + "_2"]
    out["sg_ws_t"] = np.ascontiguousarray(i["sg_ws"].transpose(0, 3, 1, 2))
    rg = np.zeros((DEPTH, P, 2, BT, P), f32)
    for g, name in enumerate(("rg_wa_2", "rg_wx_2")):
        blocks = i[name].reshape(DEPTH, BT, 2, P // 2, P // 2)
        for b in range(2):
            cut = slice(b * P // 2, (b + 1) * P // 2)
            rg[:, cut, g, :, cut] = blocks[:, :, b].transpose(0, 2, 1, 3)
    out["rg_w"] = rg.reshape(DEPTH, P, 2 * BT, P)

    def columns(a):
        return a.reshape(-1, P).T

    table = {
        "lb": columns(i["hg_lb"]), "conv_w": columns(i["rg_conv_w_2"]), "conv_b": columns(i["rg_conv_b_2"]),
        "rg_ba": columns(i["rg_ba_2"]), "rg_bx": columns(i["rg_bx_2"]), "lam": columns(i["rg_lambda_2"]),
        "gla_bg": columns(i["gla_bg_2"]), "sg_bs": columns(i["sg_bs"]), "c": columns(i["c_2"]),
        "router": i["router_w_2"].reshape(KT, P, EXPERTS).transpose(1, 0, 2).reshape(P, -1),
        "iota": np.tile(np.arange(EXPERTS, dtype=f32), (P, 1)),
    }
    out["cols"] = np.ascontiguousarray(np.concatenate([table[n] for n in COLS], axis=1))
    return {n: np.ascontiguousarray(a) for n, a in out.items()}


def kernel(**inputs):
    import concourse.bacc as bacc
    from concourse.bass_utils import run_bass_kernel_spmd

    arrays = lay_out({n: np.asarray(a) for n, a in inputs.items()})
    nc = bacc.Bacc("TRN2", target_bir_lowering=False, num_devices=1)
    w = {n: nc.dram_tensor(f"in_{n}", a.shape, mybir.dt.from_np(a.dtype), kind="ExternalInput").ap()
         for n, a in arrays.items()}
    out = nc.dram_tensor("result", (SEQ, D), F32, kind="ExternalOutput").ap()
    build(nc, w, out)
    got = run_bass_kernel_spmd(nc, [{f"in_{n}": a for n, a in arrays.items()}], core_ids=[0])
    return got.results[0]["result"].reshape(1, SEQ, D)
```

```python
from contextlib import ExitStack

import numpy as np

import concourse.bass as bass
from concourse import mybir

F32 = mybir.dt.float32
F32R = mybir.dt.float32r
U8 = mybir.dt.uint8
U32 = mybir.dt.uint32
I32 = mybir.dt.int32
ACT = mybir.ActivationFunctionType
ALU = mybir.AluOpType

P = 128
SEQ = 256
TILES = SEQ // P
D = 1024
KT = D // P
DEPTH = 2
D_FF = 2816
HEADS = 4
HALF = D // 2
BT = HALF // P
GLA_KD = 256
GLA_DK = GLA_KD // HEADS
GLA_RANK = 16
CONV_W = 4
EXPERTS = 8
CHUNK = 64
FF_CHUNK = 256
FF_TURNS = D_FF // FF_CHUNK
N = 512
UNIT = 4 * N

ALPHA = (2 * DEPTH) ** 0.25
LN_EPS = 1e-5
RMS_EPS = 1e-6
RG_C = 8.0
GLA_TAU = 16.0
LN_SHIFT = 64
LN_LOW = 2.0 ** -60

RAW_SLOTS = 4
SPLIT_SLOTS = 4
LOAD_GROUPS = 4

COLS = {}
_at = 0
for _name, _n in (("lb", DEPTH * HEADS), ("conv_w", DEPTH * CONV_W * BT), ("conv_b", DEPTH * BT),
                  ("rg_ba", DEPTH * BT), ("rg_bx", DEPTH * BT), ("lam", DEPTH * BT),
                  ("gla_bg", DEPTH * 2), ("sg_bs", DEPTH * HEADS), ("c", KT),
                  ("router", KT * EXPERTS), ("iota", EXPERTS)):
    COLS[_name] = (_at, _n)
    _at += _n
N_COLS = _at

LEVELS = [1, 2, 4, 8, 16, 32, 64, 128]
LOCAL = len(LEVELS)


def level_masks():
    s, t = np.arange(P)[:, None], np.arange(P)[None, :]
    out = np.zeros((P, len(LEVELS) + 1, P), np.float32)
    for i, b in enumerate(LEVELS):
        if b == 1:
            out[:, i] = s == t
        else:
            out[:, i] = (s // b == t // b) & (s % b < b // 2) & (t % b >= b // 2)
    out[:, LOCAL] = (s <= t) & (s // CHUNK == t // CHUNK)
    return out.reshape(P, -1)


class Queue:

    def __init__(self, engine, semaphore):
        self.engine = engine
        self.done = semaphore
        self.count = 0
        self.seen = {}
        self.tape = None
        self.second = True

    def wait(self, *tokens):
        for t in tokens:
            if t is None:
                continue
            if isinstance(t, list):
                self.wait(*t)
                continue
            sem, value = t
            if self.seen.get(id(sem), 0) < value:
                self.seen[id(sem)] = value
                self._issue(lambda e, sem=sem, value=value: e.wait_ge(sem, value))

    def now(self):
        return (self.done, self.count) if self.count else None

    def free(self, issue, *tokens):
        self.wait(*tokens)
        self.count += 1
        self._issue(lambda e: issue(e).then_inc(self.done, 1))
        return self.done, self.count

    def then(self, issue, *tokens):
        return self.free(issue, self.now(), *tokens)

    def quiet(self, issue, *tokens):
        self.wait(*tokens)
        self._issue(issue)

    def second_only(self, issue, *tokens):
        self.wait(*tokens)
        self._issue(issue, True)

    def _issue(self, issue, second_only=False):
        if self.tape is None:
            issue(self.engine)
        else:
            self.tape.append((issue, second_only))

    def record(self):
        self.tape = []

    def play_if(self, has_second):
        tape, self.tape = self.tape, None
        for second in (True, False):
            self.second = second
            with self.engine.If(has_second) if second else self.engine.Else():
                for issue, second_only in tape:
                    if second or not second_only:
                        issue(self.engine)
        self.second = True


def build(nc, w, out):
    with ExitStack() as ctx:
        def sb(name, shape, dtype=F32, where=ctx):
            return where.enter_context(nc.sbuf_tensor(name, shape, dtype))

        def sem(name):
            return ctx.enter_context(nc.semaphore(name))

        pe, act = Queue(nc.tensor, sem("pe_done")), Queue(nc.scalar, sem("act_done"))
        dve, pool = Queue(nc.vector, sem("dve_done")), Queue(nc.gpsimd, sem("pool_done"))
        sp = Queue(nc.sync, None)
        group_loaded = [sem(f"group_loaded_{i}") for i in range(LOAD_GROUPS)]
        first_loaded = sem("first_loaded")
        out_written = sem("out_written")
        raw_loaded = [sem(f"raw_loaded_{i}") for i in range(RAW_SLOTS)]

        banks = [ctx.enter_context(nc.psum_tensor(f"bank{i}", [P, N], F32)) for i in range(8)]
        bank_read = [None] * 8

        raw = sb("raw", [P, RAW_SLOTS, UNIT])
        w_hi = sb("w_hi", [P, SPLIT_SLOTS, UNIT], F32R)
        w_lo = sb("w_lo", [P, SPLIT_SLOTS, UNIT], F32R)
        x = sb("x", [P, TILES, D])
        y = sb("y", [P, TILES, D])
        xt_hi = sb("xt_hi", [P, KT, SEQ], F32R)
        xt_lo = sb("xt_lo", [P, KT, SEQ], F32R)
        with ExitStack() as mixer_view:
            ws = sb("ws", [P, HEADS, P], F32, mixer_view)
            scores_x = sb("scores_x", [P, HEADS, P], F32, mixer_view)
        ht_hi = sb("ht_hi", [P, 2, SEQ], F32R)
        ht_lo = sb("ht_lo", [P, 2, SEQ], F32R)
        hidden2 = sb("hidden2", [P, 2 * TILES * FF_CHUNK])
        silu_a = hidden2[:, 0:TILES * FF_CHUNK].rearrange("p (t n) -> p t n", t=TILES)
        hidden = hidden2[:, TILES * FF_CHUNK:].rearrange("p (t n) -> p t n", t=TILES)
        ident = sb("ident", [P, P])
        causal = sb("causal", [P, P])
        masks = sb("masks", [P, LOCAL + 1, P], U8)
        cols = sb("cols", [P, N_COLS])
        c_hi = sb("c_hi", [P, KT, P], F32R)
        c_lo = sb("c_lo", [P, KT, P], F32R)
        stats = sb("stats", [P, TILES, 2, 6])
        mean_var = sb("mean_var", [P, TILES, 2])
        rstd = sb("rstd", [P, TILES])
        sums = sb("sums", [P, 8])
        root_of_one = sb("root_of_one", [P, 1])
        lb = sb("lb", [P, 8, HEADS])
        decay_c = sb("decay_c", [P, 6, DEPTH * BT])
        gates = sb("gates", [P, TILES, EXPERTS])
        tiny = sb("tiny", [P, 64])

        def col(name, i, n=1):
            at = COLS[name][0] + i
            return cols[:, at:at + n]

        group_count = [0] * LOAD_GROUPS
        groups = [0]

        def load(pairs, *tokens):
            g = groups[0] % LOAD_GROUPS
            groups[0] += 1
            pool.wait(*tokens)
            if group_count[g]:
                pool.wait((group_loaded[g], group_count[g]))
            for dst, src in pairs:
                group_count[g] += 16
                pool.quiet(lambda e: e.dma_start(dst, src).then_inc(group_loaded[g], 16))
            return group_loaded[g], group_count[g]

        stream = []

        def product_units(array, first, n):
            stream.extend((array[first + i], UNIT) for i in range(n))

        def feed_forward_units(up, down, first_turn, turns, before, last):
            for j in range(turns):
                product_units(up, 2 * (first_turn + j), 2)
                if before or j:
                    product_units(down, first_turn + j - 1, 1)
            if last:
                product_units(down, first_turn + turns - 1, 1)

        for l in range(DEPTH):
            feed_forward_units(w["ffn1_up"][l], w["ffn1_down"][l], 0, FF_TURNS, False, True)
            product_units(w["mix_in"][l], 0, 20)
            product_units(w["branch_a"][l], 0, 2)
            product_units(w["branch_b"][l], 0, 2)
            product_units(w["mix_out"][l], 0, 4)
            feed_forward_units(w["ffn2_up"][l], w["ffn2_down"][l], 0, FF_TURNS, False, True)
        for l in range(DEPTH):
            product_units(w["ada"][l], 0, 12)
            stream.append((w["mix_in_2_tail"][l], KT * P))
            product_units(w["mix_in_2"][l], 0, 4)
            product_units(w["mix_in_2"][l], 4, 6)
            product_units(w["ada"][l], 12, 8)
            product_units(w["mix_out_2"][l], 0, 4)
            product_units(w["ada"][l], 20, 4)
            if l % 2 == 0:
                feed_forward_units(w["dense_up"][l // 2], w["dense_down"][l // 2], 0, FF_TURNS, False, True)
            else:
                for x_of in range(EXPERTS):
                    feed_forward_units(w["moe_up"][l // 2], w["moe_down"][l // 2], x_of * FF_TURNS, FF_TURNS, False, True)

        used = []
        split = []
        loads = [0]

        def load_unit():
            n = loads[0]
            if n >= len(stream):
                return
            loads[0] += 1
            src, size = stream[n]
            slot = n % RAW_SLOTS
            if n >= RAW_SLOTS:
                sp.wait(split[n - RAW_SLOTS])
            sp.quiet(lambda e: e.dma_start(raw[:, slot, 0:size], src).then_inc(raw_loaded[slot], 16))

        def split_unit():
            n = len(split)
            if n >= len(stream):
                return
            size = stream[n][1]
            src = raw[:, n % RAW_SLOTS, 0:size]
            hi, lo = w_hi[:, n % SPLIT_SLOTS, 0:size], w_lo[:, n % SPLIT_SLOTS, 0:size]
            arrived = (raw_loaded[n % RAW_SLOTS], 16 * (n // RAW_SLOTS + 1))
            free = used[n - SPLIT_SLOTS] if n >= SPLIT_SLOTS else None
            rounded = act.free(lambda e: e.activation(hi, src, ACT.Copy), arrived, free)
            split.append(dve.free(lambda e: e.tensor_tensor(lo, src, hi.bitcast(F32), ALU.subtract),
                                  arrived, free, rounded))
            load_unit()

        for tile in range(TILES):
            sp.quiet(lambda e: e.dma_start(x[:, tile, :], w["x"][tile]).then_inc(first_loaded, 16))
        sp.quiet(lambda e: e.dma_start(ident[:, :], w["ident"]).then_inc(first_loaded, 16))
        first_in = (first_loaded, 16 * (TILES + 1))
        for _ in range(RAW_SLOTS):
            load_unit()

        taken = [0]

        def split_ahead():
            while len(split) < min(len(used) + SPLIT_SLOTS, len(stream)):
                split_unit()

        def unit():
            n = taken[0]
            taken[0] += 1
            split_ahead()
            slot = n % SPLIT_SLOTS
            hi = w_hi[:, slot, :].rearrange("p (k n) -> p k n", n=N)
            lo = w_lo[:, slot, :].rearrange("p (k n) -> p k n", n=N)
            return hi, lo, split[n]

        side = []

        def beside():
            side[:] = [g for g in side if next(g, "ended") != "ended"]

        def product(dst, hi_l, lo_l, hi_r, lo_r, start, stop, skip=False):
            for i, (a, b) in enumerate(((hi_l, hi_r), (hi_l, lo_r), (lo_l, hi_r))):
                first, last = start and i == 0, stop and i == 2
                yield lambda e, a=a, b=b, first=first, last=last: e.matmul(
                    dst, a, b, start=first, stop=last, skip_group_check=skip)

        def issue_all(steps, *tokens):
            steps = list(steps)
            pe.wait(*tokens)
            for s in steps[:-1]:
                pe.quiet(s)
            return pe.free(steps[-1])

        def unit_steps(bank, lhs_hi, lhs_lo, kt0, tile, hi, lo, start, stop):
            cut = slice(tile * P, (tile + 1) * P)
            for k in range(4):
                yield from product(banks[bank][:, :], lhs_hi[:, kt0 + k, cut], lhs_lo[:, kt0 + k, cut],
                                   hi[:, k, :], lo[:, k, :], start and k == 0, stop and k == 3)

        def token_block(pair, x_ready=(None, None)):
            done = [None] * TILES
            for u in range(2):
                hi, lo, ready = unit()
                for tile in range(TILES):
                    done[tile] = issue_all(unit_steps(pair[tile], xt_hi, xt_lo, 4 * u, tile, hi, lo, u == 0, u == 1),
                                           ready, bank_read[pair[tile]], x_ready[tile])
                    if tile == TILES - 1:
                        used.append(done[tile])
                    beside()
            return done

        def tile_major(blocks, units, x_ready, hooks={}):
            parts = [(b, u, unit()) for b in range(len(blocks)) for u in range(units)]
            done = [[None] * len(blocks) for _ in range(TILES)]
            for tile in range(TILES):
                for i, (b, u, (hi, lo, ready)) in enumerate(parts):
                    if (tile, i) in hooks:
                        hooks[tile, i]()
                    bank, kt0 = blocks[b][0][tile], blocks[b][1]
                    done[tile][b] = issue_all(unit_steps(bank, xt_hi, xt_lo, kt0 + 4 * u, tile, hi, lo, u == 0, u == units - 1),
                                              ready, bank_read[bank], x_ready[tile]() if callable(x_ready[tile]) else x_ready[tile])
                    if tile == TILES - 1:
                        used.append(done[tile][b])
            return done

        def feature_block(pair, *tokens):
            for u in range(2):
                hi, lo, ready = unit()
                for m in range(4):
                    dst = banks[pair[m // 2]][:, (m % 2) * SEQ:(m % 2 + 1) * SEQ]
                    s = []
                    for k in range(4):
                        kt = 4 * u + k
                        cut = slice(m * P, (m + 1) * P)
                        s += product(dst, hi[:, k, cut], lo[:, k, cut], xt_hi[:, kt, :], xt_lo[:, kt, :],
                                     u == 0 and k == 0 and m % 2 == 0, u == 1 and k == 3, skip=True)
                    done = issue_all(s, ready, bank_read[pair[m // 2]], *tokens)
                    if m == 3:
                        used.append(done)
                    if m % 2:
                        beside()
            return done

        def condition(b):
            for u in range(2):
                hi, lo, ready = unit()
                for k in range(4):
                    kt = 4 * u + k
                    s = product(banks[b][:, :], c_hi[:, kt, :], c_lo[:, kt, :], hi[:, k, :], lo[:, k, :],
                                u == 0 and k == 0, u == 1 and k == 3)
                    done = issue_all(s, ready, c_ready, bank_read[b])
                    if k == 3:
                        used.append(done)
                    if k % 2:
                        beside()
            return b, done

        def start_transposes(src_of, kts, k0, tile, dst_hi, dst_lo, pair, *tokens):
            pending = []
            for g in range(0, len(kts), 4):
                group = kts[g:g + 4]
                b = pair[g // 4]
                bank = banks[b]
                turned = issue_all([lambda e, i=i, k=k: e.transpose(bank[:, i * P:(i + 1) * P], src_of(k), ident[:, :])
                                    for i, k in enumerate(group)], bank_read[b], *tokens)
                cut = slice(tile * P, (tile + 1) * P)
                hi = dst_hi[:, k0 + g:k0 + g + len(group), cut]
                lo = dst_lo[:, k0 + g:k0 + g + len(group), cut]
                src = bank[:, 0:len(group) * P].rearrange("p (k t) -> p k t", t=P)
                rounded = act.free(lambda e: e.activation(hi, src, ACT.Copy), turned)
                pending.append((b, lo, src, hi, rounded))
            return pending

        def finish_transposes(pending):
            for b, lo, src, hi, rounded in pending:
                bank_read[b] = dve.free(lambda e: e.tensor_tensor(lo, src, hi.bitcast(F32), ALU.subtract), rounded)
            return bank_read[b]

        def ready_the_root():
            act.then(lambda e: e.activation(root_of_one[:, :], ident[:, 0:1], ACT.Sqrt))

        def rstd_of(dst, src, scale, eps, *tokens):
            t = dve.then(lambda e: e.tensor_scalar(dst, src, scale, eps, ALU.mult, ALU.add), *tokens)
            t = act.then(lambda e: e.activation(dst, dst, ACT.Sqrt), t)
            return dve.then(lambda e: e.reciprocal(dst, dst), t)

        def finish_norm(src, tile, n, gain, shift, params):
            t = dve.then(lambda e: e.bn_aggr(mean_var[:, tile, :], stats[:, tile, 0:n, :].rearrange("p a b -> p (a b)")))
            t = rstd_of(rstd[:, tile:tile + 1], mean_var[:, tile, 1:2], 1.0, LN_EPS, t)
            t = dve.then(lambda e: e.scalar_tensor_tensor(src, src, mean_var[:, tile, 0:1], gain, ALU.subtract, ALU.mult), t, params)
            return dve.then(lambda e: e.scalar_tensor_tensor(src, src, rstd[:, tile:tile + 1], shift, ALU.mult, ALU.add), t)

        def norm_x(tile, pair, params):
            t = dve.then(lambda e: e.bn_aggr(mean_var[:, tile, :], stats[:, tile, :, :].rearrange("p a b -> p (a b)")))
            rstd_of(rstd[:, tile:tile + 1], mean_var[:, tile, 1:2], 1.0, LN_EPS, t)
            pending = []
            for half in range(2):
                cut = slice(half * N, (half + 1) * N)
                part = x[:, tile, cut]
                dve.then(lambda e: e.scalar_tensor_tensor(
                    part, part, mean_var[:, tile, 0:1], ln_p[:, 0, cut], ALU.subtract, ALU.mult), params)
                dve.then(lambda e: e.scalar_tensor_tensor(
                    part, part, rstd[:, tile:tile + 1], ln_p[:, 1, cut], ALU.mult, ALU.add))
                kts = range(half * KT // 2, (half + 1) * KT // 2)
                pending += start_transposes(lambda k: x[:, tile, k * P:(k + 1) * P], kts, kts[0], tile, xt_hi, xt_lo,
                                            (pair[half],), dve.now())
            return pending

        def feed_forward(turns, x_ready):
            def up(j):
                done = tile_major([((0, 1), 0)], 2, x_ready) if j == 0 else [[d] for d in token_block((0, 1))]
                ready = []
                for tile in range(TILES):
                    bank = banks[tile]
                    a, b = bank[:, 0:FF_CHUNK], bank[:, FF_CHUNK:N]
                    s = act.free(lambda e, tile=tile, a=a: e.activation(silu_a[:, tile, :], a, ACT.Silu), done[tile][0])
                    ready.append(dve.free(lambda e, tile=tile, b=b: e.tensor_tensor(
                        hidden[:, tile, :], b, silu_a[:, tile, :], ALU.mult), s))
                    bank_read[tile] = ready[tile]
                return ready

            def turn(ready):
                b = 2
                pe.wait(bank_read[b], ready)
                for k in range(2):
                    for tile in range(TILES):
                        step = lambda e, k=k, tile=tile: e.transpose(
                            banks[b][:, k * SEQ + tile * P:k * SEQ + (tile + 1) * P],
                            hidden[:, tile, k * P:(k + 1) * P], ident[:, :])
                        if k == 1 and tile == 1:
                            turned = pe.free(step)
                        else:
                            pe.quiet(step)
                src = banks[b][:, :].rearrange("p (k t) -> p k t", t=SEQ)
                rounded = act.free(lambda e: e.activation(ht_hi[:, :, :], src, ACT.Copy), turned)
                bank_read[b] = dve.free(lambda e: e.tensor_tensor(
                    ht_lo[:, :, :], src, ht_hi[:, :, :].bitcast(F32), ALU.subtract), rounded)
                return bank_read[b]

            def down(j, ready):
                hi, lo, there = unit()
                pe.wait(there, ready)
                done = [[], []]
                for tile in range(TILES):
                    for half in range(2):
                        bank = 4 + 2 * tile + half
                        s = []
                        for k in range(2):
                            cut = slice(tile * P, (tile + 1) * P)
                            s += product(banks[bank][:, :], ht_hi[:, k, cut], ht_lo[:, k, cut],
                                         hi[:, 2 * k + half, :], lo[:, 2 * k + half, :],
                                         j == 0 and k == 0, j == turns - 1 and k == 1)
                        done[tile].append(issue_all(s, bank_read[bank] if j == 0 else None))
                used.append(done[1][1])
                return done

            turned = None
            for j in range(turns):
                ready = up(j)
                if j:
                    down(j - 1, turned)
                turned = turn(ready)
            return down(turns - 1, turned)

        def add_residual(tile, bank_of, scale, done):
            for half in range(2):
                b = bank_of(tile, half)
                cut = slice(half * N, (half + 1) * N)
                bank_read[b] = dve.then(lambda e: e.scalar_tensor_tensor(
                    x[:, tile, cut], banks[b][:, :], scale, x[:, tile, cut], ALU.mult, ALU.add), done[tile][half])
                dve.then(lambda e: e.bn_stats(stats[:, tile, half, :], x[:, tile, cut]))

        def start_x(tile, pair, src=None):
            src = x if src is None else src
            return start_transposes(lambda k: src[:, tile, k * P:(k + 1) * P], range(KT), 0, tile, xt_hi, xt_lo,
                                    pair, dve.now())

        def scale_x():
            for tile in range(TILES):
                dve.free(lambda e: e.tensor_scalar(x[:, tile, :], x[:, tile, :], ALPHA, None, ALU.mult), pe.now())

        def normalise_and_turn(bank_of, scale, params, done):
            ready_the_root()
            add_residual(0, bank_of, scale, done)
            first = norm_x(0, (0, 1), params)
            add_residual(1, bank_of, scale, done)
            ready = [finish_transposes(first)]
            ready.append(finish_transposes(norm_x(1, (2, 3), params)))
            scale_x()
            return ready

        masks_f = y[:, :, :].rearrange("p a b -> p (a b)")[:, 0:(LOCAL + 1) * P]
        consts_in = load([(cols[:, :], w["cols"]), (causal[:, :], w["causal"]), (masks_f, w["masks"])])
        pe.wait(first_in)
        x_ready = [finish_transposes(start_x(tile, ((0, 1), (2, 3))[tile])) for tile in range(TILES)]
        dve.wait(first_in)
        scale_x()
        dve.wait(consts_in)
        act.wait(consts_in)
        dve.then(lambda e: e.tensor_copy(masks[:, :, :].rearrange("p a b -> p (a b)"), masks_f))

        t = act.then(lambda e: e.activation(tiny[:, 0:KT], col("c", 0, KT), ACT.Silu))
        wide = tiny[:, 0:KT].unsqueeze(2).broadcast_to([P, KT, P])
        t = act.then(lambda e: e.activation(c_hi[:, :, :], wide, ACT.Copy), t)
        c_ready = dve.then(lambda e: e.tensor_tensor(c_lo[:, :, :], wide, c_hi[:, :, :].bitcast(F32), ALU.subtract), t)

        def constants():
            L = lambda i: lb[:, i, :]
            raw_lb = lambda l: col("lb", l * HEADS, HEADS)
            dve.then(lambda e: e.tensor_tensor(L(2), raw_lb(0), raw_lb(1), ALU.max))
            dve.then(lambda e: e.tensor_tensor(L(0), raw_lb(0), L(2), ALU.subtract))
            t = dve.then(lambda e: e.tensor_tensor(L(1), raw_lb(1), L(2), ALU.subtract))
            t = act.then(lambda e: e.activation(lb[:, 0:2, :], lb[:, 0:2, :], ACT.Exp), t)
            yield
            dve.then(lambda e: e.tensor_tensor(L(2), L(0), L(1), ALU.add), t)
            dve.then(lambda e: e.reciprocal(L(2), L(2)))
            dve.then(lambda e: e.tensor_tensor(L(0), L(0), L(2), ALU.mult))
            dve.then(lambda e: e.tensor_tensor(L(1), L(1), L(2), ALU.mult))
            dve.then(lambda e: e.tensor_tensor(L(3), L(0), L(1), ALU.add))
            dve.then(lambda e: e.tensor_tensor(L(4), L(0), L(0), ALU.subtract))
            dve.then(lambda e: e.tensor_tensor(L(5), L(3), L(0), ALU.subtract))
            dve.then(lambda e: e.tensor_scalar(lb[:, 6:8, :], lb[:, 4:6, :], -1.0, 1.0, ALU.mult, ALU.add))

            R = lambda i: decay_c[:, i, :]
            lam = col("lam", 0, DEPTH * BT)
            yield
            t = act.then(lambda e: e.activation(R(1), lam, ACT.Abs))
            t = act.then(lambda e: e.activation(R(1), R(1), ACT.Exp, scale=-1.0), t)
            dve.then(lambda e: e.tensor_scalar(R(2), R(1), 2.0, None, ALU.add), t)
            dve.then(lambda e: e.reciprocal(R(2), R(2)))
            dve.then(lambda e: e.tensor_tensor(R(1), R(1), R(2), ALU.mult))
            dve.then(lambda e: e.tensor_tensor(R(2), R(1), R(1), ALU.mult))
            dve.then(lambda e: e.memset(R(3), 1.0 / 19))
            for n in range(17, 0, -2):
                yield
                dve.then(lambda e: e.tensor_tensor(R(3), R(3), R(2), ALU.mult))
                dve.then(lambda e, n=n: e.tensor_scalar(R(3), R(3), 1.0 / n, None, ALU.add))
            dve.then(lambda e: e.tensor_tensor(R(3), R(3), R(1), ALU.mult))
            dve.then(lambda e: e.tensor_scalar(R(4), lam, -1.0, 0.0, ALU.mult, ALU.max))
            dve.then(lambda e: e.scalar_tensor_tensor(R(0), R(3), 2.0, R(4), ALU.mult, ALU.add))
            dve.then(lambda e: e.tensor_scalar(R(5), R(0), -RG_C, None, ALU.mult))
            dve.then(lambda e: e.tensor_scalar(R(0), R(0), RG_C, None, ALU.mult))

        side.append(constants())

        def level(bc, diff, scale, block, groups, plain_right):
            half = block // 2
            n = groups * SEQ // block
            v = bc.rearrange("p h t -> p (h t)").rearrange("p (n b) -> p n b", b=block)
            d = diff.rearrange("p h t -> p (h t)").rearrange("p (n b) -> p n b", b=block)
            left, right, mid = v[:, :, 0:half], v[:, :, half:], v[:, :, half - 1:half].broadcast_to([P, n, half])
            t = pool.then(lambda e: e.tensor_tensor(d[:, :, 0:half], mid, left, ALU.subtract), dve.now(), act.now())
            if plain_right:
                t = pool.then(lambda e: e.tensor_copy(d[:, :, half:], right))
            else:
                t = pool.then(lambda e: e.tensor_tensor(d[:, :, half:], right, mid, ALU.subtract))
            return d, half, lambda: act.then(lambda e: e.activation(diff, diff, ACT.Exp, scale=scale), t)

        def attend(scores, scores_x, v_of, values_ready):
            for tile in range(TILES):
                s = []
                for h in range(HEADS):
                    cut = slice(h * P, (h + 1) * P)
                    s.append(lambda e, tile=tile, h=h, cut=cut: e.matmul(
                        banks[2 + tile][:, cut], scores[:, tile * HEADS + h, :], v_of(tile)[:, cut],
                        start=True, stop=tile == 0))
                    if tile:
                        s.append(lambda e, h=h, cut=cut: e.matmul(
                            banks[3][:, cut], scores_x[:, h, :], v_of(0)[:, cut], start=False, stop=True))
                done = issue_all(s, bank_read[2 + tile], *values_ready)
            return done

        def head_norm(done, gain_of, gate, dst, params, junk):
            for tile in range(TILES):
                for h in range(HEADS):
                    cut = slice(h * P, (h + 1) * P)
                    t = act.free(lambda e, tile=tile, h=h, cut=cut: e.activation(
                        junk[:, cut], banks[2 + tile][:, cut], ACT.Square,
                        accum_out=sums[:, tile * HEADS + h:tile * HEADS + h + 1]), done, dve.now(), act.now())
                yield
            t = rstd_of(sums[:, :], sums[:, :], 1.0 / P, RMS_EPS, t)
            for tile in range(TILES):
                for h in range(HEADS):
                    i = tile * HEADS + h
                    cut = slice(h * P, (h + 1) * P)
                    t = dve.then(lambda e, tile=tile, cut=cut, i=i, h=h: e.scalar_tensor_tensor(
                        dst[:, tile, cut], banks[2 + tile][:, cut], sums[:, i:i + 1], gain_of(h),
                        ALU.mult, ALU.mult), params)
                bank_read[2 + tile] = t
                t = dve.then(lambda e, tile=tile: e.tensor_tensor(
                    dst[:, tile, :], dst[:, tile, :], gate[:, tile, :], ALU.mult), act.now())
                if tile == 0:
                    yield

        def take_scores(scores, index, bank_tokens):
            for tile in range(TILES):
                mask = masks[:, index:index + 1, :].broadcast_to([P, HEADS, P])
                bank_read[2 + tile] = dve.then(lambda e, tile=tile, mask=mask: e.copy_predicated(
                    scores[:, tile * HEADS:(tile + 1) * HEADS, :], mask,
                    banks[2 + tile][:, :].rearrange("p (h t) -> p h t", t=P)), bank_tokens)

        def score_products(k_of, q_of, ready):
            s = []
            pe.wait(bank_read[2], bank_read[3])
            for tile in range(TILES):
                for h in range(HEADS):
                    cut = slice(tile * P, (tile + 1) * P)
                    s.append(lambda e, tile=tile, h=h, cut=cut: e.matmul(
                        banks[2 + tile][:, h * P:(h + 1) * P], k_of(h)[:, cut], q_of(h)[:, cut],
                        start=True, stop=True))
            return issue_all(s, ready)

        def cross_products(scores_x, k_of, q_of, ready):
            s = [lambda e, h=h: e.matmul(banks[2][:, h * P:(h + 1) * P], k_of(h)[:, 0:P], q_of(h)[:, P:SEQ],
                                         start=True, stop=True) for h in range(HEADS)]
            done = issue_all(s, ready, bank_read[2])
            bank_read[2] = act.then(lambda e: e.activation(
                scores_x[:, :, :], banks[2][:, :].rearrange("p (h t) -> p h t", t=P), ACT.Copy), done)
            return bank_read[2]

        def restart_mask(tile, n, *tokens):
            t = pool.then(lambda e: e.memset(tile[:, 0:n], 1.0), *tokens)
            return pool.then(lambda e: e.memset(tile[:, 0:n].rearrange("p (c t) -> p c t", t=CHUNK)[:, :, 0:1], 0.0), t)

        def all_done():
            return [t for t in (pe.now(), act.now(), dve.now(), pool.now()) if t]

        first = ExitStack()
        with first:
            def sb1(name, shape, dtype=F32):
                return sb(name, shape, dtype, first)

            ln_p = sb1("ln_p", [P, 2, D])
            q_t = sb1("q_t", [P, HEADS, SEQ])
            k_t = sb1("k_t", [P, HEADS, SEQ])
            logf = sb1("logf", [P, HEADS, SEQ])
            logf_2 = hidden2[:, :].rearrange("p (h t) -> p h t", t=SEQ)
            bc = sb1("bc", [P, HEADS, SEQ])
            qe = sb1("qe", [P, HEADS, SEQ])
            ke = sb1("ke", [P, HEADS, SEQ])
            scores = sb1("scores", [P, TILES * HEADS, P])
            values = sb1("values", [P, TILES, HALF])
            gate_g = sb1("gate_g", [P, TILES, HALF])
            u_sg = sb1("u_sg", [P, TILES, HALF])
            v_sg = sb1("v_sg", [P, TILES, HALF])
            sig_b = sb1("sig_b", [P, TILES, D])

            flat = lambda a: a[:, :, :].rearrange("p a b -> p (a b)")
            ln_flat = flat(ln_p)
            hg_gain, sg_gain, sg_shift = (ln_flat[:, i * HALF:(i + 1) * HALF] for i in range(3))

            def load_ln(l, i, *tokens):
                return load([(ln_p[:, 0, :], w["ln_g"][l, i, :].partition_broadcast(P)),
                             (ln_p[:, 1, :], w["ln_b"][l, i, :].partition_broadcast(P))], *tokens)

            def hgrn(l, fed):
                f_pair, f_done = fed["f"]
                for i in range(2):
                    src = banks[f_pair[i]][:, :].rearrange("p (m t) -> p m t", t=SEQ)
                    act.then(lambda e, i=i, src=src: e.activation(logf[:, 2 * i:2 * i + 2, :], src, ACT.Sigmoid), f_done)
                    t = act.then(lambda e, i=i, src=src: e.activation(k_t[:, 2 * i:2 * i + 2, :], src, ACT.Sigmoid, scale=-1.0))
                    bank_read[f_pair[i]] = t
                for h in range(HEADS):
                    less, bound = lb[:, 6 + l, h:h + 1], lb[:, 4 + l, h:h + 1]
                    dve.then(lambda e, h=h, less=less, bound=bound: e.tensor_scalar(
                        logf[:, h, :], logf[:, h, :], less, bound, ALU.mult, ALU.add), t)
                    f_set = dve.then(lambda e, h=h, less=less: e.tensor_scalar(
                        k_t[:, h, :], k_t[:, h, :], less, None, ALU.mult))
                    if h % 2:
                        yield
                t = act.then(lambda e: e.activation(flat(qe), flat(logf), ACT.Ln, scale=2.0 ** LN_SHIFT), f_set)
                yield
                dve.then(lambda e: e.tensor_scalar(flat(ke).bitcast(U32), flat(logf), LN_LOW, None, ALU.is_lt))
                low = dve.then(lambda e: e.tensor_scalar(flat(qe), flat(qe), -LN_SHIFT * float(np.log(2.0)), None, ALU.add), t)
                t = act.then(lambda e: e.activation(flat(logf), flat(logf), ACT.Ln), low)
                yield
                t = dve.then(lambda e: e.copy_predicated(flat(logf), flat(ke).bitcast(U32), flat(qe)), t)
                restart = restart_mask(flat(qe), HEADS * SEQ, t)
                yield
                t = dve.then(lambda e: e.tensor_tensor_scan(flat(bc), flat(qe), flat(logf), 0.0, ALU.mult, ALU.add), restart)
                zeroed = pool.then(lambda e: e.memset(scores[:, :, :], 0.0), pe.now())
                while "q" not in fed:
                    yield
                q_pair, q_done = fed["q"]
                for i in range(2):
                    src = banks[q_pair[i]][:, :].rearrange("p (m t) -> p m t", t=SEQ)
                    bank_read[q_pair[i]] = act.then(lambda e, i=i, src=src: e.activation(
                        q_t[:, 2 * i:2 * i + 2, :], src, ACT.Copy), q_done)
                blocks = LEVELS + [SEQ]
                prepare = lambda index: level(bc[:, :, :], (logf, logf_2)[index % 2][:, :, :], 1.0, blocks[index], HEADS,
                                              blocks[index] >= P)
                d, half, exponential = prepare(1)
                ready = [act.now(), dve.now()]
                yield
                ready = score_products(lambda h: k_t[:, h, :], lambda h: q_t[:, h, :], ready)
                decays = exponential()
                d_next, half_next, exponential = prepare(2)
                yield
                take_scores(scores, 0, [ready, zeroed])
                for index in range(1, len(blocks)):
                    block = blocks[index]
                    view = lambda a: flat(a).rearrange("p (n b) -> p n b", b=block)
                    dve.then(lambda e: e.tensor_tensor(view(qe)[:, :, half:], view(q_t)[:, :, half:], d[:, :, half:], ALU.mult),
                             decays, pe.now())
                    t = dve.then(lambda e: e.tensor_tensor(view(ke)[:, :, 0:half], view(k_t)[:, :, 0:half], d[:, :, 0:half], ALU.mult))
                    d, half = d_next, half_next
                    yield
                    pair = (lambda h: ke[:, h, :], lambda h: qe[:, h, :], t)
                    if block == SEQ:
                        crossed = cross_products(scores_x, *pair)
                    else:
                        ready = score_products(*pair)
                        decays = exponential()
                        if index + 2 < len(blocks):
                            if blocks[index + 2] == SEQ:
                                v = flat(bc).rearrange("p (n c t) -> p n c t", c=2, t=CHUNK)
                                last = v[:, :, 0, CHUNK - 1:CHUNK].broadcast_to([P, HEADS * TILES, CHUNK])
                                pool.then(lambda e: e.tensor_tensor(v[:, :, 1, :], v[:, :, 1, :], last, ALU.add), act.now())
                            d_next, half_next, exponential = prepare(index + 2)
                        yield
                        take_scores(scores, index, [ready, zeroed])
                scored = [crossed, dve.now()]
                while "gate" not in fed:
                    yield
                yield
                done = attend(scores, scores_x, lambda tile: values[:, tile, :], [*scored, fed["values"]])
                yield
                yield from head_norm(done, lambda h: hg_gain[:, h * P:(h + 1) * P], gate_g, fed["o"], fed["params"], flat(ke))

            def token_mixing(l, fed):
                for h in range(HEADS):
                    dve.then(lambda e: e.tensor_tensor(ws[:, h, :], ws[:, h, :], causal[:, :], ALU.mult), fed["params"])
                while "u" not in fed:
                    yield
                for tile in range(TILES):
                    dve.then(lambda e: e.bn_stats(stats[:, tile, 0, :], v_sg[:, tile, :]), fed["v"])
                    dve.then(lambda e: e.bn_aggr(mean_var[:, tile, :], stats[:, tile, 0:1, :].rearrange("p a b -> p (a b)")))
                t = dve.then(lambda e: e.tensor_scalar(rstd[:, :], mean_var[:, :, 1], 1.0, LN_EPS, ALU.mult, ALU.add))
                yield
                root = act.then(lambda e: e.activation(rstd[:, :], rstd[:, :], ACT.Sqrt), t)
                for tile in range(TILES):
                    v = v_sg[:, tile, :]
                    dve.then(lambda e: e.scalar_tensor_tensor(v, v, mean_var[:, tile, 0:1], sg_gain, ALU.subtract, ALU.mult), fed["params"])
                yield
                dve.then(lambda e: e.reciprocal(rstd[:, :], rstd[:, :]), root)
                for tile in range(TILES):
                    v = v_sg[:, tile, :]
                    v_ready = dve.then(lambda e: e.scalar_tensor_tensor(v, v, rstd[:, tile:tile + 1], sg_shift, ALU.mult, ALU.add))
                yield
                s = []
                for tile in range(TILES):
                    for h in range(HEADS):
                        cut = slice(h * P, (h + 1) * P)
                        s.append(lambda e, tile=tile, h=h, cut=cut: e.matmul(
                            banks[4 + tile][:, cut], ws[:, h, :], v_sg[:, tile, cut], start=True, stop=True))
                mixed = issue_all(s, v_ready, bank_read[4], bank_read[5])
                for tile in range(TILES):
                    yield
                    for h in range(HEADS):
                        cut = slice(h * P, (h + 1) * P)
                        bank_read[4 + tile] = dve.then(lambda e: e.scalar_tensor_tensor(
                            u_sg[:, tile, cut], banks[4 + tile][:, cut], col("sg_bs", l * HEADS + h), u_sg[:, tile, cut],
                            ALU.add, ALU.mult), mixed, fed["u"])

            for l in range(DEPTH):
                params = load_ln(l, 0, dve.now())
                done = feed_forward(FF_TURNS, x_ready)
                x_ready = normalise_and_turn(lambda tile, half: 4 + 2 * tile + half, 0.5, params, done)

                params = load([(hg_gain, w["hg_norm_g"][l].partition_broadcast(P)),
                               (sg_gain, w["sg_ln_g"][l].partition_broadcast(P)),
                               (sg_shift, w["sg_ln_b"][l].partition_broadcast(P)),
                               (ws[:, :, :], w["sg_ws_t"][l])], dve.now(), pe.now())
                o = flat(qe).rearrange("p (t n) -> p t n", t=TILES)
                fed = {"o": o, "params": params}
                done = tile_major([((0, 1), 0)], 2, x_ready)
                for tile in range(TILES):
                    bank_read[tile] = act.free(lambda e, tile=tile: e.activation(
                        values[:, tile, :], banks[tile][:, :], ACT.Copy), done[tile][0])
                fed["values"] = act.now()
                fed["f"] = ((4, 5), feature_block((4, 5), x_ready))
                side.extend([hgrn(l, fed), token_mixing(l, fed)])
                fed["q"] = ((6, 7), feature_block((6, 7)))
                done = token_block((4, 5))
                for tile in range(TILES):
                    bank_read[4 + tile] = act.free(lambda e, tile=tile: e.activation(
                        v_sg[:, tile, :], banks[4 + tile][:, :], ACT.Gelu_apprx_tanh), done)
                fed["v"] = act.now()
                done = token_block((6, 7))
                for tile in range(TILES):
                    bank_read[6 + tile] = act.free(lambda e, tile=tile: e.activation(
                        u_sg[:, tile, :], banks[6 + tile][:, :], ACT.Gelu_apprx_tanh), done)
                fed["u"] = act.now()
                done = token_block((0, 1))
                for tile in range(TILES):
                    bank_read[tile] = act.free(lambda e, tile=tile: e.activation(
                        gate_g[:, tile, :], banks[tile][:, :], ACT.Silu), done)
                fed["gate"] = act.now()
                for i, pair in enumerate(((6, 7), (0, 1), (4, 5), (6, 7))):
                    done = token_block(pair)
                    dst = (y, sig_b)[i // 2]
                    for tile in range(TILES):
                        bank_read[pair[tile]] = act.free(lambda e, tile=tile, i=i, dst=dst, pair=pair: e.activation(
                            dst[:, tile, (i % 2) * N:(i % 2 + 1) * N], banks[pair[tile]][:, :], ACT.Sigmoid), done)
                while side:
                    beside()
                sigmoids_in = act.now()
                params = load_ln(l, 1, dve.now())
                ready = []
                for tile in range(TILES):
                    p = start_transposes(lambda k: u_sg[:, tile, k * P:(k + 1) * P], range(BT), BT, tile,
                                         xt_hi, xt_lo, (2 * tile,), dve.now())
                    p += start_transposes(lambda k: o[:, tile, k * P:(k + 1) * P], range(BT), 0, tile,
                                          xt_hi, xt_lo, (2 * tile + 1,), dve.now())
                    ready.append(finish_transposes(p))

                def gated_sum(tile, done, banks_of):
                    for i in range(4):
                        b = banks_of[i]
                        dst = (y, sig_b)[i // 2][:, tile, (i % 2) * N:(i % 2 + 1) * N]
                        bank_read[b] = dve.then(lambda e: e.tensor_tensor(dst, banks[b][:, :], dst, ALU.mult),
                                                done[i], sigmoids_in)
                    dve.then(lambda e: e.tensor_tensor(y[:, tile, :], y[:, tile, :], sig_b[:, tile, :], ALU.add))

                own = ((4, 5, 6, 7), (0, 1, 2, 3))
                done = [[None] * 4, [None] * 4]
                parts = [unit() for _ in range(4)]
                y_ready = [None, None]
                for tile in range(TILES):
                    for i, (hi, lo, there) in enumerate(parts):
                        if tile == 1 and i == 3:
                            p = start_x(0, (4, 5), y)
                            y_ready[0] = finish_transposes(p)
                        b = own[tile][i]
                        done[tile][i] = issue_all(unit_steps(b, xt_hi, xt_lo, (i // 2) * BT, tile, hi, lo, True, True),
                                                  there, bank_read[b], ready[tile])
                        if tile == 1:
                            used.append(done[tile][i])
                        if tile == 0 and i == 3:
                            gated_sum(0, done[0], own[0])
                gated_sum(1, done[1], own[1])

                def turn_y1():
                    y_ready[1] = finish_transposes(start_x(1, (0, 1), y))

                bank_of = lambda tile, half: (6, 2)[tile] + half
                x_ready = [None, None]

                def norm_x0():
                    add_residual(0, bank_of, 1.0, [out_done[0], None])
                    x_ready[0] = finish_transposes(norm_x(0, (4, 5), params))

                parts = [(half, u, unit()) for half in range(2) for u in range(2)]
                ready_the_root()
                out_done = [[None, None], [None, None]]
                for tile in range(TILES):
                    for i, (half, u, (hi, lo, there)) in enumerate(parts):
                        if i == 3:
                            (turn_y1, norm_x0)[tile]()
                        b = bank_of(tile, half)
                        out_done[tile][half] = issue_all(
                            unit_steps(b, xt_hi, xt_lo, 4 * u, tile, hi, lo, u == 0, u == 1),
                            there, bank_read[b], y_ready[tile])
                        if tile == 1:
                            used.append(out_done[tile][half])
                add_residual(1, bank_of, 1.0, out_done)
                x_ready[1] = finish_transposes(norm_x(1, (0, 1), params))
                scale_x()
                params = load_ln(l, 2, dve.now())

                norm = lambda tile: finish_norm(x[:, tile, :], tile, 2, ln_p[:, 0, :], ln_p[:, 1, :], params)
                done = feed_forward(FF_TURNS, x_ready)
                if l < DEPTH - 1:
                    x_ready = normalise_and_turn(lambda tile, half: 4 + 2 * tile + half, 0.5, params, done)
                    continue
                early = []
                for tile in range(TILES):
                    early.append(condition(tile))
                    add_residual(tile, lambda tile, half: 4 + 2 * tile + half, 0.5, done)
                    norm(tile)
                early.append(condition(2))

        second = ctx.enter_context(ExitStack())

        def sb2(name, shape, dtype=F32):
            return sb(name, shape, dtype, second)

        norm_g = sb2("norm_g", [P, D])
        sh = sb2("sh", [P, D])
        sc = sb2("sc", [P, D])
        gt = [sb2(f"gt_{n}", [P, D]) for n in ("mix", "ffn")]
        router_hi = sb2("router_hi", [P, KT, EXPERTS], F32R)
        router_lo = sb2("router_lo", [P, KT, EXPERTS], F32R)
        mixer_memory = ctx.enter_context(ExitStack())

        def sbm(name, shape, dtype=F32):
            return sb(name, shape, dtype, mixer_memory)

        g_norm = sbm("g_norm", [P, P])
        wg2 = sbm("wg2", [GLA_RANK, GLA_KD])
        block_w = sbm("block_w", [P, 2 * BT, P])
        x_pad = sbm("x_pad", [P, BT, SEQ + CONV_W - 1])
        u_rg = sbm("u_rg", [P, BT, SEQ])
        r_rg = sbm("r_rg", [P, BT, SEQ])
        th_rg = sbm("th_rg", [P, BT, SEQ])
        i_rg = sbm("i_rg", [P, BT, SEQ])
        q_g = sbm("q_g", [P, 2, SEQ])
        k_g = sbm("k_g", [P, 2, SEQ])
        lf_g = sbm("lf_g", [P, 2, SEQ])
        bc_g = sbm("bc_g", [P, 2, SEQ])
        ke_g = sbm("ke_g", [P, 2, SEQ])
        scores = sbm("scores_2", [P, TILES * HEADS, P])
        scores_x_2 = flat(x_pad)[:, 0:HEADS * P].rearrange("p (h t) -> p h t", t=P)
        qe_g = hidden2[:, :].rearrange("p (h t) -> p h t", t=SEQ)
        values = flat(y)[:, 0:TILES * HALF].rearrange("p (t n) -> p t n", t=TILES)
        gate_g = flat(y)[:, TILES * HALF:].rearrange("p (t n) -> p t n", t=TILES)

        over = all_done() + [(s, n) for s, n in zip(group_loaded, group_count) if n]
        for q in (act, dve, pool):
            q.wait(*over)

        router = col("router", 0, KT * EXPERTS).rearrange("p (k e) -> p k e", e=EXPERTS)
        t = act.then(lambda e: e.activation(router_hi[:, :, :], router, ACT.Copy))
        router_ready = dve.then(lambda e: e.tensor_tensor(router_lo[:, :, :], router, router_hi[:, :, :].bitcast(F32), ALU.subtract), t)

        def load_bias(l, indices, targets, *tokens):
            return load([(target[:, :], w["ada_b"][l, i * D:(i + 1) * D].partition_broadcast(P))
                         for i, target in zip(indices, targets)], *tokens)

        def add_bias(target, half, made, bias):
            b, done = made
            dst = target[:, half * N:(half + 1) * N]
            bank_read[b] = dve.then(lambda e: e.tensor_tensor(dst, banks[b][:, :], dst, ALU.add), done, bias)

        def gain_of_scale(params):
            dve.then(lambda e: e.scalar_tensor_tensor(sc[:, :], sc[:, :], 1.0, norm_g[:, :], ALU.add, ALU.mult), params)

        def rms_rstd(tile, *tokens):
            mine = rstd[:, tile:tile + 1]
            t = act.then(lambda e: e.activation(y[:, tile, :], x[:, tile, :], ACT.Square, accum_out=mine),
                         dve.now(), *tokens)
            return rstd_of(mine, mine, 1.0 / D, RMS_EPS, t)

        def modulated(tile):
            dve.then(lambda e: e.scalar_tensor_tensor(
                y[:, tile, :], x[:, tile, :], rstd[:, tile:tile + 1], sc[:, :], ALU.mult, ALU.mult))
            return dve.then(lambda e: e.tensor_tensor(y[:, tile, :], y[:, tile, :], sh[:, :], ALU.add))

        def add_gated(part, tile, bank_of, done):
            for half in range(2):
                b = bank_of(tile, half)
                cut = slice(half * N, (half + 1) * N)
                bank_read[b] = dve.then(lambda e: e.tensor_tensor(
                    y[:, tile, cut], banks[b][:, :], gt[part][:, cut], ALU.mult), done[half])
            dve.then(lambda e: e.tensor_tensor(x[:, tile, :], x[:, tile, :], y[:, tile, :], ALU.add))

        def expert_stage():
            def sbe(name, shape, dtype=F32):
                return sb(name, shape, dtype, second)

            h_hi, h_lo = sbe("h_hi", [P, TILES, D], F32R), sbe("h_lo", [P, TILES, D], F32R)
            slots_hi = (xt_hi, sbe("xe_hi", [P, KT, SEQ], F32R))
            slots_lo = (xt_lo, sbe("xe_lo", [P, KT, SEQ], F32R))
            to_slot = sbe("to_slot", [P, TILES, SEQ], F32R)
            from_slot = sbe("from_slot", [P, TILES, SEQ])
            slot_iota = sbe("slot_iota", [P, SEQ])
            before, ones = sbe("before", [P, P]), sbe("ones", [P, P])
            chosen = sbe("chosen", [P, TILES, EXPERTS])
            rank = sbe("rank", [P, TILES + 1, EXPERTS])
            counts = sbe("counts", [P, EXPERTS], I32)
            total = (sh, sc)
            slot_out = y

            def count_and_rank():
                dve.then(lambda e: e.tensor_tensor(before[:, :], causal[:, :], ident[:, :], ALU.subtract))
                t = dve.then(lambda e: e.memset(ones[:, :], 1.0))
                sums_of = (((before, 0),), ((ones, 0), (before, 1)), ((ones, 0), (ones, 1)))
                s = []
                for i, parts in enumerate(sums_of):
                    for n, (m, tile) in enumerate(parts):
                        s.append(lambda e, i=i, n=n, m=m, tile=tile, last=n == len(parts) - 1: e.matmul(
                            banks[3][:, i * EXPERTS:(i + 1) * EXPERTS], m[:, :], chosen[:, tile, :],
                            start=n == 0, stop=last))
                done = issue_all(s, t, bank_read[3])
                bank_read[3] = dve.then(lambda e: e.tensor_copy(
                    rank[:, :, :].rearrange("p a b -> p (a b)"), banks[3][:, 0:(TILES + 1) * EXPERTS]), done)
                return dve.then(lambda e: e.tensor_copy(counts[:, :], rank[:, TILES, :]))

            def build_to_slot(x_of, *tokens):
                for tile in range(TILES):
                    t = dve.then(lambda e, tile=tile: e.tensor_scalar(
                        to_slot[:, tile, :], slot_iota[:, :], rank[:, tile, x_of:x_of + 1],
                        chosen[:, tile, x_of:x_of + 1], ALU.is_equal, ALU.mult), *tokens)
                return t

            def gather(x_of, r, ready, b=3):
                hi_to, lo_to = slots_hi[x_of % 2], slots_lo[x_of % 2]
                s = []
                for k in range(2):
                    cut = slice((2 * r + k) * P, (2 * r + k + 1) * P)
                    parts = [(part, tile) for tile in range(TILES) for part in (h_hi, h_lo)]
                    for n, (part, tile) in enumerate(parts):
                        s.append(lambda e, k=k, cut=cut, n=n, part=part, tile=tile: e.matmul(
                            banks[b][:, k * SEQ:(k + 1) * SEQ], part[:, tile, cut], to_slot[:, tile, :],
                            start=n == 0, stop=n == 2 * TILES - 1))
                done = issue_all(s, ready, bank_read[b])
                src = banks[b][:, :].rearrange("p (k t) -> p k t", t=SEQ)
                hi, lo = hi_to[:, 2 * r:2 * r + 2, :], lo_to[:, 2 * r:2 * r + 2, :]
                t = act.free(lambda e: e.activation(hi, src, ACT.Copy), done)
                bank_read[b] = dve.free(lambda e: e.tensor_tensor(lo, src, hi.bitcast(F32), ALU.subtract), t)
                return bank_read[b]

            def turn_from_slot():
                pe.wait(bank_read[3])
                for st in range(TILES):
                    for tile in range(TILES):
                        step = lambda e, st=st, tile=tile: e.transpose(
                            banks[3][:, st * SEQ + tile * P:st * SEQ + (tile + 1) * P],
                            to_slot[:, tile, st * P:(st + 1) * P].bitcast(F32), ident[:, :])
                        if st == 1 and tile == 1:
                            done = pe.free(step)
                        else:
                            pe.quiet(step)
                bank_read[3] = act.free(lambda e: e.activation(
                    from_slot[:, :, :], banks[3][:, :].rearrange("p (s t) -> p s t", t=SEQ), ACT.Copy), done)
                return done, bank_read[3]

            def two_tiles(steps_of, *tokens):
                pe.wait(*tokens)
                for s in steps_of(1):
                    pe.second_only(s)
                steps = list(steps_of(0))
                for s in steps[:-1]:
                    pe.quiet(s)
                return pe.free(steps[-1])

            def up(x_of, x_ready):
                hi_x, lo_x = slots_hi[x_of % 2], slots_lo[x_of % 2]
                for u in range(2):
                    hi, lo, ready = unit()

                    def steps_of(tile):
                        cut = slice(tile * P, (tile + 1) * P)
                        for k in range(4):
                            yield from product(banks[tile][:, :], hi_x[:, 4 * u + k, cut], lo_x[:, 4 * u + k, cut],
                                               hi[:, k, :], lo[:, k, :], u == 0 and k == 0, u == 1 and k == 3)
                    done = two_tiles(steps_of, ready, x_ready, bank_read[0], bank_read[1])
                    used.append(done)
                for tile in range(TILES):
                    a, b = banks[tile][:, 0:FF_CHUNK], banks[tile][:, FF_CHUNK:N]
                    t = act.free(lambda e: e.activation(silu_a[:, tile, :], a, ACT.Silu), done)
                    bank_read[tile] = dve.free(lambda e: e.tensor_tensor(
                        hidden[:, tile, :], b, silu_a[:, tile, :], ALU.mult), t)
                return bank_read[1]

            def turn(ready):
                pe.wait(bank_read[2], ready)
                for k in range(2):
                    for tile in range(TILES):
                        step = lambda e, k=k, tile=tile: e.transpose(
                            banks[2][:, k * SEQ + tile * P:k * SEQ + (tile + 1) * P],
                            hidden[:, tile, k * P:(k + 1) * P], ident[:, :])
                        if k == 1 and tile == 1:
                            done = pe.free(step)
                        else:
                            pe.quiet(step)
                src = banks[2][:, :].rearrange("p (k t) -> p k t", t=SEQ)
                t = act.free(lambda e: e.activation(ht_hi[:, :, :], src, ACT.Copy), done)
                bank_read[2] = dve.free(lambda e: e.tensor_tensor(
                    ht_lo[:, :, :], src, ht_hi[:, :, :].bitcast(F32), ALU.subtract), t)
                return bank_read[2]

            def down(j, ready):
                hi, lo, there = unit()

                def steps_of(tile):
                    cut = slice(tile * P, (tile + 1) * P)
                    for half in range(2):
                        for k in range(2):
                            yield from product(banks[4 + 2 * tile + half][:, :], ht_hi[:, k, cut], ht_lo[:, k, cut],
                                               hi[:, 2 * k + half, :], lo[:, 2 * k + half, :],
                                               j == 0 and k == 0, j == FF_TURNS - 1 and k == 1)
                done = two_tiles(steps_of, there, ready, *(bank_read[4:8] if j == 0 else ()))
                used.append(done)
                return done

            def scatter(x_of, ready):
                pe.wait(ready, *bank_read[4:8])
                for tile in range(TILES):
                    cut = slice(tile * P, (tile + 1) * P)
                    for half in range(2):
                        wide = slice(half * N, (half + 1) * N)
                        bank = banks[4 + 2 * tile + half]
                        pe.second_only(lambda e, bank=bank, cut=cut, wide=wide: e.matmul(
                            bank[:, :], from_slot[:, 1, cut], slot_out[:, 1, wide], start=True, stop=False))
                        done = pe.free(lambda e, bank=bank, cut=cut, wide=wide: e.matmul(
                            bank[:, :], from_slot[:, 0, cut], slot_out[:, 0, wide], start=not pe.second, stop=True))
                        gate = gates[:, tile, x_of:x_of + 1]
                        dst = total[tile][:, wide]
                        if x_of == 0:
                            t = dve.free(lambda e: e.tensor_scalar(dst, bank[:, :], gate, None, ALU.mult), done)
                        else:
                            t = dve.free(lambda e: e.scalar_tensor_tensor(dst, bank[:, :], gate, dst, ALU.mult, ALU.add), done)
                        bank_read[4 + 2 * tile + half] = t

            def has_second(x_of):
                return nc.tensor.value_load(counts[0:1, x_of:x_of + 1]) > P

            def run(x_ready, meanwhile):
                loaded = load([(slot_iota[:, :], w["slots"])], *all_done())
                split_h = []
                for tile in range(TILES):
                    t = act.free(lambda e, tile=tile: e.activation(h_hi[:, tile, :], y[:, tile, :], ACT.Copy), x_ready)
                    split_h.append(dve.free(lambda e, tile=tile: e.tensor_tensor(
                        h_lo[:, tile, :], y[:, tile, :], h_hi[:, tile, :].bitcast(F32), ALU.subtract), t))
                counted = count_and_rank()
                t = build_to_slot(0, loaded)
                for r, b in enumerate((4, 5, 6, 7)):
                    gathered = gather(0, r, [t, *split_h], b)
                meanwhile()
                pe.wait(counted)
                out_ready = split_h
                returned = None
                for x_of in range(EXPERTS):
                    branch = has_second(x_of)
                    pe.record()
                    hidden_in = up(x_of, gathered)
                    pe.play_if(branch)
                    if x_of:
                        branch = has_second(x_of - 1)
                        pe.record()
                        scatter(x_of - 1, [out_ready, returned])
                        pe.play_if(branch)
                    branch = has_second(x_of)
                    pe.record()
                    for j in range(FF_TURNS):
                        if j:
                            hidden_in = up(x_of, gathered)
                            down(j - 1, turned)
                        turned = turn(hidden_in)
                        if j == 1:
                            slot_used, returned = turn_from_slot()
                        if x_of < EXPERTS - 1:
                            if j == 3:
                                t = build_to_slot(x_of + 1, slot_used)
                            if j in (5, 6, 7, FF_TURNS - 1):
                                next_in = gather(x_of + 1, min(j - 5, 3), t)
                    done = down(FF_TURNS - 1, turned)
                    pe.play_if(branch)
                    for tile in range(TILES):
                        for half in range(2):
                            b = 4 + 2 * tile + half
                            bank_read[b] = act.free(lambda e, tile=tile, half=half, b=b: e.activation(
                                slot_out[:, tile, half * N:(half + 1) * N], banks[b][:, :], ACT.Copy), done, out_ready)
                    out_ready = act.now()
                    if x_of < EXPERTS - 1:
                        gathered = next_in
                branch = has_second(EXPERTS - 1)
                pe.record()
                scatter(EXPERTS - 1, [out_ready, returned])
                pe.play_if(branch)

            run.chosen = chosen
            return run

        head_rows = lambda h: slice((h % 2) * GLA_DK, (h % 2 + 1) * GLA_DK)

        def log_decay(l, low_in, params, free):
            s = [lambda e, m=m: e.matmul(banks[2][:, m * SEQ:(m + 1) * SEQ], wg2[:, m * P:(m + 1) * P],
                                         ke_g[0:GLA_RANK, 0, :], start=True, stop=True) for m in range(2)]
            done = issue_all(s, low_in, params, bank_read[2])
            for m in range(2):
                bank_read[2] = dve.then(lambda e: e.tensor_scalar(
                    lf_g[:, m, :], banks[2][:, m * SEQ:(m + 1) * SEQ], col("gla_bg", l * 2 + m), None, ALU.add), done, free)
            yield
            act.then(lambda e: e.activation(flat(bc_g), flat(lf_g), ACT.Abs), dve.now())
            t = act.then(lambda e: e.activation(flat(bc_g), flat(bc_g), ACT.Exp, scale=-1.0))
            yield
            t = dve.then(lambda e: e.tensor_scalar(flat(bc_g), flat(bc_g), 1.0, None, ALU.add), t)
            yield
            t = act.then(lambda e: e.activation(flat(bc_g), flat(bc_g), ACT.Ln), t)
            yield
            t = dve.then(lambda e: e.scalar_tensor_tensor(flat(lf_g), flat(lf_g), 0.0, flat(bc_g), ALU.min, ALU.subtract), t)
            restart = restart_mask(flat(ke_g), 2 * SEQ, t, pe.now())
            yield
            dve.then(lambda e: e.tensor_tensor_scan(flat(bc_g), flat(ke_g), flat(lf_g), 0.0, ALU.mult, ALU.add), restart)

        def multiplier(l, gates_in):
            for f in range(BT):
                act.then(lambda e: e.activation(th_rg[:, f, :], r_rg[:, f, :], ACT.Tanh, scale=decay_c[:, 0, l * BT + f:l * BT + f + 1]))
            for f in range(BT):
                t = act.then(lambda e: e.activation(r_rg[:, f, :], r_rg[:, f, :], ACT.Exp, scale=decay_c[:, 5, l * BT + f:l * BT + f + 1]))
            yield
            spare = flat(x_pad)[:, 0:BT * SEQ]
            dve.then(lambda e: e.tensor_scalar(spare, flat(th_rg), 1.0, None, ALU.add), t)
            for i in range(4):
                part = spare[:, i * SEQ:(i + 1) * SEQ]
                dve.then(lambda e: e.reciprocal(part, part))
                if i % 2:
                    yield
            t = dve.then(lambda e: e.scalar_tensor_tensor(flat(th_rg), flat(th_rg), 2.0, spare, ALU.mult, ALU.mult))
            dve.then(lambda e: e.tensor_tensor(flat(i_rg), flat(i_rg), flat(u_rg), ALU.mult), gates_in)
            yield
            t = act.then(lambda e: e.activation(flat(th_rg), flat(th_rg), ACT.Sqrt), t)
            yield
            dve.then(lambda e: e.memset(th_rg[:, :, 0:1], 1.0), t)
            dve.then(lambda e: e.memset(r_rg[:, :, 0:1], 0.0))
            dve.then(lambda e: e.tensor_tensor(flat(i_rg), flat(i_rg), flat(th_rg), ALU.mult))

        def recurrence(l, fed):
            free, params = fed["free"], fed["params"]
            padded = pool.then(lambda e: e.memset(x_pad[:, :, 0:CONV_W - 1], 0.0), *free)
            pair, done = fed["rg_x"]
            for i in range(2):
                src = banks[pair[i]][:, :].rearrange("p (m t) -> p m t", t=SEQ)
                t = bank_read[pair[i]] = act.then(lambda e: e.activation(
                    x_pad[:, 2 * i:2 * i + 2, CONV_W - 1:], src, ACT.Copy), done, free, padded)
            for f in range(BT):
                tap = lambda n: (x_pad[:, f, n:n + SEQ], col("conv_w", (l * CONV_W + n) * BT + f))
                dve.then(lambda e: e.tensor_scalar(
                    u_rg[:, f, :], tap(0)[0], tap(0)[1], col("conv_b", l * BT + f), ALU.mult, ALU.add), t)
                for n in range(1, CONV_W):
                    dve.then(lambda e: e.scalar_tensor_tensor(
                        u_rg[:, f, :], tap(n)[0], tap(n)[1], u_rg[:, f, :], ALU.mult, ALU.add))
                if f < BT - 1:
                    yield
            u_ready = dve.now()
            yield

            for g, (dst, bias) in enumerate(((r_rg, "rg_ba"), (i_rg, "rg_bx"))):
                s = [lambda e, f=f: e.matmul(banks[2 + f // 2][:, (f % 2) * SEQ:(f % 2 + 1) * SEQ],
                                             block_w[:, g * BT + f, :], u_rg[:, f, :], start=True, stop=True)
                     for f in range(BT)]
                done = issue_all(s, u_ready, params, bank_read[2], bank_read[3])
                for f in range(BT):
                    bank_read[2 + f // 2] = act.then(lambda e: e.activation(
                        dst[:, f, :], banks[2 + f // 2][:, (f % 2) * SEQ:(f % 2 + 1) * SEQ], ACT.Sigmoid,
                        bias=col(bias, l * BT + f)), done)
                yield
            gates_in = act.now()
            yield from multiplier(l, gates_in)
            fed["spare_free"] = dve.now()
            yield
            h_ready = fed["h"] = dve.then(lambda e: e.tensor_tensor_scan(flat(u_rg), flat(r_rg), flat(i_rg), 0.0, ALU.mult, ALU.add))
            while "rg_gate" not in fed:
                yield
            pair, done = fed["rg_gate"]
            for i in range(2):
                src = banks[pair[i]][:, :].rearrange("p (m t) -> p m t", t=SEQ)
                t = bank_read[pair[i]] = act.then(lambda e: e.activation(
                    th_rg[:, 2 * i:2 * i + 2, :], src, ACT.Gelu_apprx_tanh), done, h_ready)
            yield
            t = dve.then(lambda e: e.tensor_tensor(flat(u_rg), flat(u_rg), flat(th_rg), ALU.mult), t)
            while "g" not in fed:
                yield
            t = act.then(lambda e: e.activation(xt_hi[:, 0:BT, :], u_rg[:, :, :], ACT.Copy), fed["g"][0], t)
            dve.then(lambda e: e.tensor_tensor(xt_lo[:, 0:BT, :], u_rg[:, :, :], xt_hi[:, 0:BT, :].bitcast(F32), ALU.subtract), t)

        def attention(l, fed):
            free, params = fed["free"], fed["params"]
            pool.then(lambda e: e.memset(qe_g, 0.0), *free)
            zeroed = pool.then(lambda e: e.memset(scores[:, :, :], 0.0))
            yield from log_decay(l, fed["low"], params, free)
            while "qk" not in fed:
                yield
            pair, done = fed["qk"]
            for i, dst in enumerate((q_g, k_g)):
                src = banks[pair[i]][:, :].rearrange("p (m t) -> p m t", t=SEQ)
                bank_read[pair[i]] = act.then(lambda e: e.activation(
                    dst[:, :, :], src, ACT.Copy, scale=(GLA_DK ** -0.5, 1.0)[i]), done)
            yield

            mid = flat(bc_g).rearrange("p (n b) -> p n b", b=CHUNK)[:, :, CHUNK // 2 - 1:CHUNK // 2].broadcast_to([P, 2 * SEQ // CHUNK, CHUNK])
            chunks = lambda a: flat(a).rearrange("p (n b) -> p n b", b=CHUNK)
            centred = dve.then(lambda e: e.tensor_tensor(chunks(lf_g), chunks(bc_g), mid, ALU.subtract))
            yield
            decays = act.then(lambda e: e.activation(flat(ke_g), flat(lf_g), ACT.Exp, scale=1.0 / GLA_TAU), centred)
            yield
            for h in range(2):
                rows = head_rows(h)
                t = dve.then(lambda e: e.tensor_tensor(
                    qe_g[rows, h::2, :], q_g[rows, :, :], ke_g[rows, :, :], ALU.mult), decays, zeroed)
            yield
            t = act.then(lambda e: e.activation(flat(ke_g), flat(lf_g), ACT.Exp, scale=-1.0 / GLA_TAU), t)
            yield
            t = dve.then(lambda e: e.tensor_tensor(flat(ke_g), flat(ke_g), flat(k_g), ALU.mult), t)
            prepare = lambda block: level(bc_g[:, :, :], lf_g[:, :, :], 1.0 / GLA_TAU, block, 2, True)
            d, half, exponential = prepare(P)
            k_of, q_of = (lambda h: ke_g[:, h // 2, :]), (lambda h: qe_g[:, h, :])
            yield
            scored = score_products(k_of, q_of, t)
            decays = exponential()
            yield
            take_scores(scores, LOCAL, [scored, zeroed])

            for block in (P, SEQ):
                for h in range(2):
                    rows = head_rows(h)
                    qv = qe_g[rows, h::2, :].rearrange("p h (n b) -> p h n b", b=block)[:, :, :, half:]
                    src = q_g[rows, :, :].rearrange("p h (n b) -> p h n b", b=block)[:, :, :, half:]
                    dv = lf_g[rows, :, :].rearrange("p h (n b) -> p h n b", b=block)[:, :, :, half:]
                    dve.then(lambda e: e.tensor_tensor(qv, src, dv, ALU.mult), decays, pe.now())
                view = lambda a: flat(a).rearrange("p (n b) -> p n b", b=block)
                t = dve.then(lambda e: e.tensor_tensor(view(ke_g)[:, :, 0:half], view(k_g)[:, :, 0:half], d[:, :, 0:half], ALU.mult))
                if block == P:
                    v = flat(bc_g).rearrange("p (n c t) -> p n c t", c=2, t=CHUNK)
                    last = v[:, :, 0, CHUNK - 1:CHUNK].broadcast_to([P, 2 * TILES, CHUNK])
                    dve.then(lambda e: e.tensor_tensor(v[:, :, 1, :], v[:, :, 1, :], last, ALU.add))
                    d, half, exponential = prepare(SEQ)
                    yield
                    scored = score_products(k_of, q_of, t)
                    decays = exponential()
                    yield
                    take_scores(scores, LEVELS.index(P), scored)
                else:
                    while "spare_free" not in fed:
                        yield
                    act.wait(fed["spare_free"])
                    yield
                    crossed = cross_products(scores_x_2, k_of, q_of, t)
            scored = [crossed, dve.now()]
            while "g" not in fed:
                yield
            done = attend(scores, scores_x_2, lambda tile: values[:, tile, :], [*scored, fed["values"]])
            yield
            while "h" not in fed:
                yield
            yield from head_norm(done, lambda h: g_norm[:, :], gate_g, fed["o"], params, flat(i_rg))

        x_tile_bank = lambda tile, half: 4 + 2 * tile + half
        gain_in = load([(norm_g[:, :], w["norm_mix_g"][0].partition_broadcast(P))])
        bias = load_bias(0, (0, 1, 2), (sh, sc, gt[0]))
        early.append(condition(3))
        for tile in range(TILES):
            rms_rstd(tile)
        for l in range(DEPTH):
            for i, target in enumerate((sh, sc, gt[0])):
                for half in range(2):
                    add_bias(target, half, early.pop(0) if early else condition(2 * (i % 2) + half), bias)
                if i == 1:
                    gain_of_scale(gain_in)
                    turns = [modulated(tile) for tile in range(TILES)]
            started = [start_transposes(lambda k: y[:, tile, k * P:(k + 1) * P], range(KT), 0, tile, xt_hi, xt_lo,
                                        ((4, 5), (6, 7))[tile], turns[tile]) for tile in range(TILES)]
            x_ready = [finish_transposes(p) for p in started]
            free = all_done()
            params = load([(g_norm[:, :], w["gla_norm_g"][l].partition_broadcast(P)),
                           (wg2[:, :], w["gla_wg2"][l]), (block_w[:, :, :], w["rg_w"][l])], *free)
            gain_in = load([(norm_g[:, :], w["norm_ffn_g"][l].partition_broadcast(P))], *free)
            bias = load_bias(l, (3, 4, 5), (sh, sc, gt[1]), *free)

            o = flat(r_rg).rearrange("p (t n) -> p t n", t=TILES)
            fed = {"free": free, "params": params, "o": o}
            hi, lo, ready = unit()
            s = []
            tail = lambda a: a.rearrange("p k n -> p (k n)")[:, 0:KT * P].rearrange("p (k n) -> p k n", n=P)
            for k in range(KT):
                s += product(banks[0][:, 0:SEQ], tail(hi)[:, k, :], tail(lo)[:, k, :], xt_hi[:, k, :], xt_lo[:, k, :],
                             k == 0, k == KT - 1)
            done = issue_all(s, ready, bank_read[0], x_ready)
            used.append(done)
            fed["low"] = bank_read[0] = act.then(lambda e: e.activation(
                ke_g[0:GLA_RANK, 0, :], banks[0][0:GLA_RANK, 0:SEQ], ACT.Copy), done, free)
            side.append(attention(l, fed))
            fed["rg_x"] = ((4, 5), feature_block((4, 5)))
            side.append(recurrence(l, fed))
            fed["qk"] = ((6, 7), feature_block((6, 7)))
            done = token_block((4, 5))
            for tile in range(TILES):
                bank_read[4 + tile] = act.free(lambda e: e.activation(
                    values[:, tile, :], banks[4 + tile][:, :], ACT.Copy), done)
            fed["values"] = act.now()
            fed["rg_gate"] = ((6, 7), feature_block((6, 7)))
            done = token_block((0, 1))
            for tile in range(TILES):
                bank_read[tile] = act.free(lambda e: e.activation(
                    gate_g[:, tile, :], banks[tile][:, :], ACT.Silu), done)
            fed["g"] = done
            for i, target in enumerate((sh, sc)):
                for half in range(2):
                    add_bias(target, half, condition((4, 0)[i] + half), bias)
            gain_of_scale(gain_in)
            while side:
                beside()
            started = [start_transposes(lambda k: o[:, tile, k * P:(k + 1) * P], range(BT), BT, tile, xt_hi, xt_lo,
                                        (2 + tile,), dve.now()) for tile in range(TILES)]
            y_ready = [finish_transposes(p) for p in started]

            def close_tile(tile, done):
                add_gated(0, tile, x_tile_bank, done)
                rms_rstd(tile)
                return modulated(tile)

            parts = [(half, u, unit()) for half in range(2) for u in range(2)]
            ready_the_root()
            done, turns = [[None, None], [None, None]], [None, None]
            for tile in range(TILES):
                for half, u, (hi, lo, there) in parts:
                    b = x_tile_bank(tile, half)
                    done[tile][half] = issue_all(unit_steps(b, xt_hi, xt_lo, 4 * u, tile, hi, lo, u == 0, u == 1),
                                                 there, bank_read[b], y_ready[tile])
                    if tile == TILES - 1:
                        used.append(done[tile][half])
                        split_ahead()
                turns[tile] = close_tile(tile, done[tile])
            mixed = l % 2 == 1
            started = [None, None]
            gates_of = []
            for tile in range(TILES):
                if tile == 0 or not mixed:
                    gates_of.append(condition(tile))
                started[tile] = start_transposes(lambda k: y[:, tile, k * P:(k + 1) * P], range(KT), 0, tile, xt_hi, xt_lo,
                                                 ((2, 3), (4, 5))[tile], turns[tile])
            x_ready = [finish_transposes(p) for p in started]
            if not mixed:
                for half, g in enumerate(gates_of):
                    add_bias(gt[1], half, g, bias)
            if l + 1 < DEPTH:
                next_bias = load_bias(l + 1, (0, 1, 2), (sh, sc, gt[0]), dve.now())
                gain_in = load([(norm_g[:, :], w["norm_mix_g"][l + 1].partition_broadcast(P))], dve.now())
            else:
                gain_in = load([(norm_g[:, :], w["final_g"].partition_broadcast(P))], dve.now())

            if not mixed:
                done = feed_forward(FF_TURNS, x_ready)
                ready_the_root()
                for tile in range(TILES):
                    add_gated(1, tile, x_tile_bank, done[tile])
                for tile in range(TILES):
                    rms_rstd(tile)
                bias = next_bias
            else:
                mixer_memory.close()
                experts = expert_stage()
                chosen = experts.chosen
                for tile in range(TILES):
                    s = []
                    for k in range(KT):
                        cut = slice(tile * P, (tile + 1) * P)
                        s += product(banks[6 + tile][:, 0:EXPERTS], xt_hi[:, k, cut], xt_lo[:, k, cut],
                                     router_hi[:, k, :], router_lo[:, k, :], k == 0, k == KT - 1)
                    logits_in = issue_all(s, x_ready[tile], router_ready, bank_read[6 + tile])
                    logits, top = tiny[:, 0:8], tiny[:, 8:16]
                    where, where_f = tiny[:, 16:24].bitcast(U32), tiny[:, 24:32]
                    e2, p1, p2, g2 = tiny[:, 32:33], tiny[:, 33:34], tiny[:, 34:35], tiny[:, 40:48]
                    bank_read[6 + tile] = dve.then(lambda e, tile=tile: e.tensor_copy(logits, banks[6 + tile][:, 0:EXPERTS]), logits_in)
                    dve.then(lambda e: e.max(top, logits))
                    dve.then(lambda e: e.max_index(where, top, logits))
                    dve.then(lambda e: e.tensor_copy(where_f, where))
                    t = dve.then(lambda e: e.tensor_tensor(e2, top[:, 1:2], top[:, 0:1], ALU.subtract))
                    t = act.then(lambda e: e.activation(e2, e2, ACT.Exp), t)
                    dve.then(lambda e: e.tensor_scalar(p1, e2, 1.0, None, ALU.add), t)
                    dve.then(lambda e: e.reciprocal(p1, p1))
                    dve.then(lambda e: e.tensor_tensor(p2, p1, e2, ALU.mult))
                    iota = col("iota", 0, EXPERTS)
                    dve.then(lambda e, tile=tile: e.tensor_scalar(gates[:, tile, :], iota, where_f[:, 0:1], p1, ALU.is_equal, ALU.mult))
                    dve.then(lambda e: e.tensor_scalar(g2, iota, where_f[:, 1:2], p2, ALU.is_equal, ALU.mult))
                    dve.then(lambda e, tile=tile: e.tensor_tensor(gates[:, tile, :], gates[:, tile, :], g2, ALU.add))
                    dve.then(lambda e, tile=tile: e.tensor_scalar(chosen[:, tile, :], iota, where_f[:, 0:1], None, ALU.is_equal))
                    dve.then(lambda e, tile=tile: e.scalar_tensor_tensor(
                        chosen[:, tile, :], iota, where_f[:, 1:2], chosen[:, tile, :], ALU.is_equal, ALU.add))
                gates_of.append(condition(1))
                experts(x_ready, lambda: [add_bias(gt[1], half, g, bias) for half, g in enumerate(gates_of)])
                for tile in range(TILES):
                    dve.then(lambda e: e.tensor_tensor(y[:, tile, :], (sh, sc)[tile][:, :], gt[1][:, :], ALU.mult))
                    dve.then(lambda e: e.tensor_tensor(x[:, tile, :], x[:, tile, :], y[:, tile, :], ALU.add))
                for tile in range(TILES):
                    rms_rstd(tile)
        for tile in range(TILES):
            t = dve.then(lambda e: e.scalar_tensor_tensor(
                y[:, tile, :], x[:, tile, :], rstd[:, tile:tile + 1], norm_g[:, :], ALU.mult, ALU.mult), gain_in)
            sp.wait(t)
            sp.quiet(lambda e: e.dma_start(out[tile * P:(tile + 1) * P, :], y[:, tile, :]).then_inc(out_written, 16))
        sp.quiet(lambda e: e.wait_ge(out_written, 16 * TILES))
        assert len(used) == len(stream), (len(used), len(stream))


def pack(a, order=None):
    lead, (k, n) = a.shape[:-2], a.shape[-2:]
    a = a.reshape(*lead, k // (4 * P), 4, P, n // N, N)
    m = len(lead)
    a = a.transpose(*range(m), m + 3, m, m + 2, m + 1, m + 4)
    if order is not None:
        a = a[..., order, :, :, :, :]
    return np.ascontiguousarray(a).reshape(*lead, -1, P, UNIT)


def pack_up(a, b):
    lead = a.shape[:-2]
    turns = [z.reshape(*lead, D, FF_TURNS, FF_CHUNK) for z in (a, b)]
    both = np.stack(turns, axis=-2)
    return pack(both.reshape(*lead, D, FF_TURNS * N))


def pack_down(a):
    lead = a.shape[:-2]
    m = len(lead)
    a = a.reshape(*lead, FF_TURNS, 2, P, 2, N).transpose(*range(m), m, m + 2, m + 1, m + 3, m + 4)
    return np.ascontiguousarray(a).reshape(*lead, FF_TURNS, P, UNIT)


def lay_out(i):
    f32 = np.float32
    w13 = lambda a: pack_up(a[..., :D_FF], a[..., D_FF:])
    out = {
        "x": i["x"].reshape(TILES, P, D),
        "ident": np.eye(P, dtype=f32),
        "causal": np.triu(np.ones((P, P), f32)),
        "masks": level_masks(),
        "slots": np.tile(np.arange(SEQ, dtype=f32), (P, 1)),
        "ffn1_up": w13(i["ffn1_w13"]), "ffn1_down": pack_down(i["ffn1_w2"]),
        "ffn2_up": w13(i["ffn2_w13"]), "ffn2_down": pack_down(i["ffn2_w2"]),
        "mix_in": pack(i["w_in"], [2, 1, 0, 5, 4, 3, 6, 7, 8, 9]),
        "branch_a": pack(i["w_branch_a"]), "branch_b": pack(i["w_branch_b"]), "mix_out": pack(i["w_out"]),
        "ada": pack(i["ada_w_2"]),
        "mix_in_2": pack(i["w_in_2"][:, :, :5 * N], [0, 2, 3, 1, 4]),
        "mix_out_2": pack(i["w_out_2"]),
        "dense_up": pack_up(i["ffn_w1_2"], i["ffn_w3_2"]), "dense_down": pack_down(i["ffn_w2_2"]),
    }
    up = pack_up(i["moe_w1_2"], i["moe_w3_2"])
    down = pack_down(i["moe_w2_2"])
    out["moe_up"] = up.reshape(up.shape[0], -1, P, UNIT)
    out["moe_down"] = down.reshape(down.shape[0], -1, P, UNIT)
    tail = np.zeros((DEPTH, P, KT, P), f32)
    tail[..., :GLA_RANK] = i["w_in_2"][:, :, 5 * N:].reshape(DEPTH, KT, P, GLA_RANK).transpose(0, 2, 1, 3)
    out["mix_in_2_tail"] = tail.reshape(DEPTH, P, KT * P)
    for name in ("ln_g", "ln_b", "hg_norm_g", "sg_ln_g", "sg_ln_b"):
        out[name] = i[name]
    for name in ("norm_mix_g", "norm_ffn_g", "ada_b", "final_g", "gla_norm_g", "gla_wg2"):
        out[name] = i[name + "_2"]
    out["sg_ws_t"] = np.ascontiguousarray(i["sg_ws"].transpose(0, 3, 1, 2))
    rg = np.zeros((DEPTH, P, 2, BT, P), f32)
    for g, name in enumerate(("rg_wa_2", "rg_wx_2")):
        blocks = i[name].reshape(DEPTH, BT, 2, P // 2, P // 2)
        for b in range(2):
            cut = slice(b * P // 2, (b + 1) * P // 2)
            rg[:, cut, g, :, cut] = blocks[:, :, b].transpose(0, 2, 1, 3)
    out["rg_w"] = rg.reshape(DEPTH, P, 2 * BT, P)

    def columns(a):
        return a.reshape(-1, P).T

    table = {
        "lb": columns(i["hg_lb"]), "conv_w": columns(i["rg_conv_w_2"]), "conv_b": columns(i["rg_conv_b_2"]),
        "rg_ba": columns(i["rg_ba_2"]), "rg_bx": columns(i["rg_bx_2"]), "lam": columns(i["rg_lambda_2"]),
        "gla_bg": columns(i["gla_bg_2"]), "sg_bs": columns(i["sg_bs"]), "c": columns(i["c_2"]),
        "router": i["router_w_2"].reshape(KT, P, EXPERTS).transpose(1, 0, 2).reshape(P, -1),
        "iota": np.tile(np.arange(EXPERTS, dtype=f32), (P, 1)),
    }
    out["cols"] = np.ascontiguousarray(np.concatenate([table[n] for n in COLS], axis=1))
    return {n: np.ascontiguousarray(a) for n, a in out.items()}


def kernel(**inputs):
    import concourse.bacc as bacc
    from concourse.bass_utils import run_bass_kernel_spmd

    arrays = lay_out({n: np.asarray(a) for n, a in inputs.items()})
    nc = bacc.Bacc("TRN2", target_bir_lowering=False, num_devices=1)
    w = {n: nc.dram_tensor(f"in_{n}", a.shape, mybir.dt.from_np(a.dtype), kind="ExternalInput").ap()
         for n, a in arrays.items()}
    out = nc.dram_tensor("result", (SEQ, D), F32, kind="ExternalOutput").ap()
    build(nc, w, out)
    got = run_bass_kernel_spmd(nc, [{f"in_{n}": a for n, a in arrays.items()}], core_ids=[0])
    return got.results[0]["result"].reshape(1, SEQ, D)
```
